# Optimizing a Trainium2 kernel written in Bass

```python
import math
import jax, jax.numpy as jnp
from jax import lax
import numpy as np

D_MODEL = 1024
BATCH = 1
SEQ = 128
DEPTH = 1
DEC_BATCH = 1
DEC_SEQ = 256
PAST_LEN = 128

GRID_W = 64
M_HEADS = 16
M_HEAD_DIM = 64
M_INNER = M_HEADS * M_HEAD_DIM
M_GROUPS = 2
M_STATE = 128
M_CONV = 5
M_CHUNK = 128
M_XBC = M_INNER + 2 * M_GROUPS * M_STATE
M_COLS = M_INNER + M_XBC + 2 * M_HEADS
R_HEADS = 16
R_HEAD_DIM = 64
R_INNER = R_HEADS * R_HEAD_DIM
R_DECAY_RANK = 64
R_ICLR_RANK = 64
R_GATE_RANK = 128
R_COLS = 3 * R_INNER + 2 * R_DECAY_RANK + 2 * R_ICLR_RANK + R_GATE_RANK
R_SPLITS = (R_INNER, 2 * R_INNER, 3 * R_INNER, 3 * R_INNER + 2 * R_DECAY_RANK,
            3 * R_INNER + 2 * R_DECAY_RANK + 2 * R_ICLR_RANK)
MIX_WIDTH = M_INNER + R_INNER
IN_COLS = M_COLS + R_COLS
E_GROUPS = 4
E_PER_GROUP = 8
N_EXPERTS = E_GROUPS * E_PER_GROUP
E_TOP_K = 2
D_EXPERT = 256
NORM_EPS = 1e-6
GN_EPS = 64e-5

kernel_name = "hybrid_ssd_rwkv7_hmoe_diffusion_step"

def rmsnorm(x, g):
    xf = x.astype(jnp.float32)
    return (xf * lax.rsqrt(jnp.mean(xf * xf, axis=-1, keepdims=True) + NORM_EPS) * g).astype(x.dtype)

def flip(t):
    return jnp.flip(t, axis=1)

def centred_depthwise_conv(u, w, b):
    out = lax.conv_general_dilated(
        u, w.astype(u.dtype)[:, None, :], window_strides=(1,),
        padding=[(M_CONV // 2, M_CONV // 2)], dimension_numbers=('NWC', 'WIO', 'NWC'),
        feature_group_count=u.shape[-1])
    return out + b

def ssd_chunked_scan(x, dt, a_head, bmat, cmat, s0):
    bsz, seqlen, nh, hp = x.shape
    nc = seqlen // M_CHUNK
    e = nh // M_GROUPS
    xd = (x * dt[..., None]).reshape(bsz, nc, M_CHUNK, M_GROUPS, e, hp)
    la = jnp.moveaxis((dt * a_head).reshape(bsz, nc, M_CHUNK, M_GROUPS, e), 2, -1)
    cs = jnp.cumsum(la, axis=-1)
    bm = bmat.reshape(bsz, nc, M_CHUNK, M_GROUPS, M_STATE)
    cm = cmat.reshape(bsz, nc, M_CHUNK, M_GROUPS, M_STATE)
    causal = jnp.tril(jnp.ones((M_CHUNK, M_CHUNK), dtype=bool))
    lmat = jnp.exp(jnp.where(causal, cs[..., :, None] - cs[..., None, :], -jnp.inf))
    scores = jnp.einsum('bcqgn,bcsgn->bcgqs', cm, bm)
    y_diag = jnp.einsum('bcgeqs,bcsgep->bcqgep', scores[:, :, :, None] * lmat, xd)
    chunk_states = jnp.einsum('bcqgn,bcgeq,bcqgep->bcgepn', bm, jnp.exp(cs[..., -1:] - cs), xd)
    chunk_decay = jnp.exp(cs[..., -1])

    def carry_step(s, inp):
        st, dec = inp
        return s * dec[..., None, None] + st, s

    s_fin, s_prev = lax.scan(carry_step, s0.astype(jnp.float32).reshape(bsz, M_GROUPS, e, hp, M_STATE),
                             (jnp.moveaxis(chunk_states, 1, 0), jnp.moveaxis(chunk_decay, 1, 0)))
    y_off = jnp.einsum('bcqgn,bcgeq,cbgepn->bcqgep', cm, jnp.exp(cs), s_prev)
    return (y_diag + y_off).reshape(bsz, seqlen, nh, hp), s_fin.reshape(bsz, nh, hp, M_STATE)

def mamba_ssd_group(u, s0_f, s0_b, conv_w, conv_b, dt_bias, a_log, d_skip, norm_w):
    bsz, seqlen, _ = u.shape
    z, xbc, dt_raw = jnp.split(u, [M_INNER, M_INNER + M_XBC], axis=-1)
    xbc = jax.nn.silu(centred_depthwise_conv(xbc, conv_w, conv_b))
    xs, bmat, cmat = jnp.split(xbc, [M_INNER, M_INNER + M_GROUPS * M_STATE], axis=-1)
    xs = xs.reshape(bsz, seqlen, M_HEADS, M_HEAD_DIM)
    bmat = bmat.reshape(bsz, seqlen, M_GROUPS, M_STATE)
    cmat = cmat.reshape(bsz, seqlen, M_GROUPS, M_STATE)
    dt = jax.nn.softplus(dt_raw.reshape(bsz, seqlen, 2, M_HEADS) + dt_bias)
    a = -jnp.exp(a_log.astype(jnp.float32))
    y_f, s_f = ssd_chunked_scan(xs, dt[:, :, 0], a[0], bmat, cmat, s0_f)
    y_b, s_b = ssd_chunked_scan(flip(xs), flip(dt[:, :, 1]), a[1], flip(bmat), flip(cmat), s0_b)
    y = y_f + flip(y_b) + xs * d_skip[:, None]
    y = (y.reshape(bsz, seqlen, M_INNER) * jax.nn.silu(z)).reshape(bsz, seqlen, M_GROUPS, M_INNER // M_GROUPS)
    y = y * lax.rsqrt(jnp.mean(y * y, axis=-1, keepdims=True) + NORM_EPS)
    return y.reshape(bsz, seqlen, M_INNER) * norm_w, s_f, s_b

def seq_bi_shift(u):
    bsz, seqlen, ch = u.shape
    u2 = u.reshape(bsz, seqlen, ch // 2, 2)
    prev = jnp.pad(u2[:, :-1, :, 0], ((0, 0), (1, 0), (0, 0)))
    nxt = jnp.pad(u2[:, 1:, :, 1], ((0, 0), (0, 1), (0, 0)))
    return jnp.stack([prev, nxt], axis=-1).reshape(bsz, seqlen, ch)

def grid_quad_shift(u):
    bsz, seqlen, ch = u.shape
    rows = seqlen // GRID_W
    g = u.reshape(bsz, rows, GRID_W, ch // 4, 4)
    left = jnp.pad(g[:, :, :-1, :, 0], ((0, 0), (0, 0), (1, 0), (0, 0)))
    right = jnp.pad(g[:, :, 1:, :, 1], ((0, 0), (0, 0), (0, 1), (0, 0)))
    up = jnp.pad(g[:, :-1, :, :, 2], ((0, 0), (1, 0), (0, 0), (0, 0)))
    down = jnp.pad(g[:, 1:, :, :, 3], ((0, 0), (0, 1), (0, 0), (0, 0)))
    return jnp.stack([left, right, up, down], axis=-1).reshape(bsz, seqlen, ch)

def wkv7_scan(r, w, k, v, kk, a, s0):
    def step(s, inp):
        r_t, w_t, k_t, v_t, kk_t, a_t = inp
        sa = jnp.einsum('bhij,bhj->bhi', s, kk_t)
        s = s * w_t[:, :, None, :] - sa[..., None] * (kk_t * a_t)[:, :, None, :] + v_t[..., None] * k_t[:, :, None, :]
        return s, jnp.einsum('bhij,bhj->bhi', s, r_t)

    xs = tuple(jnp.moveaxis(t, 1, 0) for t in (r, w, k, v, kk, a))
    s_fin, ys = lax.scan(step, s0.astype(jnp.float32), xs)
    return jnp.moveaxis(ys, 0, 1), s_fin

def rwkv7_group(u, on_grid, s0_f, s0_b, mu, w0, w_up, a0, a_up, g_up, k_k, k_a, r_k, ln_w, ln_b):
    bsz, seqlen, _ = u.shape
    shifted = grid_quad_shift(u) if on_grid else seq_bi_shift(u)
    u = u + (shifted - u) * mu
    r, k, v, wd, ad, gd = jnp.split(u, R_SPLITS, axis=-1)
    wd = jnp.tanh(wd.reshape(bsz, seqlen, 2, R_DECAY_RANK))
    ad = ad.reshape(bsz, seqlen, 2, R_ICLR_RANK)
    w_log = w0 + jnp.einsum('bldr,drc->bldc', wd, w_up)
    decay = jnp.exp(-jnp.exp(-jax.nn.softplus(-w_log) - 0.5))
    a = jax.nn.sigmoid(a0 + jnp.einsum('bldr,drc->bldc', ad, a_up))
    g = jax.nn.sigmoid(gd) @ g_up

    def hs(t):
        return t.reshape(bsz, seqlen, R_HEADS, R_HEAD_DIM)

    kk = hs(k * k_k)
    kk = kk / jnp.maximum(jnp.sqrt(jnp.sum(kk * kk, axis=-1, keepdims=True)), 1e-12)
    k_dir = k[:, :, None, :] * (1.0 + (a - 1.0) * k_a)
    rh, vh = hs(r), hs(v)
    y_f, s_f = wkv7_scan(rh, hs(decay[:, :, 0]), hs(k_dir[:, :, 0]), vh, kk, hs(a[:, :, 0]), s0_f)
    y_b, s_b = wkv7_scan(flip(rh), flip(hs(decay[:, :, 1])), flip(hs(k_dir[:, :, 1])), flip(vh), flip(kk),
                         flip(hs(a[:, :, 1])), s0_b)
    y = y_f + flip(y_b)
    mean = jnp.mean(y, axis=-1, keepdims=True)
    var = jnp.mean(jnp.square(y - mean), axis=-1, keepdims=True)
    y = ((y - mean) * lax.rsqrt(var + GN_EPS)).reshape(bsz, seqlen, R_INNER) * ln_w + ln_b
    bonus = jnp.sum(rh * hs(k_dir[:, :, 0] + k_dir[:, :, 1]) * r_k, axis=-1, keepdims=True) * vh
    return (y + bonus.reshape(bsz, seqlen, R_INNER)) * g, s_f, s_b

def hierarchical_moe(h, w_grp, b_grp, w_exp, b_exp, w_gate, w_up, w_down):
    shp = h.shape
    t = h.reshape(-1, shp[-1])
    n_tok = t.shape[0]
    grp_logits = (t @ w_grp).astype(jnp.float32) + b_grp
    grp_idx = jnp.argmax(grp_logits, axis=-1)
    grp_prob = jnp.take_along_axis(jax.nn.softmax(grp_logits, axis=-1), grp_idx[:, None], axis=-1)
    exp_logits = ((t @ w_exp).astype(jnp.float32) + b_exp).reshape(n_tok, E_GROUPS, E_PER_GROUP)
    in_grp = jnp.take_along_axis(exp_logits, grp_idx[:, None, None], axis=1)[:, 0]
    top_v, top_i = lax.top_k(in_grp, E_TOP_K)
    top_w = jax.nn.softmax(top_v, axis=-1) * grp_prob
    expert_id = grp_idx[:, None] * E_PER_GROUP + top_i
    gates = jnp.sum(jax.nn.one_hot(expert_id, N_EXPERTS, dtype=jnp.float32) * top_w[..., None], axis=1)
    hid = jax.nn.silu(jnp.einsum('td,edf->tef', t, w_gate)) * jnp.einsum('td,edf->tef', t, w_up)
    out = jnp.einsum('tef,efd->td', hid * gates[..., None].astype(hid.dtype), w_down)
    return out.reshape(shp)

def trunk_layer(x, cond, on_grid, s_ssm_f, s_ssm_b, s_wkv_f, s_wkv_b,
                w_ada, b_ada, norm1_w, w_in, m_conv_w, m_conv_b, m_dt_bias, m_a_log, m_d_skip, m_norm_w,
                r_mu, r_w0, r_w_up, r_a0, r_a_up, r_g_up, r_k_k, r_k_a, r_r_k, r_ln_w, r_ln_b,
                w_out, norm2_w, moe_w_grp, moe_b_grp, moe_w_exp, moe_b_exp, moe_w_gate, moe_w_up, moe_w_down):
    shift1, scale1, gate1, shift2, scale2, gate2 = jnp.split(jax.nn.silu(cond) @ w_ada + b_ada, 6, axis=-1)
    h = rmsnorm(x, norm1_w) * (1.0 + scale1) + shift1
    u = (h @ w_in).astype(jnp.float32)
    ym, sm_f, sm_b = mamba_ssd_group(u[..., :M_COLS], s_ssm_f, s_ssm_b, m_conv_w, m_conv_b, m_dt_bias,
                                     m_a_log, m_d_skip, m_norm_w)
    yr, sr_f, sr_b = rwkv7_group(u[..., M_COLS:], on_grid, s_wkv_f, s_wkv_b, r_mu, r_w0, r_w_up, r_a0, r_a_up,
                                 r_g_up, r_k_k, r_k_a, r_r_k, r_ln_w, r_ln_b)
    mix = jnp.concatenate([ym, yr], axis=-1) @ w_out
    x = x + (gate1 * mix).astype(x.dtype)
    h = rmsnorm(x, norm2_w) * (1.0 + scale2) + shift2
    x = x + (gate2 * hierarchical_moe(h, moe_w_grp, moe_b_grp, moe_w_exp, moe_b_exp, moe_w_gate, moe_w_up,
                                      moe_w_down)).astype(x.dtype)
    return x, sm_f, sm_b, sr_f, sr_b

def setup_inputs(seed: int = 0) -> dict:
    key = jax.random.key(seed)
    ks = iter(jax.random.split(key, 64))

    def nrm(shape, s):
        return jax.random.normal(next(ks), shape, jnp.float32) * s

    def uni(shape, lo, hi):
        return jax.random.uniform(next(ks), shape, jnp.float32, lo, hi)

    L = DEPTH
    dt0 = jnp.exp(uni((L, 2, M_HEADS), math.log(1e-3), math.log(1e-1)))
    return {
        "x_prompt": nrm((BATCH, SEQ, D_MODEL), 1.0),
        "x_sample": nrm((DEC_BATCH, DEC_SEQ, D_MODEL), 1.0),
        "state_ssm_fwd": nrm((DEC_BATCH, L, M_HEADS, M_HEAD_DIM, M_STATE), 0.1),
        "state_ssm_bwd": nrm((DEC_BATCH, L, M_HEADS, M_HEAD_DIM, M_STATE), 0.1),
        "state_wkv_fwd": nrm((DEC_BATCH, L, R_HEADS, R_HEAD_DIM, R_HEAD_DIM), 0.3),
        "state_wkv_bwd": nrm((DEC_BATCH, L, R_HEADS, R_HEAD_DIM, R_HEAD_DIM), 0.3),
        "c": nrm((DEC_BATCH, D_MODEL), 1.0),
        "c_ctx": nrm((D_MODEL,), 1.0),
        "w_ada": nrm((L, D_MODEL, 6 * D_MODEL), 0.5 * D_MODEL ** -0.5),
        "b_ada": nrm((L, 6 * D_MODEL), 0.02),
        "norm1_w": 1.0 + nrm((L, D_MODEL), 0.1),
        "w_in": nrm((L, D_MODEL, IN_COLS), D_MODEL ** -0.5),
        "m_conv_w": nrm((L, M_CONV, M_XBC), M_CONV ** -0.5),
        "m_conv_b": nrm((L, M_XBC), 0.02),
        "m_dt_bias": dt0 + jnp.log(-jnp.expm1(-dt0)),
        "m_a_log": jnp.log(uni((L, 2, M_HEADS), 1.0, 16.0)),
        "m_d_skip": 1.0 + nrm((L, M_HEADS), 0.1),
        "m_norm_w": 1.0 + nrm((L, M_INNER), 0.1),
        "r_mu": uni((L, R_COLS), 0.0, 1.0),
        "r_w0": uni((L, 2, R_INNER), -3.0, 1.0),
        "r_w_up": nrm((L, 2, R_DECAY_RANK, R_INNER), 0.1),
        "r_a0": nrm((L, 2, R_INNER), 0.5),
        "r_a_up": nrm((L, 2, R_ICLR_RANK, R_INNER), 0.5 * R_ICLR_RANK ** -0.5),
        "r_g_up": nrm((L, R_GATE_RANK, R_INNER), R_GATE_RANK ** -0.5),
        "r_k_k": 1.0 + nrm((L, R_INNER), 0.1),
        "r_k_a": 1.0 + nrm((L, R_INNER), 0.1),
        "r_r_k": nrm((L, R_HEADS, R_HEAD_DIM), 0.1),
        "r_ln_w": 1.0 + nrm((L, R_INNER), 0.1),
        "r_ln_b": nrm((L, R_INNER), 0.02),
        "w_out": nrm((L, MIX_WIDTH, D_MODEL), MIX_WIDTH ** -0.5),
        "norm2_w": 1.0 + nrm((L, D_MODEL), 0.1),
        "moe_w_grp": nrm((L, D_MODEL, E_GROUPS), D_MODEL ** -0.5),
        "moe_b_grp": nrm((L, E_GROUPS), 0.01),
        "moe_w_exp": nrm((L, D_MODEL, N_EXPERTS), D_MODEL ** -0.5),
        "moe_b_exp": nrm((L, N_EXPERTS), 0.01),
        "moe_w_gate": nrm((L, N_EXPERTS, D_MODEL, D_EXPERT), D_MODEL ** -0.5),
        "moe_w_up": nrm((L, N_EXPERTS, D_MODEL, D_EXPERT), D_MODEL ** -0.5),
        "moe_w_down": nrm((L, N_EXPERTS, D_EXPERT, D_MODEL), D_EXPERT ** -0.5),
        "final_norm_w": 1.0 + nrm((D_MODEL,), 0.1),
    }

def reference(x_prompt, x_sample, state_ssm_fwd, state_ssm_bwd, state_wkv_fwd, state_wkv_bwd, c, c_ctx,
              w_ada, b_ada, norm1_w, w_in, m_conv_w, m_conv_b, m_dt_bias, m_a_log, m_d_skip, m_norm_w,
              r_mu, r_w0, r_w_up, r_a0, r_a_up, r_g_up, r_k_k, r_k_a, r_r_k, r_ln_w, r_ln_b,
              w_out, norm2_w, moe_w_grp, moe_b_grp, moe_w_exp, moe_b_exp, moe_w_gate, moe_w_up, moe_w_down,
              final_norm_w):
    nb = x_prompt.shape[0]
    zeros_ssm = jnp.zeros((nb, M_HEADS, M_HEAD_DIM, M_STATE), jnp.float32)
    zeros_wkv = jnp.zeros((nb, R_HEADS, R_HEAD_DIM, R_HEAD_DIM), jnp.float32)
    ctx_cond = c_ctx[None, None, :]
    lat_cond = c[:, None, :]
    xp, xs = x_prompt, x_sample
    ssm_f_list, ssm_b_list, wkv_f_list, wkv_b_list = [], [], [], []
    for i in range(DEPTH):
        lp = dict(w_ada=w_ada[i], b_ada=b_ada[i], norm1_w=norm1_w[i], w_in=w_in[i], m_conv_w=m_conv_w[i],
                  m_conv_b=m_conv_b[i], m_dt_bias=m_dt_bias[i], m_a_log=m_a_log[i], m_d_skip=m_d_skip[i],
                  m_norm_w=m_norm_w[i], r_mu=r_mu[i], r_w0=r_w0[i], r_w_up=r_w_up[i], r_a0=r_a0[i],
                  r_a_up=r_a_up[i], r_g_up=r_g_up[i], r_k_k=r_k_k[i], r_k_a=r_k_a[i], r_r_k=r_r_k[i],
                  r_ln_w=r_ln_w[i], r_ln_b=r_ln_b[i], w_out=w_out[i], norm2_w=norm2_w[i],
                  moe_w_grp=moe_w_grp[i], moe_b_grp=moe_b_grp[i], moe_w_exp=moe_w_exp[i],
                  moe_b_exp=moe_b_exp[i], moe_w_gate=moe_w_gate[i], moe_w_up=moe_w_up[i],
                  moe_w_down=moe_w_down[i])
        xp, smf, smb, srf, srb = trunk_layer(xp, ctx_cond, False, zeros_ssm, zeros_ssm, zeros_wkv, zeros_wkv, **lp)
        ssm_f_list.append(smf)
        ssm_b_list.append(smb)
        wkv_f_list.append(srf)
        wkv_b_list.append(srb)
        xs, _, _, _, _ = trunk_layer(xs, lat_cond, True, state_ssm_fwd[:, i], state_ssm_bwd[:, i],
                                     state_wkv_fwd[:, i], state_wkv_bwd[:, i], **lp)
    y_prompt = rmsnorm(xp, final_norm_w)
    y_sample = rmsnorm(xs, final_norm_w)
    new_ssm_fwd = jnp.stack(ssm_f_list, axis=1)
    new_ssm_bwd = jnp.stack(ssm_b_list, axis=1)
    new_wkv_fwd = jnp.stack(wkv_f_list, axis=1)
    new_wkv_bwd = jnp.stack(wkv_b_list, axis=1)
    return (y_prompt, y_sample, new_ssm_fwd, new_ssm_bwd, new_wkv_fwd, new_wkv_bwd)


_drawn_inputs = setup_inputs


def setup_inputs(seed=0):
    import zlib

    import numpy as np

    out = dict(_drawn_inputs(seed))
    spreads = {}
    factors = {'state_wkv_fwd': 8.0,
     'state_wkv_bwd': 8.0,
     'm_d_skip': 16.854,
     'r_ln_w': 4.637,
     'r_ln_b': 24.732,
     'moe_b_grp': 183.96,
     'moe_b_exp': 29.988,
     'state_ssm_fwd': 6.558,
     'state_ssm_bwd': 5.004,
     'm_norm_w': 2.82}
    for name, (base, spread) in spreads.items():
        noise = np.random.default_rng([zlib.crc32(name.encode()), seed]).standard_normal(out[name].shape)
        drawn = base * np.exp(spread * noise) if base else spread * noise
        out[name] = __import__('jax').numpy.asarray(drawn.astype(out[name].dtype))
    for name, factor in factors.items():
        out[name] = (out[name] * factor).astype(out[name].dtype)
    return out
```

```python
from contextlib import ExitStack

import concourse.bass as bass
from concourse import mybir

ALU = mybir.AluOpType
ACT = mybir.ActivationFunctionType
AX = mybir.AxisListType
F32 = mybir.dt.float32
I32 = mybir.dt.int32
U32 = mybir.dt.uint32
ds = bass.ds

P = 128
D = 1024
KT = D // P
NTILE = 3
T = NTILE * P
GRID = 64
BLK = 512
HM, PM, NS = 16, 64, 128
XBC = 12
DTC = 2560
RC = 2592
RT = 27
RING = 3
NEG_C = -0.6065306597126334
NE, EG, EPG, DE = 32, 4, 8, 256
N_OVER = (2 * T - 1) // P
N_TILES = NE + N_OVER

V0 = dict(b_ada=0, norm1=48, conv_w=56, conv_b=116)
V1 = dict(mu=0, w0=27, a0=43, k_k=59, k_a=67, r_k=75, ln_w=83, ln_b=91, norm2=99, m_norm=107)
V1N = 115

ADA_A, XB, Z, R, ADA_B, GATES, WOUT = 0, 4, 7, 9, 16, 20, 24
ADA_COLS = [0, 1, 2, 3, 6, 7, 8, 9]


OFF = ((1, 0, 0), (2, 1, 0), (2, 0, 1), (1, 1, 1))


class Chain:

    def __init__(self, eng, sem):
        self.eng, self.sem, self.n = eng, sem, 0

    def did(self, ins):
        ins.then_inc(self.sem, 1)
        self.n += 1
        return self.n

    def wait(self, n=None):
        self.eng.wait_ge(self.sem, self.n if n is None else n)

    def do(self, ins):
        self.did(ins)
        self.wait()


class LoopChain:

    def __init__(self, eng, sem, i, per):
        self.eng, self.sem, self.i, self.per, self.n = eng, sem, i, per, 0

    def did(self, ins):
        ins.then_inc(self.sem, 1)
        self.n += 1
        return self.n

    def wait(self, n=None):
        self.eng.wait_ge(self.sem, self.i * self.per + (self.n if n is None else n))

    def do(self, ins):
        self.did(ins)
        self.wait()

    def end(self):
        assert self.n == self.per, (self.n, self.per)


def program(nc, a, out, dump=None):
    ctx = ExitStack()
    with ctx:
        def sb(name, shape, dt=F32):
            return ctx.enter_context(nc.sbuf_tensor(name, shape, dt))

        def sem(name):
            return ctx.enter_context(nc.semaphore(name))

        ps = ctx.enter_context(nc.psum_tensor("ps", [P, 8, 512], F32))

        ident = sb("ident", [P, P])
        ones = sb("ones", [P, P])
        bones = sb("bones", [P, P])
        tri = sb("tri", [P, 4, P])
        trin = sb("trin", [P, 4, P])
        lvl = sb("lvl", [P, 7, 2, P])
        sel32 = sb("sel32", [P, 32])
        par = sb("par", [P, 6])
        rst = sb("rst", [P, 2, T])
        vrows = sb("vrows", [P, 2, P])
        crows = sb("crows", [16, P])
        pv0 = sb("pv0", [P, P])
        pv1 = sb("pv1", [P, P])
        cond = sb("cond", [P, KT, 32])
        mod = sb("mod", [P, 32, 2])
        aff1 = sb("aff1", [P, KT, 2])
        aff2 = sb("aff2", [P, KT, 2])
        mum = sb("mum", [P, 7, RT])
        kam = sb("kam", [P, KT])
        drow = sb("drow", [P, 32 + 32 + 16])
        stat = sb("stat", [P, 16])
        dt = sb("dt", [P, NTILE, 32])
        dtmp = sb("dtmp", [P, NTILE, 32])
        dtl = sb("dtl", [P, NTILE, 32])
        dtr = sb("dtr", [P, NTILE, 32])
        la = sb("la", [P, NTILE, 32])
        ecs = sb("ecs", [P, 288])
        wdt = sb("wdt", [P, KT, 32])

        ring_a = sb("ring_a", [P, RING * KT * BLK])
        um_a = sb("um_a", [P, RT, T])
        mixm = sb("mixm", [P, KT, T])
        hT = sb("hT", [P, KT, T])
        misc = sb("misc", [P, 12288])

        ring = ring_a[:, :].rearrange("p (s k c) -> p s k c", s=RING, k=KT)
        xt = misc[:, 0:3072].rearrange("p (j c) -> p j c", j=NTILE)
        zs = misc[:, 3072:6144].rearrange("p (j c) -> p j c", j=NTILE)
        xs = misc[:, 6144:9216].rearrange("p (j c) -> p j c", j=NTILE)
        btm = misc[:, 9216:9984].rearrange("p (j c) -> p j c", j=NTILE)
        bct = misc[:, 9984:11520].rearrange("p (i t) -> p i t", i=4)
        scratch = sb("scratch", [P, 2048 + 2 * BLK])
        raw = scratch[:, 0:784].rearrange("p (b t) -> p b t", b=2)
        acc = scratch[:, 784:1568].rearrange("p (b t) -> p b t", b=2)
        adas = scratch[:, 2048:3072].rearrange("p (b c) -> p b c", b=2)

        ring_s = [ring_a[:, 4096 * i:4096 * (i + 1)] for i in range(RING)]
        st_in = ring_s[2][:, 0:2048].rearrange("p (d i n) -> p d i n", d=2, i=8)
        st0 = ring_s[2][:, 2048:4096].rearrange("p (d c) -> p d c", d=2)
        st1 = ring_s[0][:, 0:2048].rearrange("p (d c) -> p d c", d=2)
        xdw = ring_s[0][:, 2048:4096].rearrange("p (b c) -> p b c", b=2)
        msc = ring_s[1][:, 0:1536].rearrange("p (d i q) -> p d i q", d=2, i=6)
        yoff = ring_s[1][:, 1536:2048]
        st_out = ring_s[1][:, 2048:4096].rearrange("p (d i n) -> p d i n", d=2, i=8)
        hT_flat = hT[:, :, :].rearrange("p k t -> p (k t)")
        lam = hT_flat[:, 0:2048].rearrange("p (b i s) -> p b i s", b=2, i=8)
        seg = misc[:, 0:2048].rearrange("p (b i s) -> p b i s", b=2, i=8)
        sq = misc[:, 2048:2560]
        mstat = sb("mstat", [P, 24])
        selb = sb("selb", [P, 2, P])

        def at(flat, o, *shape):
            names = "abcd"[:len(shape)]
            n = 1
            for x in shape:
                n *= x
            v = flat[:, o:o + n]
            return v if len(shape) == 1 else v.rearrange(
                f"p ({' '.join(names)}) -> p {' '.join(names)}", **dict(zip(names, shape)))

        gb = [at(r, 0, 2, 2, 2, P) for r in ring_s]
        gk = [at(r, 1024, 2, 2, 2, P) for r in ring_s]
        xinvT = [at(r, 2048, 2, 2, P) for r in ring_s]
        xinv = [at(r, 2560, 2, 2, P) for r in ring_s]
        ys = [at(r, 3072, 2, 2, P) for r in ring_s]
        rhs_s = [at(r, 3584, 4, 64) for r in ring_s]
        us = [at(r, 3840, 4, 64) for r in ring_s]
        sg = at(misc, 0, 2, T)
        am = at(misc, 768, 2, T)
        cs = at(misc, 1536, 2, T)
        csm = at(misc, 2304, 2, T)
        e_p = at(misc, 3072, 2, T)
        e_m = at(misc, 3840, 2, T)
        e_i = at(misc, 4608, 2, T)
        kd = at(misc, 5376, 2, T)
        be = at(misc, 6144, 2, NTILE, P)
        kap = at(misc, 6912, 2, NTILE, P)
        arr = at(misc, 7680, 2, NTILE, 2, P)
        kk0 = at(misc, 9216, T)
        kk = at(misc, 9600, T)
        kroot = at(misc, 9984, T)
        rb = at(misc, 10368, T)
        kroot2 = kroot
        eps_gn = sb("eps_gn", [P, 1])
        btk = at(misc, 10752, 4, P)
        ktk = at(misc, 11264, 4, P)
        vtk = at(misc, 11776, NTILE, P)
        y_c = at(hT_flat, 0, T)
        yc0 = at(hT_flat, 384, T)
        ysq_c = at(hT_flat, 768, T)
        g_c = at(hT_flat, 1152, T)
        vb = at(hT_flat, 1536, T)
        v_c = at(hT_flat, 1920, T)
        tot = at(hT_flat, 2304, 2, NTILE)
        e_half = at(hT_flat, 2310, 2, NTILE)
        r0p = at(hT_flat, 2320, 2, 2, 64)
        stw = sb("stw", [P, 3, P])
        r0all = sb("r0all", [P, 8, 2, 64])
        sall = sb("sall", [P, 8, 2, 64])
        wkv_in = scratch[0:64, 0:2048].rearrange("p (d c) -> p d c", d=2)

        s_small = sem("small_loads")
        s_x = sem("x_loaded")
        w_in_slot = [sem(f"block_in_slot_{i}") for i in range(RING)]
        s_wdt = sem("wdt_loaded")
        pool_c = sem("pool_steps")
        const_ready = sem("constants_ready")
        vec_t = sem("vectors_transposed")
        vec_ready = sem("vectors_ready")
        cond_ready = sem("cond_ready")
        ada_ps = sem("ada_in_psum")
        ada_sb = sem("ada_copied")
        ada_cols = sem("ada_columns_in_psum")
        meansq = sem("mean_squares")
        rstd = sem("roots_ready")
        xn_ready = sem("x_normalised")
        xT_ps = sem("x_transposed")
        hT_ready = sem("h_ready")
        proj = sem("projection_in_psum")
        proj_read = sem("projection_read")
        conv_acc = sem("conv_summed")
        conv_out = sem("conv_silu_done")
        conv_T = sem("conv_transposed")
        conv_tm = sem("conv_token_major")
        mix0 = sem("mix_started")
        dve_c = sem("dve_steps")
        dve_r = sem("dve_mix_steps")
        act_c = sem("act_steps")
        dt_ps = sem("dt_in_psum")
        out_done = sem("outputs_written")
        masks_ready = sem("level_masks_ready")
        dt_in = sem("softplus_input_ready")
        dt_ln = sem("softplus_log_ready")
        la_ready = sem("la_ready")
        cs_ps = sem("cumulated_la_in_psum")
        cs_exp = sem("decay_factors_ready")
        score_ps = sem("scores_in_psum")
        score_ok = sem("scores_masked")
        st_loaded = sem("ssm_states_loaded")
        st_T = sem("ssm_states_transposed")
        st0_ok = sem("ssm_states_ready")
        xdw_ok = sem("weighted_x_ready")
        cst_ps = sem("chunk_states_in_psum")
        cst_out = sem("prompt_states_copied")
        st1_ok = sem("carried_states_ready")
        lam_ok = sem("masked_la_ready")
        seg_ps = sem("segment_sums_in_psum")
        seg_exp = sem("segment_decays_ready")
        g_ok = sem("decayed_scores_ready")
        y_ps = sem("mamba_y_in_psum")
        y_sb = sem("mamba_y_read")
        off_ps = sem("state_y_in_psum")
        off_rd = sem("state_y_read")
        gated = sem("mamba_y_gated")
        ysq = sem("mamba_y_squared")
        ynorm = sem("mamba_y_normalised")
        yT_ps = sem("mamba_y_transposed")
        yT_sb = sem("mamba_mix_ready")
        act_m = sem("act_mamba_steps")
        dve_l = sem("dve_mamba_loop_steps")
        up_loaded = sem("up_projections_loaded")
        wkv_loaded = sem("wkv_states_loaded")
        wkv_T = sem("wkv_states_transposed")
        wkv_ok = sem("wkv_states_ready")
        wd_ok = sem("low_rank_activated")
        aux_ps = sem("aux_in_psum")
        aux_act = sem("aux_read_by_act")
        aux_dve = sem("aux_read_by_dve")
        ksq_ok = sem("k_squared")
        exp_in = sem("decay_sums_ready")
        exp_ok = sem("decays_ready")
        tot_ok = sem("tile_sums_ready")
        ehalf_ok = sem("half_decays_ready")
        v_ok = sem("v_copied")
        ab_ok = sem("alpha_beta_ready")
        rb_ok = sem("bonus_ready")
        i4_ok = sem("identities_ready")
        gram_ps = sem("grams_in_psum")
        gram_rd = sem("grams_masked")
        x_ok = sem("inverse_level_ready")
        yl_ps = sem("level_y_in_psum")
        yl_ok = sem("level_y_ready")
        zl_ps = sem("level_z_in_psum")
        r0_ok = sem("wkv_start_states_ready")
        rhs_ps = sem("rhs_in_psum")
        rhs_ok = sem("rhs_ready")
        u_ps = sem("u_in_psum")
        u_ok = sem("u_ready")
        yo_ps = sem("wkv_y_in_psum")
        yo_rd = sem("wkv_y_read")
        ws_ps = sem("wkv_state_in_psum")
        yc_ok = sem("wkv_y_ready")
        ysq_ok = sem("wkv_y_squared")
        root_ok = sem("wkv_root_ready")
        pair_ok = sem("wkv_pair_done")
        fin_T = sem("wkv_final_transposed")
        fin_sb = sem("wkv_final_copied")
        dve_w = sem("dve_wkv_steps")
        idle_dve = sem("idle_dve")
        idle_pool = sem("idle_pool")

        s_bufs = dict(locals())

        def slot(n):
            return ring[:, n % RING]

        def block_ready(eng, n):
            eng.wait_ge(w_in_slot[n % RING], 16 * (n // RING + 1))

        def block_used(eng, n):
            if n < XB:
                eng.wait_ge(ada_ps, n - ADA_A + 1)
            elif n < Z:
                eng.wait_ge(proj, 4 * (n - XB + 1))
            elif n < R:
                eng.wait_ge(proj, XBC + 3 * (n - Z + 1))
            elif n < ADA_B:
                eng.wait_ge(proj, XBC + 6 + min(4 * (n - R + 1), RT))
            elif n < WOUT:
                eng.wait_ge(ada_ps, 4 + n - ADA_B + 1)
            else:
                eng.wait_ge(out_ps, n - WOUT + 1)

        w_in_v = a["w_in"][0].rearrange("(k p) c -> p k c", p=P)
        w_ada_v = a["w_ada"][0].rearrange("(k p) c -> p k c", p=P)

        def block_source(n):
            if n < XB:
                return w_ada_v[:, :, BLK * n:BLK * (n + 1)]
            if n < Z:
                return w_in_v[:, :, D + BLK * (n - XB):D + BLK * (n - XB + 1)]
            if n < R:
                return w_in_v[:, :, BLK * (n - Z):BLK * (n - Z + 1)]
            if n < ADA_B:
                c = RC + BLK * (n - R)
                return w_in_v[:, :, c:min(c + BLK, RC + RT * P)]
            if n < GATES:
                c = ADA_COLS[4 + n - ADA_B]
                return w_ada_v[:, :, BLK * c:BLK * (c + 1)]

        TJ = ((0, 0), (1, 2), (2, 1))
        UNITS = ((0, 0), (1, 0), (0, 1), (1, 2))

        def wkv_pair_pe(pe, c):
            def aux(n, b):
                if n == 0:
                    pe.wait_ge(aux_dve, c * 2 + 2)
                elif n == 1:
                    pe.wait_ge(aux_act, c * 10 + 1)
                elif n <= 10:
                    pe.wait_ge(aux_act, c * 10 + n)
                else:
                    pe.wait_ge(aux_dve, c * 2 + 3)
                return ps[:, 6 + n % 2, 0:b]

            pe.wait_ge(up_loaded, c * 48 + 48)
            for n in range(4):
                r = 64 * (n % 2)
                pe.matmul(aux(n, T), stw[r:r + 64, n // 2, :], um_a[r:r + 64, 24 + n // 2, :],
                          start=True, stop=True).then_inc(aux_ps, 1)
            o = aux(4, T)
            pe.wait_ge(ksq_ok, c + 1)
            pe.matmul(o, bones[:, :], kroot, start=True, stop=True).then_inc(aux_ps, 1)
            pe.matmul(aux(5, T), stw[:, 2, :], um_a[:, 26, :], start=True, stop=True).then_inc(aux_ps, 1)
            o = aux(6, T)
            pe.wait_ge(v_ok, c + 1)
            for j in range(NTILE):
                mm = pe.transpose(o[:, P * j:P * j + P], v_c[:, P * j:P * j + P], ident[:, :])
            mm.then_inc(aux_ps, 1)
            pe.wait_ge(ab_ok, c + 1)
            for n, src in ((7, be), (8, kap)):
                o = aux(n, 4 * P)
                for i, (d, j) in enumerate(UNITS):
                    mm = pe.transpose(o[:, P * i:P * i + P], src[:, d, j, :], ident[:, :])
                mm.then_inc(aux_ps, 1)
            o = aux(9, T)
            pe.wait_ge(rb_ok, c + 1)
            pe.matmul(o, bones[:, :], rb, start=True, stop=True).then_inc(aux_ps, 1)

            for g, src in enumerate((be, kap)):
                for s in range(3):
                    if g == 0:
                        pe.wait_ge(yo_rd, c * 3 + (s + 1))
                    else:
                        pe.wait_ge(gram_rd, c * 6 + (s + 1))
                    for d in range(2):
                        j = TJ[s][d]
                        for h in range(2):
                            mm = pe.matmul(ps[:, 2 * s + h, 256 * d:256 * d + 256], src[64 * h:64 * h + 64, d, j, :],
                                           arr[64 * h:64 * h + 64, d, j, :, :].rearrange("p a t -> p (a t)"),
                                           start=True, stop=True)
                    mm.then_inc(gram_ps, 1)

            for l in range(1, 7):
                for s in range(3):
                    pe.wait_ge(x_ok, c * 21 + (3 * l - 3 + s + 1))
                    if l == 1:
                        pe.wait_ge(gram_rd, c * 6 + (3 + s + 1))
                    for h in range(2):
                        for d in range(2):
                            i = 2 * h + d
                            mm = pe.matmul(ps[:, 2 * s, P * i:P * i + P], gb[s][:, h, d, 0, :], xinv[s][:, h, d, :],
                                           start=True, stop=True)
                    mm.then_inc(yl_ps, 1)
                for s in range(3):
                    pe.wait_ge(yl_ok, c * 18 + (3 * l - 3 + s + 1))
                    for h in range(2):
                        for d in range(2):
                            o = P * (2 * h + d)
                            if l < 6:
                                mm = pe.matmul(ps[:, 2 * s + 1, o:o + P], xinvT[s][:, h, d, :], ys[s][:, h, d, :],
                                               start=True, stop=True)
                    if l >= 5:
                        b = 2 * s + (l == 6)
                        for h in range(2):
                            for d in range(2):
                                o = P * (2 * h + d)
                                mm = pe.matmul(ps[:, b, o:o + P], ys[s][:, h, d, :], xinvT[s][:, h, d, :],
                                               start=True, stop=True)
                    mm.then_inc(zl_ps, 1)

            pe.wait_ge(aux_act, c * 10 + 8)
            for s in range(3):
                pe.wait_ge(x_ok, c * 21 + (18 + s + 1))
                if s:
                    pe.wait_ge(r0_ok, c * 2 + s)
                for h in range(2):
                    for d in range(2):
                        i, j, hp = 2 * h + d, TJ[s][d], slice(64 * h, 64 * h + 64)
                        o = ps[:, 2 * s + h, 64 * d:64 * d + 64]
                        mm = pe.matmul(o, gk[s][:, h, d, 0, :], vtk[:, j, hp],
                                       start=True, stop=(s == 0))
                        if s:
                            mm = pe.matmul(o, arr[hp, d, j, 0, :], r0p[hp, s - 1, d, :],
                                           start=False, stop=True)
                mm.then_inc(rhs_ps, 1)
                pe.wait_ge(rhs_ok, c * 3 + (s + 1))
                for i in range(4):
                    mm = pe.matmul(ps[:, 2 * s + 1, 128 + 64 * i:192 + 64 * i], xinvT[s][:, i // 2, i % 2, :], rhs_s[s][:, i, :],
                                   start=True, stop=True)
                mm.then_inc(u_ps, 1)
                pe.wait_ge(u_ok, c * 3 + (s + 1))
                if s < 2:
                    pe.wait_ge(aux_act, c * 10 + 10)
                    for d in range(2):
                        for h in range(2):
                            j, hp, un = TJ[s][d], slice(64 * h, 64 * h + 64), 2 * s + d
                            o = ps[hp, 2 * s + 1, 384 + 64 * d:448 + 64 * d]
                            pe.matmul(o, ktk[:, un, hp], vtk[:, j, hp], start=True, stop=False)
                            mm = pe.matmul(o, btk[:, un, hp], us[s][:, 2 * h + d, :], start=False, stop=True)
                    mm.then_inc(ws_ps, 1)
                for h in range(2):
                    for d in range(2):
                        i, j, hp = 2 * h + d, TJ[s][d], slice(64 * h, 64 * h + 64)
                        o = ps[hp, 2 * s, 256 + P * (d if s else 0):256 + P * (d if s else 0) + P]
                        first, last = (d == 0 or s > 0), (d == 1 or s > 0)
                        pe.matmul(o, vtk[:, j, hp], gk[s][:, h, d, 1, :], start=first, stop=False)
                        mm = pe.matmul(o, us[s][:, i, :], gb[s][:, h, d, 1, :], start=False, stop=(last and s == 0))
                        if s:
                            mm = pe.matmul(o, r0p[hp, s - 1, d, :], arr[hp, d, j, 1, :], start=False, stop=True)
                mm.then_inc(yo_ps, 1)
            o = aux(10, T)
            pe.wait_ge(yc_ok, c + 1)
            pe.matmul(o, bones[:, :], y_c, start=True, stop=True).then_inc(aux_ps, 1)
            o = aux(11, T)
            pe.wait_ge(ysq_ok, c + 1)
            pe.matmul(o, bones[:, :], ysq_c, start=True, stop=True).then_inc(aux_ps, 1)

        def wkv_pair_act(act, c):
            def aux_in(n, dst, func, last=1, **kw):
                act.wait_ge(aux_ps, c * 12 + (n + 1))
                act.activation(dst, ps[:, 6 + n % 2, 0:dst.free_size()], func, **kw).then_inc(aux_act, 1)

            for n in range(4):
                base = V1["w0"] if n < 2 else V1["a0"]
                b = pv1[:, ds(c + (base + 8 * (n % 2)), 1)]
                aux_in(n, (sg if n < 2 else am)[:, n % 2, :], ACT.Sigmoid, bias=b)
            aux_in(4, kroot2, ACT.Sqrt)
            aux_in(5, g_c, ACT.Copy)
            aux_in(6, vtk.rearrange("p j t -> p (j t)"), ACT.Copy)
            act.wait_ge(tot_ok, c + 1)
            act.activation(e_half, tot, ACT.Exp, scale=0.5 * NEG_C).then_inc(ehalf_ok, 1)
            act.wait_ge(exp_in, c + 1)
            for i, (dst, src, sc) in enumerate(((e_m, csm, NEG_C), (e_p, cs, NEG_C), (e_i, cs, -NEG_C))):
                act.activation(dst, src, ACT.Exp, scale=sc).then_inc(exp_ok, 1)
            aux_in(7, btk.rearrange("p i t -> p (i t)"), ACT.Copy, scale=-1.0)
            aux_in(8, ktk.rearrange("p i t -> p (i t)"), ACT.Copy)
            for l in range(1, 7):
                for s in range(3):
                    act.wait_ge(yl_ps, c * 18 + (3 * l - 3 + s + 1))
                    act.activation(ys[s].rearrange("p a b q -> p (a b q)"), ps[:, 2 * s, :], ACT.Copy).then_inc(yl_ok, 1)
            for s in range(3):
                act.wait_ge(rhs_ps, c * 3 + (s + 1))
                act.activation(rhs_s[s].rearrange("p (h d) v -> p h (d v)", h=2), ps[:, 2 * s:2 * s + 2, 0:128],
                               ACT.Copy).then_inc(rhs_ok, 1)
                act.wait_ge(u_ps, c * 3 + (s + 4))
                act.activation(us[s].rearrange("p i v -> p (i v)"), ps[:, 2 * s + 1, 128:384],
                               ACT.Copy).then_inc(u_ok, 1)
            aux_in(11, ysq_c, ACT.Sqrt, scale=1.0 / 64, bias=eps_gn[:, 0:1])

        def wkv_pair_dve(dve, c, lc):
            def tile_of(i):
                return um_a[:, ds(c + i, 1), :].rearrange("p a t -> p (a t)")

            def col(name):
                return pv1[:, ds(c + V1[name], 1)]

            def both(ap):
                return ap.unsqueeze(1).to_broadcast([P, 2, T])

            r, k = tile_of(0), tile_of(8)
            lc.do(dve.tensor_scalar(kk0, k, col("k_k"), None, ALU.mult))
            dve.tensor_tensor(kroot, kk0, kk0, ALU.mult).then_inc(ksq_ok, 1)
            dve.wait_ge(aux_act, c * 10 + 3)
            dve.tensor_tensor_scan(cs[:, 0, :], rst[:, 0, :], sg[:, 0, :], 0.0, ALU.mult, ALU.add)
            lc.do(dve.tensor_tensor_scan(cs[:, 1, ::-1], rst[:, 1, ::-1], sg[:, 1, ::-1], 0.0, ALU.mult, ALU.add))
            dve.tensor_copy(tot[:, 0, :], cs[:, 0, P - 1::P])
            dve.tensor_copy(tot[:, 1, :], cs[:, 1, 0::P]).then_inc(tot_ok, 1)
            dve.wait_ge(tot_ok, c + 1)
            cs6 = cs.rearrange("p d (j t) -> p (d j) t", j=NTILE)
            lc.do(dve.scalar_tensor_tensor(cs6, tot.rearrange("p d j -> p (d j)").unsqueeze(2).to_broadcast([P, 6, P]), -0.5,
                                           cs6, ALU.mult, ALU.add))
            dve.tensor_tensor(csm, cs, sg, ALU.subtract).then_inc(exp_in, 1)
            dve.wait_ge(aux_act, c * 10 + 6)
            lc.do(dve.tensor_scalar(kd, am, col("k_a"), kam[:, ds(c, 1)], ALU.mult, ALU.add))
            lc.do(dve.tensor_tensor(kd, kd, both(k), ALU.mult))
            lc.do(dve.tensor_scalar(kroot2, kroot2, 1e-12, None, ALU.max))
            lc.do(dve.reciprocal(kroot2, kroot2))
            lc.do(dve.tensor_tensor(kk, kk0, kroot2, ALU.mult))
            lc.do(dve.tensor_tensor(am, am, both(kk), ALU.mult))

            def tiles(ap):
                return ap.rearrange("p d (j t) -> p d j t", j=NTILE)

            def tiles2(ap):
                return ap.rearrange("p (j t) -> p j t", j=NTILE).unsqueeze(1).to_broadcast([P, 2, NTILE, P])
            dve.wait_ge(exp_ok, c * 3 + 3)
            dve.tensor_tensor(arr[:, :, :, 0, :], tiles2(kk), tiles(e_m), ALU.mult)
            dve.tensor_tensor(arr[:, :, :, 1, :], tiles2(r), tiles(e_p), ALU.mult)
            dve.tensor_tensor(be, tiles(am), tiles(e_i), ALU.mult)
            dve.tensor_tensor(kap, tiles(kd), tiles(e_i), ALU.mult).then_inc(ab_ok, 1)
            lc.do(dve.tensor_tensor(rb, kd[:, 0, :], kd[:, 1, :], ALU.add))
            dve.scalar_tensor_tensor(rb, rb, col("r_k"), r, ALU.mult, ALU.mult).then_inc(rb_ok, 1)
            dve.wait_ge(ehalf_ok, c + 1)
            for d in range(2):
                j = TJ[1][d]
                ins = dve.tensor_scalar(r0p[:, 0, d, :], r0all[:, ds(c, 1), d, :].rearrange("p a v -> p (a v)"),
                                        e_half[:, d, j:j + 1], None, ALU.mult)
            ins.then_inc(r0_ok, 1)
            dve.wait_ge(aux_ps, c * 12 + 10)
            dve.wait_ge(v_ok, c + 1)
            dve.tensor_tensor(vb, ps[:, 7, 0:T], v_c, ALU.mult).then_inc(aux_dve, 1)

            for g in range(2):
                for s in range(3):
                    dve.wait_ge(gram_ps, c * 6 + (3 * g + s + 1))
                    dst = (gb, gk)[g][s].rearrange("p h a b q -> p h (a b q)")
                    m = (trin, tri)[g][:, :, :].rearrange("p i q -> p (i q)").unsqueeze(1).to_broadcast([P, 2, 512])
                    ins = dve.tensor_tensor(dst, ps[:, 2 * s:2 * s + 2, :], m, ALU.mult)
                    ins.then_inc(gram_rd, 1)
                    if g == 0:
                        dve.wait_ge(gram_rd, c * 6 + (s + 1))
                        dve.wait_ge(i4_ok, c * 3 + (s + 1))
                        dve.sem_inc(idle_dve, 1)
                        for h in range(2):
                            ins = dve.copy_predicated(xinvT[s][:, h], lvl[:, 0, ::-1, :].bitcast(I32), gb[s][:, h, :, 0, :])
                        lc.do(ins)
                        dve.transpose(xinv[s].rearrange("p a b q -> p (a b q)"),
                                      xinvT[s].rearrange("p a b q -> p (a b q)")).then_inc(x_ok, 1)
            for l in range(1, 7):
                for s in range(3):
                    dve.wait_ge(zl_ps, c * 18 + (3 * l - 3 + s + 1))
                    dve.sem_inc(idle_dve, 1)
                    z = ps[:, 2 * s + 1, :].rearrange("p (h d q) -> p h d q", h=2, d=2)
                    zt = ps[:, 2 * s + (l == 6), :].rearrange("p (h d q) -> p h d q", h=2, d=2)
                    for h in range(2):
                        if l < 6:
                            ins = dve.copy_predicated(xinv[s][:, h], lvl[:, l, :, :].bitcast(I32), z[:, h])
                        if l >= 5:
                            ins = dve.copy_predicated(xinvT[s][:, h], lvl[:, l, ::-1, :].bitcast(I32), zt[:, h])
                    if l < 5:
                        lc.do(ins)
                        ins = dve.transpose(xinvT[s].rearrange("p a b q -> p (a b q)"),
                                            xinv[s].rearrange("p a b q -> p (a b q)"))
                    ins.then_inc(x_ok, 1)
            for s in range(3):
                if s < 2:
                    dve.wait_ge(ws_ps, c * 2 + (s + 1))
                    for d in range(2):
                        j, o = TJ[s][d], ps[:, 2 * s + 1, 384 + 64 * d:448 + 64 * d]
                        if s == 0:
                            lc.do(dve.tensor_scalar(sall[:, ds(c, 1), d, :].rearrange("p a v -> p (a v)"), o,
                                                    e_half[:, d, 0:1], None, ALU.mult))
                        else:
                            j2 = TJ[2][d]
                            lc.do(dve.tensor_tensor(r0p[:, 1, d, :], o, r0p[:, 0, d, :], ALU.add))
                            ins = dve.tensor_scalar(r0p[:, 1, d, :], r0p[:, 1, d, :], e_half[:, d, j:j + 1],
                                                    e_half[:, d, j2:j2 + 1], ALU.mult, ALU.mult)
                    if s == 1:
                        ins.then_inc(r0_ok, 1)
                dve.wait_ge(yo_ps, c * 3 + (s + 1))
                o = ps[:, 2 * s, 256:512]
                if s == 0:
                    ins = dve.tensor_copy(y_c[:, 0:P], o[:, 0:P])
                elif s == 1:
                    ins = lc.do(dve.tensor_copy(y_c[:, P:T], o))
                    ins = None
                else:
                    dve.tensor_tensor(y_c[:, P:2 * P], y_c[:, P:2 * P], o[:, P:2 * P], ALU.add)
                    ins = dve.tensor_tensor(y_c[:, 2 * P:T], y_c[:, 2 * P:T], o[:, 0:P], ALU.add)
                if s == 1:
                    dve.sem_inc(yo_rd, 1)
                else:
                    ins.then_inc(yo_rd, 1)
            dve.wait_ge(yo_rd, c * 3 + 6)
            dve.sem_inc(yc_ok, 1)
            dve.wait_ge(aux_ps, c * 12 + 11)
            dve.scalar_tensor_tensor(yc0, ps[:, 6, 0:T], -1.0 / 64, y_c, ALU.mult, ALU.add).then_inc(aux_dve, 1)
            dve.wait_ge(aux_dve, c * 2 + 4)
            dve.tensor_tensor(ysq_c, yc0, yc0, ALU.mult).then_inc(ysq_ok, 1)
            dve.wait_ge(aux_act, c * 10 + 11)
            lc.do(dve.reciprocal(ysq_c, ysq_c))
            lc.do(dve.tensor_tensor(yc0, yc0, ysq_c, ALU.mult))
            lc.do(dve.tensor_scalar(yc0, yc0, col("ln_w"), col("ln_b"), ALU.mult, ALU.add))
            lc.do(dve.tensor_tensor(yc0, yc0, vb, ALU.add))
            dve.tensor_tensor(r, yc0, g_c, ALU.mult).then_inc(pair_ok, 1)

        x1 = at(misc, 0, NTILE, D)
        g1 = at(misc, 3072, 2, D)
        g2 = at(misc, 5120, 2, D)
        h2 = at(misc, 7168, NTILE, D)
        brow = misc[0:2, 10240:12288]
        um_f = um_a[:, :, :].rearrange("p i t -> p (i t)")
        xg = at(um_f, 0, 2, D)
        xgT = at(um_f, 2048, 2, KT, P)
        yg = at(um_f, 4096, 2, D)
        hs = at(um_f, 6144, 2, DE)
        hid = at(um_f, 6656, 2, DE)
        hidT = at(um_f, 7168, 2, 2, P)
        wr = at(um_f, 7680, KT, 36)
        h2sq = at(um_f, 0, D)
        mx_f = mixm[:, :, :].rearrange("p i t -> p (i t)")
        fnw = at(mx_f, 0, D)
        ymoe = at(mx_f, 1024, D)
        lg = at(scratch, 0, NTILE, 36)
        msk = at(scratch, 108, NTILE, 32)
        tmp = at(scratch, 204, NTILE, 32)
        oh = at(scratch, 300, 2, NTILE, 32)
        both_oh = at(scratch, 492, NTILE, 32)
        slot_v = at(scratch, 588, NTILE, 32)
        ghot = at(scratch, 684, NTILE, 4)
        grp2 = at(scratch, 696, NTILE, 4)
        s3 = at(scratch, 708, 10, NTILE)
        cnt = at(scratch, 738, 4, 32)
        slots = at(scratch, 866, 2, NTILE)
        meta = at(scratch, 872, 8)
        rowsT = scratch[0:N_TILES, 880:1008]
        tokid = at(scratch, 1008, NTILE)
        erow = at(scratch, 1011, 32)
        down = at(scratch, 1043, 36)
        brt = at(scratch, 1079, 36)
        fst = mstat[:, 0:12]
        wcol = at(scratch, 1127, 2, NTILE)
        wdt_f = wdt[:, :, :].rearrange("p k c -> p (k c)")
        slots_i = wdt_f[:, 0:6].bitcast(U32)
        meta_i = wdt_f[:, 8:16].bitcast(I32)
        idx = wdt_f[:, 16:16 + N_TILES].bitcast(U32)
        idx1 = wdt_f[:, 56:58].bitcast(U32)
        zrow = vrows[0:N_TILES, 0, :]
        cmb = at(um_f, 0, 2, 2, D)
        zero_z = sem("zeros_made")
        rconst = sem("router_constants")
        half = [ring_a[:, 6144 * i:6144 * (i + 1)] for i in range(2)]
        wgu = [at(h, 0, KT, 2 * DE) for h in half]
        wdn = [at(h, 4096, 2, D) for h in half]
        h_dram = nc.dram_tensor("h_rows", [T, D], F32).ap()
        slot_dram = nc.dram_tensor("slot_tokens", [N_TILES * P, 1], F32).ap()
        y_dram = nc.dram_tensor("expert_rows", [N_TILES * P, D], F32).ap()

        x_again = sem("x_loaded_again")
        brow_in = sem("gate_bias_loaded")
        gate_ps = sem("gate_rows_in_psum")
        gate_ok = sem("gates_ready")
        bias_ok = sem("gate_rows_biased")
        out_ps = sem("mix_product_in_psum")
        x1_ok = sem("x1_ready")
        late_in = sem("router_and_norm_loaded")
        sq2_ok = sem("x1_squared")
        xn2_ok = sem("x1_normalised")
        h2T_ps = sem("x1_transposed")
        h2T_ok = sem("h2_channel_major_ready")
        h2_ps = sem("h2_transposed_back")
        h2_ok = sem("h2_token_major_ready")
        h2_out = sem("h2_rows_stored")
        lg_ps = sem("logits_in_psum")
        rt_act = sem("router_exps")
        rt_dve = sem("router_steps_for_act")
        a_ok = sem("assignments_ready")
        rank_ps = sem("ranks_in_psum")
        slots_ok = sem("slots_ready")
        zero_ok = sem("slot_table_zeroed")
        scat = sem("tokens_scattered")
        rows_in = sem("slot_rows_loaded")
        rows_ps = sem("slot_rows_transposed")
        idx_ok = sem("gather_indices_ready")
        idc = sem("index_column_ready")
        xg_in = [sem("rows_gathered_0"), sem("rows_gathered_1")]
        gu_in = [sem("gate_up_loaded_0"), sem("gate_up_loaded_1")]
        dn_in = [sem("down_loaded_0"), sem("down_loaded_1")]
        yst = [sem("expert_rows_stored_0"), sem("expert_rows_stored_1")]
        xg_ov, gu_ov, dn_ov, y_ov = sem("overflow_gathered"), sem("overflow_gate_up"), sem("overflow_down"), sem("overflow_stored")
        xt_ps = sem("rows_transposed")
        xt_rd = sem("rows_ready")
        gu_ps = sem("gate_up_in_psum")
        silu_ok = sem("silu_ready")
        hid_ok = sem("hidden_ready")
        ht_ps = sem("hidden_transposed")
        ht_rd = sem("hidden_channel_major_ready")
        dn_ps = sem("down_in_psum")
        yg_ok = sem("expert_rows_ready")
        comb = [sem("combined_rows_0"), sem("combined_rows_1")]
        moe_ok = sem("moe_summed")
        y_ok = sem("y_ready")

        def wout_block(n):
            return ring[:, n % RING].rearrange("p k c -> p (k c)").rearrange("p (k c) -> p k c", k=4)

        def gate_rows(pe, i):
            pe.wait_ge(bias_ok, i + 1)
            for v in range(2):
                if i:
                    pe.wait_ge(gate_ok, 2 * i - 1 + v)
                pe.matmul(ps[:, 6 + v, :], selb[:, v, :], adas[:, i % 2, :], start=True, stop=True).then_inc(gate_ps, 1)

        def gather(pool, n, b, ov=None):
            if ov is None:
                if not (isinstance(n, int) and n < 2):
                    pool.wait_ge(xt_ps, n - 1)
            else:
                pool.wait_ge(dn_ps, n)
            pool.sem_inc(idle_pool, 1)
            pool.tensor_copy(idx1[:, b:b + 1], idx[:, ds(n, 1)]).then_inc(idc, 1)
            pool.wait_ge(idc, n + 1)
            pool.sem_inc(idle_pool, 1)
            pool.indirect_dma_start(out=xg[:, b, :], out_offset=None, in_=h_dram,
                                    in_offset=bass.IndirectOffsetOnAxis(ap=idx1[:, b:b + 1], axis=0)
                                    ).then_inc(xg_in[b] if ov is None else xg_ov, 16)

        def expert_weights(sp, n, e, b, ov=False):
            if ov:
                sp.wait_ge(dn_ps, n)
            elif not (isinstance(n, int) and n < 2):
                sp.wait_ge(gu_ps, n - 1)
            for i, name in enumerate(("moe_w_gate", "moe_w_up")):
                sp.dma_start(wgu[b][:, :, DE * i:DE * i + DE],
                             a[name][0, ds(e, 1)].rearrange("a (k p) f -> p (a k) f", p=P)).then_inc(gu_ov if ov else gu_in[b], 16)
            if not ov and not (isinstance(n, int) and n < 2):
                sp.wait_ge(dn_ps, n - 1)
            sp.dma_start(wdn[b], a["moe_w_down"][0, ds(e, 1)].rearrange("a (k p) c -> p (a k) c", p=P)
                         ).then_inc(dn_ov if ov else dn_in[b], 16)

        def rows_T(pe, n, b):
            if not (isinstance(n, int) and n < 1):
                pe.wait_ge(xt_rd, n)
            for k in range(KT):
                mm = pe.transpose(ps[:, k // 4, P * (k % 4):P * (k % 4) + P], xg[:, b, P * k:P * k + P], ident[:, :])
            mm.then_inc(xt_ps, 1)

        def gate_up(pe, n, b):
            pe.wait_ge(xt_rd, n + 1)
            if not (isinstance(n, int) and n < 2):
                pe.wait_ge(hid_ok, n - 1)
            for k in range(KT):
                mm = pe.matmul(ps[:, 2 + b, :], xgT[:, b, k, :], wgu[b][:, k, :], start=(k == 0), stop=(k == KT - 1))
            mm.then_inc(gu_ps, 1)

        def down_proj(pe, m, b):
            pe.wait_ge(hid_ok, m + 1)
            if not (isinstance(m, int) and m < 1):
                pe.wait_ge(ht_rd, m)
            for k in range(2):
                mm = pe.transpose(ps[:, 4, P * k:P * k + P], hid[:, b, P * k:P * k + P], ident[:, :])
            mm.then_inc(ht_ps, 1)
            pe.wait_ge(ht_rd, m + 1)
            if not (isinstance(m, int) and m < 1):
                pe.wait_ge(yg_ok, m)
            for c in range(2):
                for k in range(2):
                    mm = pe.matmul(ps[:, 5 + c, :], hidT[:, b, k, :], wdn[b][:, k, BLK * c:BLK * c + BLK],
                                   start=(k == 0), stop=(k == 1))
            mm.then_inc(dn_ps, 1)

        def rows_copy(dve, n, b):
            dve.wait_ge(xt_ps, n + 1)
            if not (isinstance(n, int) and n < 2):
                dve.wait_ge(gu_ps, n - 1)
            dve.tensor_copy(xgT[:, b, :, :].rearrange("p (g k) t -> p g (k t)", g=2), ps[:, 0:2, :]).then_inc(xt_rd, 1)

        def hidden(dve, m, b):
            dve.wait_ge(silu_ok, m + 1)
            if not (isinstance(m, int) and m < 2):
                dve.wait_ge(ht_ps, m - 1)
            dve.tensor_tensor(hid[:, b, :], hs[:, b, :], ps[:, 2 + b, DE:2 * DE], ALU.mult).then_inc(hid_ok, 1)
            dve.wait_ge(ht_ps, m + 1)
            if not (isinstance(m, int) and m < 2):
                dve.wait_ge(dn_ps, m - 1)
            dve.tensor_copy(hidT[:, b, :, :].rearrange("p k t -> p (k t)"), ps[:, 4, 0:256]).then_inc(ht_rd, 1)

        def silu_gate(act, n, b):
            act.wait_ge(gu_ps, n + 1)
            if not (isinstance(n, int) and n < 2):
                act.wait_ge(hid_ok, n - 1)
            act.activation(hs[:, b, :], ps[:, 2 + b, 0:DE], ACT.Silu).then_inc(silu_ok, 1)

        def expert_out(act, m, b, ov=None):
            act.wait_ge(dn_ps, m + 1)
            if ov is not None:
                act.wait_ge(yst[b], 16 * (NE // 2))
                act.wait_ge(y_ov, ov * 16 + 16)
            elif not (isinstance(m, int) and m < 2):
                act.wait_ge(yst[b], (m - b) * 8)
            act.activation(yg[:, b, :].rearrange("p (c n) -> p c n", c=2), ps[:, 5:7, :], ACT.Copy).then_inc(yg_ok, 1)
            act.wait_ge(yg_ok, m + 1)
            act.dma_start(y_dram[ds(m * P, P), :], yg[:, b, :]).then_inc(yst[b] if ov is None else y_ov, 16)

        block = ctx.enter_context(nc.Block())

        @block.sync
        def _(sp):
            rows = [(vrows[0:48, 0, :], a["b_ada"].rearrange("a (t p) -> (a t) p", p=P)),
                    (vrows[48:56, 0, :], a["norm1_w"].rearrange("a (t p) -> (a t) p", p=P)),
                    (vrows[56:116, 0, :], a["m_conv_w"].rearrange("a j (t p) -> (a j t) p", p=P)),
                    (vrows[116:128, 0, :], a["m_conv_b"].rearrange("a (t p) -> (a t) p", p=P)),
                    (vrows[0:27, 1, :], a["r_mu"].rearrange("a (t p) -> (a t) p", p=P)),
                    (vrows[27:43, 1, :], a["r_w0"].rearrange("a d (t p) -> (a d t) p", p=P)),
                    (vrows[43:59, 1, :], a["r_a0"].rearrange("a d (t p) -> (a d t) p", p=P)),
                    (vrows[59:67, 1, :], a["r_k_k"].rearrange("a (t p) -> (a t) p", p=P)),
                    (vrows[67:75, 1, :], a["r_k_a"].rearrange("a (t p) -> (a t) p", p=P)),
                    (vrows[75:83, 1, :], a["r_r_k"].rearrange("a (t h) n -> (a t) (h n)", h=2)),
                    (vrows[83:91, 1, :], a["r_ln_w"].rearrange("a (t p) -> (a t) p", p=P)),
                    (vrows[91:99, 1, :], a["r_ln_b"].rearrange("a (t p) -> (a t) p", p=P)),
                    (vrows[99:107, 1, :], a["norm2_w"].rearrange("a (t p) -> (a t) p", p=P)),
                    (vrows[107:115, 1, :], a["m_norm_w"].rearrange("a (t p) -> (a t) p", p=P)),
                    (crows[0:8, :], a["c_ctx"].rearrange("(t p) -> t p", p=P)),
                    (crows[8:16, :], a["c"].rearrange("a (t p) -> (a t) p", p=P)),
                    (drow[:, 0:32], a["m_dt_bias"].rearrange("a d h -> a (d h)").broadcast_to([P, 32])),
                    (drow[:, 32:64], a["m_a_log"].rearrange("a d h -> a (d h)").broadcast_to([P, 32])),
                    (drow[:, 64:80], a["m_d_skip"].broadcast_to([P, 16]))]
            assert len(rows) == N_SMALL
            for dst, src in rows:
                sp.dma_start(dst, src).then_inc(s_small, 16)
            sp.dma_start(xt[:, 0, :], a["x_prompt"][0]).then_inc(s_x, 16)
            sp.dma_start(xt[:, 1:3, :], a["x_sample"][0].rearrange("(j p) c -> p j c", p=P)).then_inc(s_x, 16)
            for n in range(GATES):
                if n >= RING:
                    block_used(sp, n - RING)
                src = block_source(n)
                sp.dma_start(slot(n)[:, :, 0:src.shape[2]], src).then_inc(w_in_slot[n % RING], 16)
                if n == XB:
                    sp.dma_start(wdt[:, :, :], w_in_v[:, :, DTC:DTC + 32]).then_inc(s_wdt, 16)
            sp.wait_ge(zero_z, 1)
            zsrc = zrow[0:32, :].unsqueeze(1)
            sp.dma_start(y_dram[NE * P:N_TILES * P, :].rearrange("(p r) (s c) -> p (r s) c", p=32, c=P),
                         zsrc.to_broadcast([32, N_OVER * P * D // P // 32, P])).then_inc(zero_ok, 16)
            sp.dma_start(slot_dram.rearrange("(n p) a -> n (p a)", p=P), zrow[:, :]).then_inc(zero_ok, 16)
            sp.wait_ge(ada_ps, 6)
            for d, name in enumerate(("state_ssm_fwd", "state_ssm_bwd")):
                sp.dma_start(st_in[:, d], a[name][0, 0].rearrange("(i h) p n -> (h p) i n", h=2)).then_inc(st_loaded, 16)
            for d in range(2):
                sp.wait_ge(cst_out, d + 1)
                sp.dma_start(out[2 + d][0, 0].rearrange("(i h) p n -> (h p) i n", h=2), st_out[:, d]).then_inc(out_done, 16)
            sp.wait_ge(conv_tm, 10)
            sp.wait_ge(conv_out, XBC)
            for d, name in enumerate(("state_wkv_fwd", "state_wkv_bwd")):
                sp.dma_start(wkv_in[:, d, :].rearrange("v (h n) -> v h n", h=16),
                             a[name][0, 0].rearrange("h v n -> v h n")).then_inc(wkv_loaded, 16)

            ups = [a["r_w_up"][0].rearrange("d r c -> (d r) c"), a["r_a_up"][0].rearrange("d r c -> (d r) c"),
                   a["r_g_up"][0]]
            for i, w in enumerate(ups):
                sp.dma_start(stw[:, i, :], w[:, 0:P]).then_inc(up_loaded, 16)
            with sp.Fori(0, 7) as c:
                sp.wait_ge(aux_ps, c * 12 + 6)
                for i, w in enumerate(ups):
                    sp.dma_start(stw[:, i, :], w[:, ds(c * P + P, P)]).then_inc(up_loaded, 16)
            sp.wait_ge(pair_ok, 9)
            x_row = [(x1[:, 0, :], a["x_prompt"][0]),
                     (x1[:, 1:3, :], a["x_sample"][0].rearrange("(j p) c -> p j c", p=P))]
            for v in range(2):
                for i, c in enumerate((2, 5)):
                    sp.dma_start(brow[v:v + 1, D * i:D * i + D], a["b_ada"][:, D * c:D * c + D]).then_inc(brow_in, 16)
            for n in range(GATES, WOUT + 4):
                if n >= GATES + RING:
                    block_used(sp, n - RING)
                if n < WOUT:
                    c = (4, 5, 10, 11)[n - GATES]
                    sp.dma_start(slot(n), w_ada_v[:, :, BLK * c:BLK * (c + 1)]).then_inc(w_in_slot[n % RING], 16)
                else:
                    q = n - WOUT
                    sp.dma_start(wout_block(n), a["w_out"][0, BLK * q:BLK * (q + 1)].rearrange("(k p) c -> p k c", p=P)
                                 ).then_inc(w_in_slot[n % RING], 16)
                if n == GATES + 2:
                    for dst, src in x_row:
                        sp.dma_start(dst, src).then_inc(x_again, 16)
            sp.wait_ge(fin_sb, 2)
            for d in range(2):
                sp.dma_start(out[4 + d][0, 0].rearrange("h v n -> v h n"),
                             wkv_in[:, d, :].rearrange("v (h n) -> v h n", h=16)).then_inc(out_done, 16)
            sp.wait_ge(out_done, 16 * 4)
            sp.wait_ge(out_ps, 4)
            sp.dma_start(brt[:, 0:4], a["moe_b_grp"].broadcast_to([P, 4])).then_inc(late_in, 16)
            sp.dma_start(brt[:, 4:36], a["moe_b_exp"].broadcast_to([P, 32])).then_inc(late_in, 16)
            sp.dma_start(wr[:, :, 0:4], a["moe_w_grp"][0].rearrange("(k p) c -> p k c", p=P)).then_inc(late_in, 16)
            sp.dma_start(wr[:, :, 4:36], a["moe_w_exp"][0].rearrange("(k p) c -> p k c", p=P)).then_inc(late_in, 16)
            sp.dma_start(fnw, a["final_norm_w"].rearrange("(a c) -> a c", a=1).broadcast_to([P, D])).then_inc(late_in, 16)
            for n in range(2):
                expert_weights(sp, n, n, n)
            sp.wait_ge(h2_ok, 3)
            sp.dma_start(h_dram.rearrange("(j p) c -> p j c", p=P), h2).then_inc(h2_out, 16)
            sp.wait_ge(scat, 16 * 6)
            sp.dma_start(rowsT, slot_dram.rearrange("(n p) a -> n (p a)", p=P)).then_inc(rows_in, 16)
            with sp.Fori(1, NE // 2) as i:
                for b in range(2):
                    expert_weights(sp, i * 2 + b, i * 2 + b, b)
            n_over = sp.value_load(meta_i[0:1, N_OVER:N_OVER + 1], min_val=1, max_val=N_OVER)
            with sp.Fori(0, n_over) as q:
                e = sp.value_load(meta_i[0:1, ds(q, 1)], min_val=0, max_val=NE - 1)
                expert_weights(sp, q + NE, e, 0, ov=True)
            for j in range(NTILE):
                sp.wait_ge(y_ok, j + 1)
                dst = out[0][0] if j == 0 else out[1][0, P * (j - 1):P * j, :]
                sp.dma_start(dst, x1[:, j, :]).then_inc(out_done, 16)
            sp.wait_ge(out_done, 16 * 7)
            if dump:
                for eng_sem, v in dump["after"](s_bufs):
                    sp.wait_ge(eng_sem, v)
                nd = 0
                for name, (ap, _) in dump["what"](s_bufs).items():
                    sp.dma_start(dump["to"][name], ap).then_inc(out_done, 16)
                    nd += 1
                sp.wait_ge(out_done, 16 * (nd + N_OUT))

        @block.gpsimd
        def _(pool):
            g = Chain(pool, pool_c)
            pool.memset(ident[:, :], 0.0)
            pool.memset(ones[:, :], 1.0)
            pool.memset(tri[:, :, :], 1.0)
            pool.memset(lvl[:, :, :, :], 0.0)
            pool.memset(rst[:, :, :], 1.0)
            pool.memset(cond[:, :, :], 0.0)
            g.do(pool.memset(raw[:, :, :], 0.0))
            pool.affine_select(out=ident[:, :], in_=ident[:, :], compare_op=ALU.not_equal, fill=1.0, base=0,
                               pattern=[[-1, P]], channel_multiplier=1)
            for i, (step, cm, base) in enumerate([(1, -1, -1), (1, -1, 0), (-1, 1, -1), (-1, 1, 0)]):
                ins = pool.affine_select(out=tri[:, i, :], in_=tri[:, i, :], compare_op=ALU.is_ge, fill=0.0, base=base,
                                   pattern=[[step, P]], channel_multiplier=cm)
            g.did(ins)
            pool.memset(rst[:, 0, :].rearrange("p (j t) -> p j t", j=NTILE)[:, :, 0:1], 0.0)
            pool.memset(rst[:, 1, :].rearrange("p (j t) -> p j t", j=NTILE)[:, :, P - 1:P], 0.0)
            g.wait()
            pool.tensor_scalar(trin[:, :, :], tri[:, :, :], -1.0, None, ALU.mult).then_inc(const_ready, 1)
            for l in range(7):
                b = 1 << l
                for up in range(2):
                    v = lvl[:, l, up, :].rearrange("p (n h b) -> p n h b", h=2, b=b)[:, :, up, :]
                    g.do(pool.memset(v, 1.0))
                    lo = 0 if up else -b
                    g.do(pool.affine_select(out=v, in_=v, compare_op=ALU.is_ge, fill=0.0, base=lo,
                                            pattern=[[-2 * b, P // (2 * b)], [0, b]], channel_multiplier=1))
                    g.do(pool.affine_select(out=v, in_=v, compare_op=ALU.is_ge, fill=0.0, base=-lo + b - 1,
                                            pattern=[[2 * b, P // (2 * b)], [0, b]], channel_multiplier=-1))
            pool.nop().then_inc(masks_ready, 1)
            pool.wait_ge(vec_t, 1)
            pool.memset(zrow[:, :], 0.0).then_inc(zero_z, 1)
            pool.wait_ge(la_ready, 1)
            pool.wait_ge(proj, XBC + 6 + RT)
            with pool.Fori(0, NTILE) as j:
                for i in range(4):
                    pool.wait_ge(seg_ps, j * 4 + (i + 1))
                    for d in range(2):
                        h0 = 16 * d + 4 * i
                        ins = pool.tensor_tensor(
                            lam[:, i % 2, 4 * d:4 * d + 4, :],
                            tri[:, 2 - 2 * d, :].unsqueeze(1).to_broadcast([P, 4, P]),
                            la[:, ds(j, 1), h0:h0 + 4].rearrange("p a h -> p (a h)").unsqueeze(2).to_broadcast([P, 4, P]),
                            ALU.mult)
                    ins.then_inc(lam_ok, 1)

            pool.wait_ge(off_ps, 8)
            pool.wait_ge(cst_out, 2)
            pool.wait_ge(seg_ps, 14)
            with pool.Fori(0, 8) as c:
                pool.wait_ge(pair_ok, c + 1)
                pool.sem_inc(idle_pool, 1)
                pool.tensor_copy(v_c, um_a[:, ds(c + 16, 1), :].rearrange("p a t -> p (a t)")).then_inc(v_ok, 1)
                for s in range(3):
                    pool.wait_ge(u_ps, c * 3 + (s + 1))
                    pool.sem_inc(idle_pool, 1)
                    pool.tensor_copy(xinvT[s].rearrange("p a b q -> p (a b) q"),
                                     ident[:, :].unsqueeze(1).to_broadcast([P, 4, P])).then_inc(i4_ok, 1)

            pool.wait_ge(out_done, 16 * 4)
            pool.iota(tokid, pattern=[[P, NTILE]], base=0, channel_multiplier=1, allow_small_or_imprecise_dtypes=True)
            pool.iota(erow, pattern=[[1, 32]], base=0, channel_multiplier=0, allow_small_or_imprecise_dtypes=True)
            pool.iota(down[:, 0:4], pattern=[[-1, 4]], base=4, channel_multiplier=0, allow_small_or_imprecise_dtypes=True)
            pool.iota(down[:, 4:36], pattern=[[-1, 32]], base=32, channel_multiplier=0,
                      allow_small_or_imprecise_dtypes=True).then_inc(rconst, 1)
            pool.wait_ge(rconst, 1)
            pool.wait_ge(zero_ok, 32)
            pool.wait_ge(slots_ok, 1)
            for i in range(6):
                pool.indirect_dma_start(out=slot_dram, out_offset=bass.IndirectOffsetOnAxis(ap=slots_i[:, i:i + 1], axis=0),
                                        in_=tokid[:, i % 3:i % 3 + 1], in_offset=None).then_inc(scat, 16)
            pool.wait_ge(h2_out, 16)
            pool.wait_ge(idx_ok, 1)
            for n in range(2):
                gather(pool, n, n)
            with pool.Fori(1, NE // 2) as i:
                for b in range(2):
                    gather(pool, i * 2 + b, b)
            n_over = pool.value_load(meta_i[0:1, N_OVER:N_OVER + 1], min_val=1, max_val=N_OVER)
            with pool.Fori(0, n_over) as q:
                gather(pool, q + NE, 0, ov=q)
            pool.wait_ge(yst[0], 16 * (NE // 2))
            pool.wait_ge(yst[1], 16 * (NE // 2))
            pool.wait_ge(y_ov, n_over * 16 + 16)
            pool.sem_inc(idle_pool, 1)
            for j in range(NTILE):
                if j == 2:
                    pool.wait_ge(moe_ok, 1)
                for k in range(2):
                    pool.indirect_dma_start(out=cmb[:, j % 2, k, :], out_offset=None, in_=y_dram,
                                            in_offset=bass.IndirectOffsetOnAxis(ap=slots_i[:, 3 * k + j:3 * k + j + 1], axis=0)
                                            ).then_inc(comb[j % 2], 16)

        @block.tensor
        def _(pe):
            pe.wait_ge(const_ready, 1)
            pe.wait_ge(s_small, 16 * N_SMALL)
            pe.transpose(ps[:, 0, 0:16], crows[:, :], ident[0:16, 0:16])
            pe.transpose(ps[:, 1, 0:P], vrows[:, 0, :], ident[:, :])
            pe.transpose(ps[:, 2, 0:V1N], vrows[0:V1N, 1, :], ident[0:V1N, 0:V1N]).then_inc(vec_t, 1)

            def ada_block(n, i):
                block_ready(pe, n)
                if i >= 2:
                    pe.wait_ge(ada_sb, i - 1)
                for k2 in range(2):
                    for q in range(4):
                        mm = pe.matmul(ps[32 * q:32 * q + 32, 4 + i % 2, :], cond[:, 2 * q + k2, :],
                                       slot(n)[:, 2 * q + k2, :], start=(k2 == 0), stop=(k2 == 1),
                                       tile_position=(0, 32 * q), skip_group_check=True)
                mm.then_inc(ada_ps, 1)

            def ada_columns(i):
                pe.wait_ge(ada_sb, i + 1)
                for c in range(4):
                    o = 8 * i + 2 * c
                    mm = pe.matmul(ps[:, 6, o:o + 2], adas[:, i % 2, P * c:P * c + P], sel32[:, 0:2],
                                   start=True, stop=True)
                mm.then_inc(ada_cols, 1)

            pe.wait_ge(cond_ready, 1)
            for i in range(4):
                ada_block(ADA_A + i, i)
                if i:
                    ada_columns(i - 1)
            ada_columns(3)

            pe.wait_ge(xn_ready, 1)
            for k in range(KT):
                if k >= 4:
                    pe.wait_ge(hT_ready, k - 3)
                for j in range(NTILE):
                    mm = pe.transpose(ps[:, k % 4, P * j:P * j + P], xt[:, j, P * k:P * k + P], ident[:, :])
                mm.then_inc(xT_ps, 1)

            def project(n, c, t):
                for k in range(KT):
                    mm = pe.matmul(ps[:, t % 4 if isinstance(t, int) else t, 0:T],
                                   slot(n)[:, k, P * c:P * c + P], hT[:, k, :],
                                   start=(k == 0), stop=(k == KT - 1))
                return mm

            def conv_transpose(t):
                pe.wait_ge(conv_out, t + 1)
                if t >= 2:
                    pe.wait_ge(conv_tm, t - 1)
                src = bct[:, t - 8, :] if t >= 8 else acc[:, t % 2, :]
                for j in range(NTILE):
                    if t >= 8:
                        v = src[:, P * j:P * j + P]
                    else:
                        v = src[:, P * j + (2 if j else 0):P * j + (2 if j else 0) + P]
                    mm = pe.transpose(ps[:, 4 + t % 2, P * j:P * j + P], v, ident[:, :])
                mm.then_inc(conv_T, 1)

            pe.wait_ge(hT_ready, KT)
            for t in range(XBC):
                if t % 4 == 0:
                    block_ready(pe, XB + t // 4)
                if t >= 4:
                    pe.wait_ge(proj_read, t - 3)
                mm = project(XB + t // 4, t % 4, t)
                mm.then_inc(proj, 1)
                if 2 <= t < 12:
                    conv_transpose(t - 2)
            for i in range(6):
                n, j = Z + i // 3, i % 3
                if j == 0:
                    block_ready(pe, n)
                pe.wait_ge(proj_read, XBC - 3 + i)
                for k in range(KT):
                    mm = pe.matmul(ps[:, i % 4, :], hT[:, k, P * j:P * j + P], slot(n)[:, k, :],
                                   start=(k == 0), stop=(k == KT - 1))
                mm.then_inc(proj, 1)
            pe.wait_ge(s_wdt, 16)
            for j in range(NTILE):
                for k in range(KT):
                    mm = pe.matmul(ps[:, 7, 32 * j:32 * j + 32], hT[:, k, P * j:P * j + P], wdt[:, k, :],
                                   start=(k == 0), stop=(k == KT - 1))
            mm.then_inc(dt_ps, 1)
            with pe.Fori(0, 2) as r:
                for n in range(RING):
                    pe.wait_ge(w_in_slot[n], 64 + 16 * r)
                    for c in range(4):
                        pe.wait_ge(proj_read, r * 12 + (XBC + 6 + 4 * n + c - 3))
                        mm = project(R + n, c, (XBC + 6 + 4 * n + c) % 4)
                        mm.then_inc(proj, 1)
            block_ready(pe, R + 6)
            for c in range(3):
                pe.wait_ge(proj_read, XBC + 6 + 24 + c - 3)
                mm = project(R + 6, c, XBC + 6 + 24 + c)
                mm.then_inc(proj, 1)

            pe.wait_ge(proj_read, XBC + 6 + RT)
            pe.wait_ge(conv_tm, 10)
            for i in range(4, 8):
                ada_block(ADA_B + i - 4, i)
                if i > 4:
                    ada_columns(i - 1)
            ada_columns(7)

            pe.sem_inc(seg_ps, 2)
            pe.sem_inc(y_ps, 2)
            pe.wait_ge(la_ready, 1)
            for i, (m, lo) in enumerate(((1, 0), (3, 16), (2, 0), (0, 16))):
                pe.matmul(ps[:, 7, 48 * i:48 * i + 48], tri[:, m, :], la[:, :, lo:lo + 16], start=True, stop=True)
            pe.matmul(ps[:, 7, 192:288], ones[:, :], la[:, :, :], start=True, stop=True).then_inc(cs_ps, 1)
            for i in range(6):
                j, grp = i // 2, i % 2
                mm = pe.matmul(ps[:, 4 + i // 4, P * (i % 4):P * (i % 4) + P], bct[:, grp, P * j:P * j + P],
                               bct[:, 2 + grp, P * j:P * j + P], start=True, stop=True)
            mm.then_inc(score_ps, 1)
            pe.wait_ge(st_loaded, 32)
            for d in range(2):
                for i in range(8):
                    mm = pe.transpose(ps[:, 2 * d + i // 4, P * (i % 4):P * (i % 4) + P], st_in[:, d, i, :], ident[:, :])
            mm.then_inc(st_T, 1)
            for job in range(4):
                d, j = job % 2, (0, 0, 1, 2)[job]
                pe.wait_ge(xdw_ok, job + 1)
                if job == 0:
                    pe.wait_ge(st0_ok, 1)
                if job >= 2:
                    pe.wait_ge(cst_out, job - 1)
                b = 2 * d
                if job < 2:
                    for i in range(8):
                        grp = i // 4
                        mm = pe.matmul(ps[:, b + i // 4, P * (i % 4):P * (i % 4) + P], xdw[:, job % 2, P * i:P * i + P],
                                       btm[:, j, P * grp:P * grp + P], start=True, stop=True)
                else:
                    for grp in range(2):
                        mm = pe.matmul(ps[:, b + grp, :], btm[:, j, P * grp:P * grp + P],
                                       xdw[:, job % 2, BLK * grp:BLK * grp + BLK], start=True, stop=True)
                mm.then_inc(cst_ps, 1)
            pe.wait_ge(st1_ok, 1)
            pe.wait_ge(score_ok, 1)

            def seg_sums(j, i):
                pe.wait_ge(lam_ok, j * 4 + (i + 1))
                pe.wait_ge(seg_exp, j * 4 + (i + 1))
                for d in range(2):
                    for h in range(4):
                        mm = pe.matmul(ps[:, 2 * (i % 2) + d, P * h:P * h + P], lam[:, i % 2, 4 * d + h, :],
                                       tri[:, 1 + 2 * d, :], start=True, stop=True)
                mm.then_inc(seg_ps, 1)

            def y_heads(j, i):
                pe.wait_ge(g_ok, j * 4 + (i + 1))
                if i % 2 == 0:
                    pe.wait_ge(y_sb, j * 2 + (i // 2 + 1))
                for h in range(4):
                    o = 64 * (4 * (i % 2) + h)
                    for d in range(2):
                        mm = pe.matmul(ps[:, 4 + i // 2, o:o + 64], seg[:, i % 2, 4 * d + h, :],
                                       xs[:, ds(j, 1), 64 * (4 * i + h):64 * (4 * i + h) + 64].rearrange("p a c -> p (a c)"),
                                       start=(d == 0), stop=(d == 1))
                mm.then_inc(y_ps, 1)

            with pe.Fori(0, NTILE) as j:
                seg_sums(j, 0)
                for i in range(1, 4):
                    seg_sums(j, i)
                    y_heads(j, i - 1)
                y_heads(j, 3)

            pe.wait_ge(seg_exp, 12 + 2)
            for o, (j, d, src) in enumerate(OFF):
                pe_src = (st0, st1)[src]
                for grp in range(2):
                    i = 2 * o + grp
                    if i >= 4:
                        pe.wait_ge(off_rd, i - 3)
                    pe.matmul(ps[:, i % 4, :], bct[:, 2 + grp, P * j:P * j + P], pe_src[:, d, BLK * grp:BLK * grp + BLK],
                              start=True, stop=True).then_inc(off_ps, 1)
            pe.wait_ge(ynorm, 1)
            for t in range(8):
                if t >= 2:
                    pe.wait_ge(yT_sb, t - 1)
                for j in range(NTILE):
                    mm = pe.transpose(ps[:, 6 + t % 2, P * j:P * j + P], xs[:, j, P * t:P * t + P], ident[:, :])
                mm.then_inc(yT_ps, 1)

            pe.wait_ge(yT_sb, 8)
            pe.wait_ge(wkv_loaded, 32)
            for d in range(2):
                for i in range(8):
                    mm = pe.transpose(ps[:, 6 + d, 64 * i:64 * i + 64], wkv_in[:, d, P * i:P * i + P], ident[0:64, 0:64])
            mm.then_inc(wkv_T, 1)
            pe.wait_ge(wkv_ok, 1)
            pe.wait_ge(wd_ok, 1)
            pe.sem_inc(u_ps, 3)
            with pe.Fori(0, 8) as c:
                wkv_pair_pe(pe, c)
            pe.wait_ge(pair_ok, 9)
            for d in range(2):
                for i in range(8):
                    mm = pe.transpose(ps[0:64, 2 * d + i // 4, P * (i % 4):P * (i % 4) + P], sall[:, i, d, :], ident[:, :])
                mm.then_inc(fin_T, 1)

            for i in range(4):
                ada_block(GATES + i, 8 + i)
                if i:
                    gate_rows(pe, i - 1)
            gate_rows(pe, 3)

            pe.wait_ge(fin_sb, 2)
            pe.wait_ge(gate_ok, 8)
            for q in range(4):
                block_ready(pe, WOUT + q)
                w = wout_block(WOUT + q)
                for k in range(4):
                    kk_ = 4 * q + k
                    src = mixm[:, kk_, :] if kk_ < 8 else um_a[:, kk_ - 8, :]
                    for j in range(NTILE):
                        for c in range(2):
                            mm = pe.matmul(ps[:, 2 * j + c, :], src[:, P * j:P * j + P], w[:, k, BLK * c:BLK * c + BLK],
                                           start=(kk_ == 0), stop=(kk_ == 15))
                mm.then_inc(out_ps, 1)
            pe.wait_ge(xn2_ok, 1)
            for k in range(KT):
                if k >= 2:
                    pe.wait_ge(h2T_ok, k - 1)
                for j in range(NTILE):
                    mm = pe.transpose(ps[:, 6 + k % 2, P * j:P * j + P], h2[:, j, P * k:P * k + P], ident[:, :])
                mm.then_inc(h2T_ps, 1)
            pe.wait_ge(h2T_ok, 8)
            pe.wait_ge(late_in, 16 * 5)
            for j in range(NTILE):
                for k in range(KT):
                    mm = pe.matmul(ps[:, 6, 36 * j:36 * j + 36], hT[:, k, P * j:P * j + P], wr[:, k, :],
                                   start=(k == 0), stop=(k == KT - 1))
            mm.then_inc(lg_ps, 1)
            for j in range(NTILE):
                for k in range(KT):
                    mm = pe.transpose(ps[:, 2 * j + k // 4, P * (k % 4):P * (k % 4) + P], hT[:, k, P * j:P * j + P], ident[:, :])
                mm.then_inc(h2_ps, 1)
            pe.wait_ge(a_ok, 1)
            for j in range(NTILE):
                for i in range(j + 1):
                    mm = pe.matmul(ps[:, 7, 32 * j:32 * j + 32], tri[:, 0, :] if i == j else ones[:, :], both_oh[:, i, :],
                                   start=(i == 0), stop=(i == j))
            for i in range(NTILE):
                mm = pe.matmul(ps[:, 7, 96:128], ones[:, :], both_oh[:, i, :], start=(i == 0), stop=(i == 2))
            mm.then_inc(rank_ps, 1)
            pe.wait_ge(rows_in, 16)
            pe.wait_ge(h2_ok, 3)
            pe.transpose(ps[:, 6, 0:N_TILES], rowsT, ident[0:N_TILES, 0:N_TILES]).then_inc(rows_ps, 1)

            def pe_tile(n, b, first=False, last=False):
                pe.wait_ge(gu_in[b], (n - b) * 16 + 32)
                gate_up(pe, n, b)
                if not first:
                    pe.wait_ge(dn_in[1 - b], (n - 1 - (1 - b)) * 8 + 16)
                    down_proj(pe, n - 1, 1 - b)
                if not last:
                    pe.wait_ge(xg_in[1 - b], (n + 1 - (1 - b)) * 8 + 16)
                    rows_T(pe, n + 1, 1 - b)

            pe.wait_ge(xg_in[0], 16)
            rows_T(pe, 0, 0)
            for n in range(2):
                pe_tile(n, n, first=(n == 0))
            with pe.Fori(1, NE // 2 - 1) as i:
                for b in range(2):
                    pe_tile(i * 2 + b, b)
            for b in range(2):
                pe_tile(NE - 2 + b, b, last=(b == 1))
            pe.wait_ge(dn_in[1], 8 * NE)
            down_proj(pe, NE - 1, 1)
            n_over = pe.value_load(meta_i[0:1, N_OVER:N_OVER + 1], min_val=1, max_val=N_OVER)
            with pe.Fori(0, n_over) as q:
                pe.wait_ge(xg_ov, q * 16 + 16)
                rows_T(pe, q + NE, 0)
                pe.wait_ge(gu_ov, q * 32 + 32)
                gate_up(pe, q + NE, 0)
                pe.wait_ge(dn_ov, q * 16 + 16)
                down_proj(pe, q + NE, 0)


        @block.scalar
        def _(act):
            g = Chain(act, act_c)
            act.wait_ge(s_x, 32)
            act.wait_ge(const_ready, 1)
            for j in range(NTILE):
                g.did(act.activation(zs[:, j, :], xt[:, j, :], ACT.Square, accum_out=stat[:, j:j + 1]))
            act.wait_ge(meansq, 1)
            act.activation(stat[:, 12:15], stat[:, 4:7], ACT.Sqrt).then_inc(rstd, 1)
            act.wait_ge(vec_t, 1)
            act.activation(cond[:, :, 0:2], ps[:, 0, 0:16].rearrange("p (v k) -> p k v", v=2),
                           ACT.Silu).then_inc(cond_ready, 1)
            for i in range(4):
                act.wait_ge(ada_ps, i + 1)
                if i >= 2:
                    act.wait_ge(ada_cols, i - 1)
                ins = act.activation(adas[:, i % 2, :], ps[:, 4 + i % 2, :], ACT.Copy)
                ins.then_inc(ada_sb, 1)
            def conv_in(t):
                act.wait_ge(proj, t + 1)
                if t >= 2:
                    act.wait_ge(conv_acc, t - 1)
                act.activation(raw[:, t % 2, 2:2 + P], ps[:, t % 4, 0:P], ACT.Copy)
                ins = act.activation(raw[:, t % 2, 4 + P:4 + T], ps[:, t % 4, P:T], ACT.Copy)
                ins.then_inc(proj_read, 1)

            def conv_silu(t):
                act.wait_ge(conv_acc, t + 1)
                bias = pv0[:, V0["conv_b"] + t:V0["conv_b"] + t + 1]
                for o, i, n in ((0, 0, P), (P, P + 2, T - P)):
                    src = acc[:, t % 2, i:i + n]
                    dst = bct[:, t - 8, o:o + n] if t >= 8 else src
                    ins = act.activation(dst, src, ACT.Silu, bias=bias)
                ins.then_inc(conv_out, 1)

            for t in range(XBC):
                conv_in(t)
                if t:
                    conv_silu(t - 1)
            conv_silu(XBC - 1)
            for i in range(6):
                act.wait_ge(proj, XBC + i + 1)
                n, j = i // 3, i % 3
                ins = act.activation(zs[:, j, BLK * n:BLK * n + BLK], ps[:, i % 4, :], ACT.Silu)
                ins.then_inc(proj_read, 1)
            act.wait_ge(vec_ready, 1)
            with act.Fori(0, 6) as r:
                for c in range(4):
                    t = r * 4 + c
                    act.wait_ge(proj, r * 4 + (XBC + 6 + c + 1))
                    act.activation(um_a[:, ds(t, 1), :], ps[:, (XBC + 6 + c) % 4, 0:T], ACT.Copy,
                                   scale=mum[:, 0, ds(t, 1)]).then_inc(mix0, 1)
            for t in range(24, RT):
                act.wait_ge(proj, XBC + 6 + t + 1)
                act.activation(um_a[:, t, :], ps[:, (XBC + 6 + t) % 4, 0:T], ACT.Copy,
                               scale=mum[:, 0, t:t + 1]).then_inc(mix0, 1)

            act.wait_ge(dt_in, 1)
            act.activation(drow[:, 32:64], drow[:, 32:64], ACT.Exp)
            act.activation(dtmp[:, :, :], dtmp[:, :, :], ACT.Exp).then_inc(act_m, 1)
            act.wait_ge(act_m, 1)
            act.activation(dtl[:, :, :], dtmp[:, :, :], ACT.Ln, bias=1.0).then_inc(dt_ln, 1)

            for i in range(4, 8):
                act.wait_ge(ada_ps, i + 1)
                act.wait_ge(ada_cols, i - 1)
                act.activation(adas[:, i % 2, :], ps[:, 4 + i % 2, :], ACT.Copy).then_inc(ada_sb, 1)

            act.sem_inc(seg_exp, 2)
            act.wait_ge(cs_ps, 1)
            act.activation(ecs[:, :], ps[:, 7, 0:288], ACT.Exp).then_inc(cs_exp, 1)
            act.wait_ge(st_T, 1)
            for d in range(2):
                ins = act.activation(st0[:, d, :].rearrange("p (b c) -> p b c", b=2), ps[:, 2 * d:2 * d + 2, :], ACT.Copy)
            ins.then_inc(st0_ok, 1)
            for d in range(2):
                act.wait_ge(cst_ps, d + 1)
                act.activation(st_out[:, d, :, :].rearrange("p (b i) n -> p b (i n)", b=2), ps[:, 2 * d:2 * d + 2, :],
                               ACT.Copy).then_inc(cst_out, 1)
            act.wait_ge(xn_ready, 1)
            with act.Fori(0, NTILE) as j:
                for i in range(4):
                    act.wait_ge(seg_ps, j * 4 + (i + 3))
                    act.wait_ge(y_ps, j * 4 + (i + 1))
                    act.activation(seg[:, i % 2, :, :].rearrange("p (d h) q -> p d (h q)", d=2),
                                   ps[:, 2 * (i % 2):2 * (i % 2) + 2, :], ACT.Exp).then_inc(seg_exp, 1)
            for j in range(NTILE):
                act.wait_ge(gated, j + 1)
                for grp in range(2):
                    ins = act.activation(sq[:, :], xs[:, j, BLK * grp:BLK * grp + BLK], ACT.Square,
                                         accum_out=mstat[:, 2 * j + grp:2 * j + grp + 1])
                    ins.then_inc(ysq, 1)
                    act.wait_ge(ysq, 2 * j + grp + 1)
            act.wait_ge(meansq, 2)
            act.activation(mstat[:, 12:18], mstat[:, 6:12], ACT.Sqrt).then_inc(rstd, 1)

            act.activation(um_a[:, 24, :], um_a[:, 24, :], ACT.Tanh)
            act.activation(um_a[:, 26, :], um_a[:, 26, :], ACT.Sigmoid).then_inc(wd_ok, 1)
            act.wait_ge(wkv_T, 1)
            for d in range(2):
                ins = act.activation(r0all[:, :, d, :], ps[:, 6 + d, :].rearrange("p (i v) -> p i v", v=64), ACT.Copy)
            ins.then_inc(wkv_ok, 1)
            act.wait_ge(yT_sb, 8)
            act.sem_inc(aux_act, 1)
            with act.Fori(0, 8) as c:
                wkv_pair_act(act, c)
            for d in range(2):
                act.wait_ge(fin_T, d + 1)
                act.activation(wkv_in[:, d, :].rearrange("p (b c) -> p b c", b=2), ps[0:64, 2 * d:2 * d + 2, :],
                               ACT.Copy).then_inc(fin_sb, 1)
            for i in range(4):
                act.wait_ge(ada_ps, 8 + i + 1)
                if i >= 2:
                    act.wait_ge(gate_ps, 2 * i - 2)
                act.activation(adas[:, i % 2, :], ps[:, 4 + i % 2, :], ACT.Copy).then_inc(ada_sb, 1)
                for v in range(2):
                    act.wait_ge(gate_ps, 2 * i + v + 1)
                    dst = (g1, g2)[i // 2][:, v, BLK * (i % 2):BLK * (i % 2) + BLK]
                    act.activation(dst, ps[:, 6 + v, :], ACT.Copy).then_inc(gate_ok, 1)
            act.wait_ge(x1_ok, 3)
            for j in range(NTILE):
                act.activation(h2sq, x1[:, j, :], ACT.Square, accum_out=fst[:, j:j + 1]).then_inc(sq2_ok, 1)
                act.wait_ge(sq2_ok, j + 1)
            act.wait_ge(meansq, 3)
            act.activation(fst[:, 6:9], fst[:, 3:6], ACT.Sqrt).then_inc(rstd, 1)
            for j in range(NTILE):
                act.wait_ge(h2_ps, j + 1)
                act.activation(h2[:, j, :].rearrange("p (b c) -> p b c", b=2), ps[:, 2 * j:2 * j + 2, :],
                               ACT.Copy).then_inc(h2_ok, 1)
            act.wait_ge(rt_dve, 1)
            act.activation(grp2, grp2, ACT.Exp).then_inc(rt_act, 1)
            act.wait_ge(rt_dve, 2)
            act.activation(s3[:, 5, :], s3[:, 4, :], ACT.Exp).then_inc(rt_act, 1)
            for n in range(2):
                silu_gate(act, n, n)
                if n:
                    expert_out(act, n - 1, 1 - n)
            silu_gate(act, 2, 0)
            expert_out(act, 1, 1)
            with act.Fori(1, NE // 2 - 1) as i:
                silu_gate(act, i * 2 + 1, 1)
                expert_out(act, i * 2, 0)
                silu_gate(act, i * 2 + 2, 0)
                expert_out(act, i * 2 + 1, 1)
            silu_gate(act, NE - 1, 1)
            expert_out(act, NE - 2, 0)
            expert_out(act, NE - 1, 1)
            act.sem_inc(y_ov, 16)
            n_over = act.value_load(meta_i[0:1, N_OVER:N_OVER + 1], min_val=1, max_val=N_OVER)
            with act.Fori(0, n_over) as q:
                silu_gate(act, q + NE, 0)
                expert_out(act, q + NE, 0, ov=q)
            for j in range(NTILE):
                act.wait_ge(x1_ok, j + 4)
                act.activation(h2[:, j, :], x1[:, j, :], ACT.Square, accum_out=fst[:, j:j + 1]).then_inc(sq2_ok, 1)
            act.wait_ge(meansq, 4)
            act.activation(fst[:, 6:9], fst[:, 3:6], ACT.Sqrt).then_inc(rstd, 1)

        @block.vector
        def _(dve):
            g = Chain(dve, dve_c)
            dve.memset(eps_gn[:, :], 64e-5)
            g.do(dve.memset(bones[:, :], 0.0))
            dve.memset(bones[0:64, 0:64], 1.0)
            dve.memset(bones[64:P, 64:P], 1.0)
            dve.wait_ge(const_ready, 1)
            dve.tensor_reduce(sel32[:, :], ident[:, :].rearrange("p (q v) -> p v q", v=32), AX.X, ALU.add)
            g.do(dve.tensor_reduce(par[:, 0:4], ident[:, :].rearrange("p (q v) -> p v q", v=4), AX.X, ALU.add))
            dve.tensor_copy(selb[:, :, :], sel32[:, 0:2].unsqueeze(2).to_broadcast([P, 2, P]))
            dve.tensor_tensor(par[:, 4:6], par[:, 0:2], par[:, 2:4], ALU.add)
            dve.wait_ge(vec_t, 1)
            dve.tensor_copy(pv0[:, :], ps[:, 1, 0:P])
            g.do(dve.tensor_copy(pv1[:, 0:V1N], ps[:, 2, 0:V1N]))
            mu = pv1[:, 0:RT]
            dve.tensor_scalar(mum[:, 0, :], mu, -1.0, 1.0, ALU.mult, ALU.add)
            for i in range(6):
                dve.tensor_scalar(mum[:, 1 + i, :], mu, par[:, i:i + 1], None, ALU.mult)
            dve.tensor_scalar(kam[:, :], pv1[:, V1["k_a"]:V1["k_a"] + 8], -1.0, 1.0, ALU.mult,
                              ALU.add).then_inc(vec_ready, 1)
            dve.wait_ge(act_c, 3)
            dve.tensor_scalar(stat[:, 4:7], stat[:, 0:3], 1.0 / D, 1e-6, ALU.mult, ALU.add).then_inc(meansq, 1)
            dve.wait_ge(rstd, 1)
            g.do(dve.reciprocal(stat[:, 8:11], stat[:, 12:15]))
            for j in range(NTILE):
                ins = dve.tensor_scalar(xt[:, j, :], xt[:, j, :], stat[:, 8 + j:9 + j], None, ALU.mult)
            ins.then_inc(xn_ready, 1)
            dve.wait_ge(ada_cols, 4)
            g.do(dve.tensor_tensor(mod[:, 0:16, :], ps[:, 6, 0:32].rearrange("p (t v) -> p t v", v=2),
                                   pv0[:, 0:16].unsqueeze(2).to_broadcast([P, 16, 2]), ALU.add))
            g.do(dve.tensor_scalar(aff1[:, :, :], mod[:, 8:16, :], 1.0, None, ALU.add))
            g.do(dve.tensor_tensor(aff1[:, :, :], aff1[:, :, :],
                                   pv0[:, V0["norm1"]:V0["norm1"] + 8].unsqueeze(2).to_broadcast([P, 8, 2]), ALU.mult))
            for k in range(KT):
                dve.wait_ge(xT_ps, k + 1)
                for v, (lo, hi) in enumerate(((0, P), (P, T))):
                    ins = dve.tensor_scalar(hT[:, k, lo:hi], ps[:, k % 4, lo:hi], aff1[:, k, v:v + 1],
                                            mod[:, k, v:v + 1], ALU.mult, ALU.add)
                ins.then_inc(hT_ready, 1)
            W = T + 2

            def taps(t):
                dve.wait_ge(proj_read, t + 1)
                if t >= 2 and t < 10:
                    dve.wait_ge(conv_T, t - 1)
                elif t >= 10:
                    dve.wait_ge(conv_out, t - 1)
                for j in range(5):
                    w = pv0[:, V0["conv_w"] + 12 * j + t:V0["conv_w"] + 12 * j + t + 1]
                    src = raw[:, t % 2, j:j + W]
                    if j == 0:
                        ins = dve.tensor_scalar(acc[:, t % 2, 0:W], src, w, None, ALU.mult)
                    else:
                        ins = dve.scalar_tensor_tensor(acc[:, t % 2, 0:W], src, w, acc[:, t % 2, 0:W],
                                                       ALU.mult, ALU.add)
                    if j < 4:
                        g.do(ins)
                ins.then_inc(conv_acc, 1)

            def token_major(t):
                if t >= 10:
                    return
                dve.wait_ge(conv_T, t + 1)
                dst = xs[:, :, P * t:P * t + P] if t < 8 else btm[:, :, P * (t - 8):P * (t - 8) + P]
                dve.tensor_copy(dst, ps[:, 4 + t % 2, 0:T].rearrange("p (j c) -> p j c", j=NTILE)).then_inc(conv_tm, 1)

            for t in range(XBC):
                taps(t)
                if t >= 3:
                    token_major(t - 3)
            token_major(9)

            def mix(c, t, mus, step):
                u = ps[:, c, 0:T]
                o = um_a[:, t, :] if isinstance(t, int) else um_a[:, ds(t, 1), :].rearrange("p a t -> p (a t)")
                ug = u[:, P:T].rearrange("p (r w) -> p r w", w=GRID)
                og = o[:, P:T].rearrange("p (r w) -> p r w", w=GRID)
                parts = [(o[:, 1:P], u[:, 0:P - 1], 5), (o[:, 0:P - 1], u[:, 1:P], 6),
                         (og[:, :, 1:], ug[:, :, :-1], 1), (og[:, :, :-1], ug[:, :, 1:], 2),
                         (o[:, P + GRID:T], u[:, P:T - GRID], 3), (o[:, P:T - GRID], u[:, P + GRID:T], 4)]
                for i, (dst, src, m) in enumerate(parts):
                    step(dve.scalar_tensor_tensor(dst, src, mus(m), dst, ALU.mult, ALU.add), i)

            with dve.Fori(0, 6) as r:
                lc = LoopChain(dve, dve_r, r, 20)
                for c in range(4):
                    t = r * 4 + c
                    dve.wait_ge(mix0, r * 4 + (c + 1))

                    def step(ins, i):
                        if i < 5:
                            lc.do(ins)
                        else:
                            ins.then_inc(proj_read, 1)
                    mix((XBC + 6 + c) % 4, t, lambda m: mum[:, m, ds(t, 1)], step)
                lc.end()
            for t in range(24, RT):
                dve.wait_ge(mix0, t + 1)

                def step(ins, i):
                    if i < 5:
                        g.do(ins)
                    else:
                        ins.then_inc(proj_read, 1)
                mix((XBC + 6 + t) % 4, t, lambda m: mum[:, m, t:t + 1], step)

            m = g
            dve.wait_ge(dt_ps, 1)
            m.do(dve.tensor_tensor(dt[:, :, :], ps[:, 7, 0:96].rearrange("p (j h) -> p j h", j=NTILE),
                                   drow[:, 0:32].unsqueeze(1).to_broadcast([P, NTILE, 32]), ALU.add))
            dve.scalar_tensor_tensor(dtmp[:, :, :], dt[:, :, :], -1.0, dt[:, :, :], ALU.mult,
                                     ALU.min).then_inc(dt_in, 1)
            dve.wait_ge(dt_ln, 1)
            m.do(dve.tensor_scalar(la[:, :, :], dtmp[:, :, :], 1.0, None, ALU.add))
            m.do(dve.reciprocal(dtr[:, :, :], la[:, :, :]))
            m.do(dve.tensor_scalar(la[:, :, :], la[:, :, :], 1.0, None, ALU.subtract))
            m.do(dve.tensor_tensor(dtmp[:, :, :], dtmp[:, :, :], la[:, :, :], ALU.subtract))
            m.do(dve.tensor_tensor(dtmp[:, :, :], dtmp[:, :, :], dtr[:, :, :], ALU.mult))
            m.do(dve.tensor_tensor(dtl[:, :, :], dtl[:, :, :], dtmp[:, :, :], ALU.add))
            m.do(dve.scalar_tensor_tensor(dt[:, :, :], dt[:, :, :], 0.0, dtl[:, :, :], ALU.max, ALU.add))
            dve.scalar_tensor_tensor(la[:, :, :], dt[:, :, :], -1.0,
                                     drow[:, 32:64].unsqueeze(1).to_broadcast([P, NTILE, 32]),
                                     ALU.mult, ALU.mult).then_inc(la_ready, 1)
            dve.wait_ge(ada_cols, 8)
            m.do(dve.tensor_tensor(mod[:, 16:32, :], ps[:, 6, 32:64].rearrange("p (t v) -> p t v", v=2),
                                   pv0[:, 24:40].unsqueeze(2).to_broadcast([P, 16, 2]), ALU.add))
            m.do(dve.tensor_scalar(aff2[:, :, :], mod[:, 24:32, :], 1.0, None, ALU.add))
            m.do(dve.tensor_tensor(aff2[:, :, :], aff2[:, :, :],
                                   pv1[:, V1["norm2"]:V1["norm2"] + 8].unsqueeze(2).to_broadcast([P, 8, 2]), ALU.mult))

            dve.sem_inc(y_sb, 2)
            dve.wait_ge(cs_exp, 1)
            for d in range(2):
                w = ecs[:, 96 + 48 * d:144 + 48 * d].rearrange("p (j h) -> p j h", j=NTILE)
                ins = dve.tensor_tensor(w, w, dt[:, :, 16 * d:16 * d + 16], ALU.mult)
            m.do(ins)
            dve.wait_ge(ada_ps, 8)
            dve.wait_ge(score_ps, 1)
            for d in range(2):
                for b, n in ((0, 4), (1, 2)):
                    ins = dve.tensor_tensor(msc[:, d, 4 * b:4 * b + n, :],
                                            ps[:, 4 + b, 0:P * n].rearrange("p (i q) -> p i q", i=n),
                                            tri[:, 1 + 2 * d, :].unsqueeze(1).to_broadcast([P, n, P]), ALU.mult)
            ins.then_inc(score_ok, 1)

            def heads(ap):
                return ap.rearrange("p (h c) -> p h c", c=PM)

            for job in range(4):
                d, j = job % 2, (0, 0, 1, 2)[job]
                if job >= 2:
                    dve.wait_ge(cst_ps, job - 1)
                w = ecs[:, 96 + 48 * d + 16 * j:96 + 48 * d + 16 * j + 16]
                dve.tensor_tensor(heads(xdw[:, job % 2, :]), heads(xs[:, j, :]),
                                  w.unsqueeze(2).to_broadcast([P, HM, PM]), ALU.mult).then_inc(xdw_ok, 1)
            dve.wait_ge(st0_ok, 1)
            for d in range(2):
                j = 1 + d
                dec = ecs[:, 192 + 32 * j + 16 * d:192 + 32 * j + 16 * d + 16]
                m.do(dve.tensor_tensor(heads(st1[:, d, :]), heads(st0[:, d, :]),
                                       dec.unsqueeze(2).to_broadcast([P, HM, PM]), ALU.mult))
                dve.wait_ge(cst_ps, 3 + d)
                st1v = st1[:, d, :].rearrange("p (b c) -> p b c", b=2)
                ins = dve.tensor_tensor(st1v, st1v, ps[:, 2 * d:2 * d + 2, :], ALU.add)
            ins.then_inc(st1_ok, 1)

            with dve.Fori(0, NTILE) as j:
                lc = LoopChain(dve, dve_l, j, 2)
                for i in range(4):
                    grp = i // 2
                    dve.wait_ge(seg_exp, j * 4 + (i + 3))
                    for d in range(2):
                        for h in range(4):
                            gb = seg[:, i % 2, 4 * d + h, :]
                            hh = 16 * d + 4 * i + h
                            ins = dve.scalar_tensor_tensor(
                                gb, gb, dt[:, ds(j, 1), hh:hh + 1].rearrange("p a b -> p (a b)"),
                                msc[:, d, ds(j * 2 + grp, 1), :].rearrange("p a q -> p (a q)"), ALU.mult, ALU.mult)
                    ins.then_inc(g_ok, 1)
                    if i % 2:
                        dve.wait_ge(y_ps, j * 4 + (i + 3))
                        xv = xs[:, ds(j, 1), BLK * grp:BLK * grp + BLK].rearrange("p a c -> p (a c)")
                        lc.do(dve.tensor_tensor(heads(xv), heads(xv),
                                                drow[:, 64 + 8 * grp:72 + 8 * grp].unsqueeze(2).to_broadcast([P, 8, PM]),
                                                ALU.mult))
                        ins = dve.tensor_tensor(xv, xv, ps[:, 4 + grp, :], ALU.add)
                        ins.then_inc(y_sb, 1)
                        dve.wait_ge(y_sb, j * 2 + (grp + 3))
                lc.end()

            for o, (j, d, _) in enumerate(OFF):
                for grp in range(2):
                    i = 2 * o + grp
                    dve.wait_ge(off_ps, i + 1)
                    f = ecs[:, 48 * d + 16 * j + 8 * grp:48 * d + 16 * j + 8 * grp + 8]
                    dve.tensor_tensor(heads(yoff[:, :]), heads(ps[:, i % 4, :]),
                                      f.unsqueeze(2).to_broadcast([P, 8, PM]), ALU.mult).then_inc(off_rd, 1)
                    dve.wait_ge(off_rd, i + 1)
                    xv = xs[:, j, BLK * grp:BLK * grp + BLK]
                    m.do(dve.tensor_tensor(xv, xv, yoff[:, :], ALU.add))
            for j in range(NTILE):
                dve.tensor_tensor(xs[:, j, :], xs[:, j, :], zs[:, j, :], ALU.mult).then_inc(gated, 1)
            dve.wait_ge(ysq, 6)
            dve.tensor_scalar(mstat[:, 6:12], mstat[:, 0:6], 1.0 / BLK, 1e-6, ALU.mult, ALU.add).then_inc(meansq, 1)
            dve.wait_ge(rstd, 2)
            m.do(dve.reciprocal(mstat[:, 18:24], mstat[:, 12:18]))
            for i in range(6):
                xv = xs[:, i // 2, BLK * (i % 2):BLK * (i % 2) + BLK]
                ins = dve.tensor_scalar(xv, xv, mstat[:, 18 + i:19 + i], None, ALU.mult)
            ins.then_inc(ynorm, 1)
            for t in range(8):
                dve.wait_ge(yT_ps, t + 1)
                c = V1["m_norm"] + t
                dve.tensor_scalar(mixm[:, t, :], ps[:, 6 + t % 2, 0:T], pv1[:, c:c + 1], None, ALU.mult).then_inc(yT_sb, 1)

            dve.sem_inc(aux_dve, 2)
            dve.sem_inc(yo_rd, 3)
            dve.sem_inc(pair_ok, 1)
            dve.wait_ge(wkv_ok, 1)
            with dve.Fori(0, 8) as c:
                lc = LoopChain(dve, dve_w, c, 34)
                wkv_pair_dve(dve, c, lc)
                lc.end()

            t = g
            dve.wait_ge(brow_in, 64)
            for i in range(4):
                dve.wait_ge(ada_sb, 9 + i)
                ab = adas[0:2, i % 2, :]
                dve.tensor_tensor(ab, ab, brow[:, BLK * i:BLK * i + BLK], ALU.add).then_inc(bias_ok, 1)
            dve.wait_ge(out_ps, 4)
            dve.wait_ge(x_again, 32)
            dve.wait_ge(gate_ok, 8)
            for j in range(NTILE):
                v = min(j, 1)
                t.do(dve.tensor_tensor(h2[:, j, :].rearrange("p (b c) -> p b c", b=2), ps[:, 2 * j:2 * j + 2, :],
                                       g1[:, v, :].rearrange("p (b c) -> p b c", b=2), ALU.mult))
                dve.tensor_tensor(x1[:, j, :], x1[:, j, :], h2[:, j, :], ALU.add).then_inc(x1_ok, 1)
            dve.wait_ge(sq2_ok, 3)
            dve.tensor_scalar(fst[:, 3:6], fst[:, 0:3], 1.0 / D, 1e-6, ALU.mult, ALU.add).then_inc(meansq, 1)
            dve.wait_ge(rstd, 3)
            t.do(dve.reciprocal(fst[:, 9:12], fst[:, 6:9]))
            for j in range(NTILE):
                ins = dve.tensor_scalar(h2[:, j, :], x1[:, j, :], fst[:, 9 + j:10 + j], None, ALU.mult)
            ins.then_inc(xn2_ok, 1)
            for k in range(KT):
                dve.wait_ge(h2T_ps, k + 1)
                for v, (lo, hi) in enumerate(((0, P), (P, T))):
                    ins = dve.tensor_scalar(hT[:, k, lo:hi], ps[:, 6 + k % 2, lo:hi], aff2[:, k, v:v + 1],
                                            mod[:, 16 + k, v:v + 1], ALU.mult, ALU.add)
                ins.then_inc(h2T_ok, 1)
            def cols(ap, n):
                return ap.unsqueeze(2).to_broadcast([P, NTILE, n])

            def row(ap, n):
                return ap.unsqueeze(1).to_broadcast([P, NTILE, n])

            def one_hot(dst, vals, top, places, n, scr):
                t.do(dve.tensor_tensor(scr, vals, cols(top, n), ALU.is_equal))
                t.do(dve.tensor_tensor(scr, scr, row(places, n), ALU.mult))
                t.do(dve.tensor_reduce(s3[:, 9, :], scr, AX.X, ALU.max))
                t.do(dve.tensor_tensor(dst, scr, cols(s3[:, 9, :], n), ALU.is_equal))

            dve.wait_ge(lg_ps, 1)
            dve.wait_ge(rconst, 1)
            t.do(dve.tensor_tensor(lg, ps[:, 6, 0:108].rearrange("p (j c) -> p j c", j=NTILE), row(brt, 36), ALU.add))
            gl, el = lg[:, :, 0:4], lg[:, :, 4:36]
            t.do(dve.tensor_reduce(s3[:, 0, :], gl, AX.X, ALU.max))
            dve.tensor_tensor(grp2, gl, cols(s3[:, 0, :], 4), ALU.subtract).then_inc(rt_dve, 1)
            one_hot(ghot, gl, s3[:, 0, :], down[:, 0:4], 4, ghot)
            g4 = [x.rearrange("p j (g e) -> p j g e", g=EG) for x in (msk, el, tmp)]
            gb8 = ghot.unsqueeze(3).to_broadcast([P, NTILE, EG, EPG])
            t.do(dve.tensor_tensor(g4[0], g4[1], gb8, ALU.mult))
            t.do(dve.tensor_scalar(ghot, ghot, 1e30, -1e30, ALU.mult, ALU.add))
            t.do(dve.tensor_tensor(g4[0], g4[0], gb8, ALU.add))
            t.do(dve.tensor_reduce(s3[:, 2, :], msk, AX.X, ALU.max))
            one_hot(oh[:, 0], msk, s3[:, 2, :], down[:, 4:36], 32, tmp)
            t.do(dve.scalar_tensor_tensor(msk, oh[:, 0], -3e30, msk, ALU.mult, ALU.add))
            t.do(dve.tensor_reduce(s3[:, 3, :], msk, AX.X, ALU.max))
            one_hot(oh[:, 1], msk, s3[:, 3, :], down[:, 4:36], 32, tmp)
            dve.tensor_tensor(both_oh, oh[:, 0], oh[:, 1], ALU.add).then_inc(a_ok, 1)
            dve.tensor_tensor(s3[:, 4, :], s3[:, 3, :], s3[:, 2, :], ALU.subtract).then_inc(rt_dve, 1)
            dve.wait_ge(rt_act, 1)
            t.do(dve.tensor_reduce(s3[:, 1, :], grp2, AX.X, ALU.add))
            dve.wait_ge(rt_act, 2)
            t.do(dve.tensor_scalar(s3[:, 6, :], s3[:, 5, :], 1.0, None, ALU.add))
            t.do(dve.tensor_tensor(s3[:, 6, :], s3[:, 6, :], s3[:, 1, :], ALU.mult))
            t.do(dve.reciprocal(wcol[:, 0, :], s3[:, 6, :]))
            t.do(dve.tensor_tensor(wcol[:, 1, :], wcol[:, 0, :], s3[:, 5, :], ALU.mult))
            dve.wait_ge(rank_ps, 1)
            n_e = ps[:, 7, 96:128]
            dve.tensor_scalar(cnt[:, 1, :], n_e, P + 0.5, None, ALU.is_gt)
            t.do(dve.tensor_scalar(cnt[:, 0, :], n_e, 2 * P + 0.5, None, ALU.is_gt))
            t.do(dve.tensor_tensor(cnt[:, 0, :], cnt[:, 0, :], cnt[:, 1, :], ALU.add))
            t.do(dve.tensor_tensor_scan(cnt[:, 1, :], ones[:, 0:32], cnt[:, 0, :], 0.0, ALU.mult, ALU.add))
            t.do(dve.tensor_tensor(cnt[:, 2, :], cnt[:, 1, :], cnt[:, 0, :], ALU.subtract))
            t.do(dve.tensor_tensor(cnt[:, 3, :], cnt[:, 2, :], erow, ALU.subtract))
            t.do(dve.tensor_scalar(cnt[:, 3, :], cnt[:, 3, :], float(P), float(P * (NE - 1)), ALU.mult, ALU.add))
            rank = ps[:, 7, 0:96].rearrange("p (j e) -> p j e", j=NTILE)
            t.do(dve.tensor_scalar(tmp, rank, P - 0.5, None, ALU.is_gt))
            t.do(dve.tensor_tensor(tmp, tmp, row(cnt[:, 3, :], 32), ALU.mult))
            t.do(dve.tensor_tensor(slot_v, rank, tmp, ALU.add))
            t.do(dve.scalar_tensor_tensor(slot_v, row(erow, 32), float(P), slot_v, ALU.mult, ALU.add))
            for k in range(2):
                t.do(dve.tensor_tensor(tmp, slot_v, oh[:, k], ALU.mult))
                t.do(dve.tensor_reduce(slots[:, k, :], tmp, AX.X, ALU.add))
            for q in range(N_OVER):
                t.do(dve.tensor_scalar(tmp[:, 0, :], cnt[:, 2, :], q + 0.5, None, ALU.is_lt))
                t.do(dve.tensor_scalar(tmp[:, 1, :], cnt[:, 1, :], q + 0.5, None, ALU.is_gt))
                t.do(dve.tensor_tensor(tmp[:, 0, :], tmp[:, 0, :], tmp[:, 1, :], ALU.mult))
                t.do(dve.tensor_tensor(tmp[:, 0, :], tmp[:, 0, :], erow, ALU.mult))
                t.do(dve.tensor_reduce(meta[:, q:q + 1], tmp[:, 0, :], AX.X, ALU.add))
            t.do(dve.tensor_scalar(meta[:, N_OVER:N_OVER + 1], cnt[:, 1, 31:32], 1.0, None, ALU.max))
            t.do(dve.tensor_copy(meta_i[:, 0:N_OVER + 1], meta[:, 0:N_OVER + 1]))
            dve.tensor_copy(slots_i[:, :], slots.rearrange("p k j -> p (k j)")).then_inc(slots_ok, 1)
            dve.wait_ge(rows_ps, 1)
            dve.tensor_copy(idx[:, :], ps[:, 6, 0:N_TILES]).then_inc(idx_ok, 1)
            rows_copy(dve, 0, 0)
            rows_copy(dve, 1, 1)
            for n in (1, 2):
                hidden(dve, n - 1, 1 - n % 2)
                rows_copy(dve, n + 1, 1 - n % 2)
            with dve.Fori(1, NE // 2 - 1) as i:
                hidden(dve, i * 2, 0)
                rows_copy(dve, i * 2 + 2, 0)
                hidden(dve, i * 2 + 1, 1)
                rows_copy(dve, i * 2 + 3, 1)
            hidden(dve, NE - 2, 0)
            hidden(dve, NE - 1, 1)
            n_over = dve.value_load(meta_i[0:1, N_OVER:N_OVER + 1], min_val=1, max_val=N_OVER)
            with dve.Fori(0, n_over) as q:
                rows_copy(dve, q + NE, 0)
                hidden(dve, q + NE, 0)
            for j in range(NTILE):
                b, v = j % 2, min(j, 1)
                dve.wait_ge(comb[b], 32 * (j // 2 + 1))
                if j:
                    dve.wait_ge(x1_ok, j + 3)
                t.do(dve.tensor_scalar(ymoe, cmb[:, b, 0, :], wcol[:, 0, j:j + 1], None, ALU.mult))
                dve.scalar_tensor_tensor(ymoe, cmb[:, b, 1, :], wcol[:, 1, j:j + 1], ymoe, ALU.mult,
                                         ALU.add).then_inc(moe_ok, 1)
                dve.wait_ge(moe_ok, j + 1)
                t.do(dve.tensor_tensor(ymoe, ymoe, g2[:, v, :], ALU.mult))
                dve.tensor_tensor(x1[:, j, :], x1[:, j, :], ymoe, ALU.add).then_inc(x1_ok, 1)
            dve.wait_ge(sq2_ok, 6)
            dve.tensor_scalar(fst[:, 3:6], fst[:, 0:3], 1.0 / D, 1e-6, ALU.mult, ALU.add).then_inc(meansq, 1)
            dve.wait_ge(rstd, 4)
            t.do(dve.reciprocal(fst[:, 9:12], fst[:, 6:9]))
            for j in range(NTILE):
                dve.scalar_tensor_tensor(x1[:, j, :], x1[:, j, :], fst[:, 9 + j:10 + j], fnw, ALU.mult,
                                         ALU.mult).then_inc(y_ok, 1)


N_SMALL = 19
N_OUT = 7


_OUTS = [(1, P, D), (1, 2 * P, D), (1, 1, HM, PM, NS), (1, 1, HM, PM, NS), (1, 1, 16, 64, 64), (1, 1, 16, 64, 64)]


def kernel(**inputs):
    import numpy as np
    import concourse.bacc as bacc
    from concourse.bass_utils import run_bass_kernel_spmd

    nc = bacc.Bacc("TRN2", target_bir_lowering=False, num_devices=1)
    arrays, aps = {}, {}
    for name, value in inputs.items():
        arr = np.ascontiguousarray(value)
        arrays["in_" + name] = arr
        aps[name] = nc.dram_tensor("in_" + name, arr.shape, mybir.dt.from_np(arr.dtype), kind="ExternalInput").ap()
    outs = [nc.dram_tensor(f"out_{i}", shape, F32, kind="ExternalOutput").ap() for i, shape in enumerate(_OUTS)]
    program(nc, aps, outs)
    got = run_bass_kernel_spmd(nc, [arrays], core_ids=[0]).results[0]
    return tuple(got[f"out_{i}"] for i in range(len(_OUTS)))
```

```python
from contextlib import ExitStack

import concourse.bass as bass
from concourse import mybir

ALU = mybir.AluOpType
ACT = mybir.ActivationFunctionType
AX = mybir.AxisListType
F32 = mybir.dt.float32
I32 = mybir.dt.int32
U32 = mybir.dt.uint32
ds = bass.ds

P = 128
D = 1024
KT = D // P
NTILE = 3
T = NTILE * P
GRID = 64
BLK = 512
HM, PM, NS = 16, 64, 128
XBC = 12
DTC = 2560
RC = 2592
RT = 27
RING = 3
NEG_C = -0.6065306597126334
NE, EG, EPG, DE = 32, 4, 8, 256
CH = 64
NG = NE * CH // P
N_OVER = (2 * T - 1) // CH
OV_TURNS = -(-N_OVER * CH // (2 * P))
N_GROUPS = NG + 2 * OV_TURNS
N_CHUNKS = N_GROUPS * P // CH

V0 = dict(b_ada=0, norm1=48, conv_w=56, conv_b=116)
V1 = dict(mu=0, w0=27, a0=43, k_k=59, k_a=67, r_k=75, ln_w=83, ln_b=91, norm2=99, m_norm=107)
V1N = 115

ADA_A, XB, Z, R, ADA_B, GATES, WOUT = 0, 4, 7, 9, 16, 20, 24
ADA_COLS = [0, 1, 2, 3, 6, 7, 8, 9]


OFF = ((1, 0, 0), (2, 1, 0), (2, 0, 1), (1, 1, 1))


class Chain:

    def __init__(self, eng, sem):
        self.eng, self.sem, self.n = eng, sem, 0

    def did(self, ins):
        ins.then_inc(self.sem, 1)
        self.n += 1
        return self.n

    def wait(self, n=None):
        self.eng.wait_ge(self.sem, self.n if n is None else n)

    def do(self, ins):
        self.did(ins)
        self.wait()


class LoopChain:

    def __init__(self, eng, sem, i, per):
        self.eng, self.sem, self.i, self.per, self.n = eng, sem, i, per, 0

    def did(self, ins):
        ins.then_inc(self.sem, 1)
        self.n += 1
        return self.n

    def wait(self, n=None):
        self.eng.wait_ge(self.sem, self.i * self.per + (self.n if n is None else n))

    def do(self, ins):
        self.did(ins)
        self.wait()

    def end(self):
        assert self.n == self.per, (self.n, self.per)


def program(nc, a, out, dump=None):
    ctx = ExitStack()
    with ctx:
        def sb(name, shape, dt=F32):
            return ctx.enter_context(nc.sbuf_tensor(name, shape, dt))

        def sem(name):
            return ctx.enter_context(nc.semaphore(name))

        ps = ctx.enter_context(nc.psum_tensor("ps", [P, 8, 512], F32))

        ident = sb("ident", [P, P])
        ones = sb("ones", [P, P])
        bones = sb("bones", [P, P])
        tri = sb("tri", [P, 4, P])
        trin = sb("trin", [P, 4, P])
        lvl = sb("lvl", [P, 7, 2, P])
        sel32 = sb("sel32", [P, 32])
        par = sb("par", [P, 6])
        rst = sb("rst", [P, 2, T])
        vrows = sb("vrows", [P, 2, P])
        crows = sb("crows", [16, P])
        pv0 = sb("pv0", [P, P])
        pv1 = sb("pv1", [P, P])
        cond = sb("cond", [P, KT, 32])
        mod = sb("mod", [P, 32, 2])
        aff1 = sb("aff1", [P, KT, 2])
        aff2 = sb("aff2", [P, KT, 2])
        mum = sb("mum", [P, 7, RT])
        kam = sb("kam", [P, KT])
        drow = sb("drow", [P, 32 + 32 + 16])
        stat = sb("stat", [P, 16])
        dt = sb("dt", [P, NTILE, 32])
        dtmp = sb("dtmp", [P, NTILE, 32])
        dtl = sb("dtl", [P, NTILE, 32])
        dtr = sb("dtr", [P, NTILE, 32])
        la = sb("la", [P, NTILE, 32])
        ecs = sb("ecs", [P, 288])
        wdt = sb("wdt", [P, KT, 32])

        ring_a = sb("ring_a", [P, RING * KT * BLK])
        um_a = sb("um_a", [P, RT, T])
        mixm = sb("mixm", [P, KT, T])
        hT = sb("hT", [P, KT, T])
        misc = sb("misc", [P, 12288])

        ring = ring_a[:, :].rearrange("p (s k c) -> p s k c", s=RING, k=KT)
        xt = misc[:, 0:3072].rearrange("p (j c) -> p j c", j=NTILE)
        zs = misc[:, 3072:6144].rearrange("p (j c) -> p j c", j=NTILE)
        xs = misc[:, 6144:9216].rearrange("p (j c) -> p j c", j=NTILE)
        btm = misc[:, 9216:9984].rearrange("p (j c) -> p j c", j=NTILE)
        bct = misc[:, 9984:11520].rearrange("p (i t) -> p i t", i=4)
        scratch = sb("scratch", [P, 2048 + 2 * BLK])
        raw = scratch[:, 0:784].rearrange("p (b t) -> p b t", b=2)
        acc = scratch[:, 784:1568].rearrange("p (b t) -> p b t", b=2)
        adas = scratch[:, 2048:3072].rearrange("p (b c) -> p b c", b=2)

        ring_s = [ring_a[:, 4096 * i:4096 * (i + 1)] for i in range(RING)]
        st_in = ring_s[2][:, 0:2048].rearrange("p (d i n) -> p d i n", d=2, i=8)
        st0 = ring_s[2][:, 2048:4096].rearrange("p (d c) -> p d c", d=2)
        st1 = ring_s[0][:, 0:2048].rearrange("p (d c) -> p d c", d=2)
        xdw = ring_s[0][:, 2048:4096].rearrange("p (b c) -> p b c", b=2)
        msc = ring_s[1][:, 0:1536].rearrange("p (d i q) -> p d i q", d=2, i=6)
        yoff = ring_s[1][:, 1536:2048]
        st_out = ring_s[1][:, 2048:4096].rearrange("p (d i n) -> p d i n", d=2, i=8)
        hT_flat = hT[:, :, :].rearrange("p k t -> p (k t)")
        lam = hT_flat[:, 0:2048].rearrange("p (b i s) -> p b i s", b=2, i=8)
        seg = misc[:, 0:2048].rearrange("p (b i s) -> p b i s", b=2, i=8)
        sq = misc[:, 2048:2560]
        mstat = sb("mstat", [P, 24])
        selb = sb("selb", [P, 2, P])

        def at(flat, o, *shape):
            names = "abcd"[:len(shape)]
            n = 1
            for x in shape:
                n *= x
            v = flat[:, o:o + n]
            return v if len(shape) == 1 else v.rearrange(
                f"p ({' '.join(names)}) -> p {' '.join(names)}", **dict(zip(names, shape)))

        gb = [at(r, 0, 2, 2, 2, P) for r in ring_s]
        gk = [at(r, 1024, 2, 2, 2, P) for r in ring_s]
        xinvT = [at(r, 2048, 2, 2, P) for r in ring_s]
        xinv = [at(r, 2560, 2, 2, P) for r in ring_s]
        ys = [at(r, 3072, 2, 2, P) for r in ring_s]
        rhs_s = [at(r, 3584, 4, 64) for r in ring_s]
        us = [at(r, 3840, 4, 64) for r in ring_s]
        sg = at(misc, 0, 2, T)
        am = at(misc, 768, 2, T)
        cs = at(misc, 1536, 2, T)
        csm = at(misc, 2304, 2, T)
        e_m = csm
        e_p = at(misc, 3072, 2, T)
        e_i = at(misc, 4608, 2, T)
        kd = at(misc, 5376, 2, T)
        be = at(misc, 6144, 2, NTILE, P)
        kap = at(misc, 6912, 2, NTILE, P)
        arrs = [at(misc, 7680, 2, NTILE, 2, P), at(scratch, 0, 2, NTILE, 2, P)]
        kk0 = at(misc, 9216, T)
        kk = at(misc, 9600, T)
        kroot = at(misc, 9984, T)
        rb = at(misc, 10368, T)
        eps_gn = sb("eps_gn", [P, 1])
        btks = [at(misc, 10752, 4, P), at(scratch, 1536, 4, P)]
        ktks = [at(misc, 11264, 4, P), at(scratch, 2048, 4, P)]
        vtks = [at(misc, 11776, NTILE, P), at(scratch, 2560, NTILE, P)]
        y_c = at(hT_flat, 0, T)
        yc0 = at(hT_flat, 384, T)
        ysq_c = at(hT_flat, 768, T)
        v_c = at(hT_flat, 1152, T)
        g_cs = [at(hT_flat, 1536, T), at(misc, 3840, T)]
        vbs = [at(hT_flat, 1920, T), at(misc, 4224, T)]
        tot = at(hT_flat, 2304, 2, NTILE)
        e_halfs = [at(hT_flat, 2310 + 6 * i, 2, NTILE) for i in range(2)]
        r0ps = [at(hT_flat, 2322 + 256 * i, 2, 2, 64) for i in range(2)]
        stw = sb("stw", [P, 3, P])
        r0all = sb("r0all", [P, 8, 2, 64])
        sall = sb("sall", [P, 8, 2, 64])
        wkv_in = scratch[0:64, 0:2048].rearrange("p (d c) -> p d c", d=2)

        s_small = sem("small_loads")
        s_x = sem("x_loaded")
        w_in_slot = [sem(f"block_in_slot_{i}") for i in range(RING)]
        s_wdt = sem("wdt_loaded")
        pool_c = sem("pool_steps")
        const_ready = sem("constants_ready")
        vec_t = sem("vectors_transposed")
        vec_ready = sem("vectors_ready")
        cond_ready = sem("cond_ready")
        ada_ps = sem("ada_in_psum")
        ada_sb = sem("ada_copied")
        ada_cols = sem("ada_columns_in_psum")
        meansq = sem("mean_squares")
        rstd = sem("roots_ready")
        xn_ready = sem("x_normalised")
        xT_ps = sem("x_transposed")
        hT_ready = sem("h_ready")
        proj = sem("projection_in_psum")
        proj_read = sem("projection_read")
        conv_acc = sem("conv_summed")
        conv_out = sem("conv_silu_done")
        conv_T = sem("conv_transposed")
        conv_tm = sem("conv_token_major")
        mix0 = sem("mix_started")
        dve_c = sem("dve_steps")
        dve_r = sem("dve_mix_steps")
        act_c = sem("act_steps")
        dt_ps = sem("dt_in_psum")
        out_done = sem("outputs_written")
        masks_ready = sem("level_masks_ready")
        dt_in = sem("softplus_input_ready")
        dt_ln = sem("softplus_log_ready")
        la_ready = sem("la_ready")
        cs_ps = sem("cumulated_la_in_psum")
        cs_exp = sem("decay_factors_ready")
        score_ps = sem("scores_in_psum")
        score_ok = sem("scores_masked")
        st_loaded = sem("ssm_states_loaded")
        st_T = sem("ssm_states_transposed")
        st0_ok = sem("ssm_states_ready")
        xdw_ok = sem("weighted_x_ready")
        cst_ps = sem("chunk_states_in_psum")
        cst_out = sem("prompt_states_copied")
        st1_ok = sem("carried_states_ready")
        lam_ok = sem("masked_la_ready")
        seg_ps = sem("segment_sums_in_psum")
        seg_exp = sem("segment_decays_ready")
        g_ok = sem("decayed_scores_ready")
        y_ps = sem("mamba_y_in_psum")
        y_sb = sem("mamba_y_read")
        off_ps = sem("state_y_in_psum")
        off_rd = sem("state_y_read")
        gated = sem("mamba_y_gated")
        ysq = sem("mamba_y_squared")
        ynorm = sem("mamba_y_normalised")
        yT_ps = sem("mamba_y_transposed")
        yT_sb = sem("mamba_mix_ready")
        act_m = sem("act_mamba_steps")
        dve_l = sem("dve_mamba_loop_steps")
        up_loaded = sem("up_projections_loaded")
        wkv_loaded = sem("wkv_states_loaded")
        wkv_T = sem("wkv_states_transposed")
        wkv_ok = sem("wkv_states_ready")
        wd_ok = sem("low_rank_activated")
        aux_ps = sem("aux_in_psum")
        aux_act = sem("aux_read_by_act")
        aux_dve = sem("aux_read_by_dve")
        ksq_ok = sem("k_squared")
        exp_in = sem("decay_sums_ready")
        exp_ok = sem("decays_ready")
        tot_ok = sem("tile_sums_ready")
        ehalf_ok = sem("half_decays_ready")
        v_ok = sem("v_copied")
        ab_ok = sem("alpha_beta_ready")
        rb_ok = sem("bonus_ready")
        i4_ok = sem("identities_ready")
        gram_ps = sem("grams_in_psum")
        gram_rd = sem("grams_masked")
        x_ok = sem("inverse_level_ready")
        yl_ps = sem("level_y_in_psum")
        yl_ok = sem("level_y_ready")
        zl_ps = sem("level_z_in_psum")
        r0_ok = sem("wkv_start_states_ready")
        rhs_ps = sem("rhs_in_psum")
        rhs_ok = sem("rhs_ready")
        u_ps = sem("u_in_psum")
        u_ok = sem("u_ready")
        yo_ps = sem("wkv_y_in_psum")
        yo_rd = sem("wkv_y_read")
        ws_ps = sem("wkv_state_in_psum")
        yc_ok = sem("wkv_y_ready")
        ysq_ok = sem("wkv_y_squared")
        root_ok = sem("wkv_root_ready")
        pair_ok = sem("wkv_pair_done")
        fin_T = sem("wkv_final_transposed")
        fin_sb = sem("wkv_final_copied")
        dve_w = sem("dve_wkv_steps")
        dve_p = sem("dve_preparation_steps")
        dve_q = sem("dve_group_norm_steps")
        idle_dve = sem("idle_dve")
        idle_pool = sem("idle_pool")

        s_bufs = dict(locals())

        def slot(n):
            return ring[:, n % RING]

        def block_ready(eng, n):
            eng.wait_ge(w_in_slot[n % RING], 16 * (n // RING + 1))

        def block_used(eng, n):
            if n < XB:
                eng.wait_ge(ada_ps, n - ADA_A + 1)
            elif n < Z:
                eng.wait_ge(proj, 4 * (n - XB + 1))
            elif n < R:
                eng.wait_ge(proj, XBC + 3 * (n - Z + 1))
            elif n < ADA_B:
                eng.wait_ge(proj, XBC + 6 + min(4 * (n - R + 1), RT))
            elif n < WOUT:
                eng.wait_ge(ada_ps, 4 + n - ADA_B + 1)
            else:
                eng.wait_ge(out_ps, n - WOUT + 1)

        w_in_v = a["w_in"][0].rearrange("(k p) c -> p k c", p=P)
        w_ada_v = a["w_ada"][0].rearrange("(k p) c -> p k c", p=P)

        def block_source(n):
            if n < XB:
                return w_ada_v[:, :, BLK * n:BLK * (n + 1)]
            if n < Z:
                return w_in_v[:, :, D + BLK * (n - XB):D + BLK * (n - XB + 1)]
            if n < R:
                return w_in_v[:, :, BLK * (n - Z):BLK * (n - Z + 1)]
            if n < ADA_B:
                c = RC + BLK * (n - R)
                return w_in_v[:, :, c:min(c + BLK, RC + RT * P)]
            if n < GATES:
                c = ADA_COLS[4 + n - ADA_B]
                return w_ada_v[:, :, BLK * c:BLK * (c + 1)]

        TJ = ((1, 2), (0, 0), (2, 1))
        UNITS = ((0, 1), (1, 2), (0, 0), (1, 0))

        MEAN, VAR, KSQ, W_UP, A_UP, V_T, G_UP, BE_T, KAP_T, BONUS = 0, 1, 2, 3, 5, 7, 8, 9, 10, 11

        def aux_bank(n, width):
            return ps[:, 6 + n % 2, 0:width]

        def aux_free(pe, c, n):
            if n == MEAN:
                pe.wait_ge(aux_act, c * 10 + 10)
            elif n == VAR:
                pe.wait_ge(aux_dve, c * 2 + 2)
            elif n == KSQ:
                pe.wait_ge(aux_dve, c * 2 + 3)
            else:
                pe.wait_ge(aux_act, c * 10 + (10 + n - 2))
            return aux_bank(n, T)

        def aux_there(eng, c, n):
            eng.wait_ge(aux_ps, c * 12 + (12 + n + 1))

        def prep_pe(pe, c, n):
            o = aux_free(pe, c, n)
            if n == KSQ:
                pe.wait_ge(ksq_ok, c + 2)
                pe.matmul(o, bones[:, :], kroot, start=True, stop=True).then_inc(aux_ps, 1)
            elif n < V_T:
                if n == W_UP:
                    pe.wait_ge(up_loaded, c * 48 + 96)
                i, d = (n - W_UP) // 2, (n - W_UP) % 2
                pe.matmul(o, stw[64 * d:64 * d + 64, i, :], um_a[64 * d:64 * d + 64, 24 + i, :],
                          start=True, stop=True).then_inc(aux_ps, 1)
            elif n == V_T:
                pe.wait_ge(v_ok, c + 2)
                for j in range(NTILE):
                    mm = pe.transpose(o[:, P * j:P * j + P], v_c[:, P * j:P * j + P], ident[:, :])
                mm.then_inc(aux_ps, 1)
            elif n == G_UP:
                pe.matmul(o, stw[:, 2, :], um_a[:, 26, :], start=True, stop=True).then_inc(aux_ps, 1)
            elif n < BONUS:
                pe.wait_ge(ab_ok, c * 2 + (n - BE_T + 3))
                for i, (d, j) in enumerate(UNITS):
                    mm = pe.transpose(aux_bank(n, 4 * P)[:, P * i:P * i + P], (be, kap)[n - BE_T][:, d, j, :], ident[:, :])
                mm.then_inc(aux_ps, 1)
            else:
                pe.wait_ge(rb_ok, c + 2)
                pe.matmul(o, bones[:, :], rb, start=True, stop=True).then_inc(aux_ps, 1)

        def tail_pe(pe, c, n, p):
            o = aux_free(pe, c, n)
            src, done = ((y_c, yc_ok), (ysq_c, ysq_ok))[n % 2]
            pe.wait_ge(done, p + 1)
            pe.matmul(o, bones[:, :], src, start=True, stop=True).then_inc(aux_ps, 1)

        def round_pe(pe, c, b, prev, nxt):
            arr, btk, ktk, vtk, r0p = arrs[b], btks[b], ktks[b], vtks[b], r0ps[b]

            def fill(*numbers):
                for n in numbers:
                    if n >= KSQ and nxt:
                        prep_pe(pe, c, n)
                    elif n < KSQ and prev:
                        tail_pe(pe, c, n, c - 1)

            for g, src in enumerate((be, kap)):
                for s in range(3):
                    if g == 0:
                        pe.wait_ge(yo_rd, c * 3 + (s + 1))
                    else:
                        pe.wait_ge(gram_rd, c * 6 + (s + 1))
                    for d in range(2):
                        j = TJ[s][d]
                        for h in range(2):
                            mm = pe.matmul(ps[:, 2 * s + h, 256 * d:256 * d + 256], src[64 * h:64 * h + 64, d, j, :],
                                           arr[64 * h:64 * h + 64, d, j, :, :].rearrange("p a t -> p (a t)"),
                                           start=True, stop=True)
                    mm.then_inc(gram_ps, 1)
                if g == 0:
                    fill(MEAN)

            plan = {1: (VAR, KSQ), 2: (W_UP, W_UP + 1), 3: (A_UP, A_UP + 1), 4: (V_T, G_UP)}
            for l in range(1, 7):
                for s in range(3):
                    if s == 2 and l in plan:
                        fill(plan[l][0])
                    pe.wait_ge(x_ok, c * 21 + (3 * l - 3 + s + 1))
                    if l == 1:
                        pe.wait_ge(gram_rd, c * 6 + (3 + s + 1))
                    for h in range(2):
                        for d in range(2):
                            i = 2 * h + d
                            mm = pe.matmul(ps[:, 2 * s, P * i:P * i + P], gb[s][:, h, d, 0, :], xinv[s][:, h, d, :],
                                           start=True, stop=True)
                    mm.then_inc(yl_ps, 1)
                for s in range(3):
                    if s == 2 and l in plan:
                        fill(plan[l][1])
                    pe.wait_ge(yl_ok, c * 18 + (3 * l - 3 + s + 1))
                    for h in range(2):
                        for d in range(2):
                            o = P * (2 * h + d)
                            if l < 6:
                                mm = pe.matmul(ps[:, 2 * s + 1, o:o + P], xinvT[s][:, h, d, :], ys[s][:, h, d, :],
                                               start=True, stop=True)
                    if l >= 5:
                        bank = 2 * s + (l == 6)
                        for h in range(2):
                            for d in range(2):
                                o = P * (2 * h + d)
                                mm = pe.matmul(ps[:, bank, o:o + P], ys[s][:, h, d, :], xinvT[s][:, h, d, :],
                                               start=True, stop=True)
                    mm.then_inc(zl_ps, 1)

            def rhs(s):
                pe.wait_ge(x_ok, c * 21 + (18 + s + 1))
                if s != 1:
                    pe.wait_ge(r0_ok, c * 2 + (2 if s else 1))
                for h in range(2):
                    for d in range(2):
                        j, hp = TJ[s][d], slice(64 * h, 64 * h + 64)
                        o = ps[:, 2 * s + h, 64 * d:64 * d + 64]
                        mm = pe.matmul(o, gk[s][:, h, d, 0, :], vtk[:, j, hp], start=True, stop=(s == 1))
                        if s != 1:
                            mm = pe.matmul(o, arr[hp, d, j, 0, :], r0p[hp, s // 2, d, :], start=False, stop=True)
                mm.then_inc(rhs_ps, 1)

            def u(s):
                pe.wait_ge(rhs_ok, c * 3 + (s + 1))
                for i in range(4):
                    mm = pe.matmul(ps[:, 2 * s + 1, 128 + 64 * i:192 + 64 * i], xinvT[s][:, i // 2, i % 2, :], rhs_s[s][:, i, :],
                                   start=True, stop=True)
                mm.then_inc(u_ps, 1)

            def end_state(s):
                pe.wait_ge(u_ok, c * 3 + (s + 1))
                for d in range(2):
                    for h in range(2):
                        j, hp, un = TJ[s][d], slice(64 * h, 64 * h + 64), 2 * s + d
                        o = ps[hp, 2 * s + 1, 384 + 64 * d:448 + 64 * d]
                        pe.matmul(o, ktk[:, un, hp], vtk[:, j, hp], start=True, stop=False)
                        mm = pe.matmul(o, btk[:, un, hp], us[s][:, 2 * h + d, :], start=False, stop=True)
                mm.then_inc(ws_ps, 1)

            def y_out(s):
                pe.wait_ge(u_ok, c * 3 + (s + 1))
                for h in range(2):
                    for d in range(2):
                        i, j, hp = 2 * h + d, TJ[s][d], slice(64 * h, 64 * h + 64)
                        o = ps[hp, 2 * s, 256 + P * (0 if s == 1 else d):256 + P * (0 if s == 1 else d) + P]
                        first, last = (d == 0 or s != 1), (d == 1 or s != 1)
                        pe.matmul(o, vtk[:, j, hp], gk[s][:, h, d, 1, :], start=first, stop=False)
                        mm = pe.matmul(o, us[s][:, i, :], gb[s][:, h, d, 1, :], start=False, stop=(last and s == 1))
                        if s != 1:
                            mm = pe.matmul(o, r0p[hp, s // 2, d, :], arr[hp, d, j, 1, :], start=False, stop=True)
                mm.then_inc(yo_ps, 1)

            rhs(0)
            rhs(1)
            u(0)
            u(1)
            end_state(0)
            y_out(0)
            end_state(1)
            rhs(2)
            y_out(1)
            u(2)
            fill(BE_T, KAP_T)
            y_out(2)
            fill(BONUS)

        def prep_act(act, c, b, n):
            aux_there(act, c, n)
            src = aux_bank(n, T)
            if n == KSQ:
                ins = act.activation(kroot, src, ACT.Sqrt)
            elif n < V_T:
                i, d = (n - W_UP) // 2, (n - W_UP) % 2
                bias = pv1[:, ds(c + (V1[("w0", "a0")[i]] + 8 * d + 1), 1)]
                ins = act.activation((sg, am)[i][:, d, :], src, ACT.Sigmoid, bias=bias)
            elif n == V_T:
                ins = act.activation(vtks[b].rearrange("p j t -> p (j t)"), src, ACT.Copy)
            elif n == G_UP:
                ins = act.activation(g_cs[b], src, ACT.Copy)
            elif n == BE_T:
                ins = act.activation(btks[b].rearrange("p i t -> p (i t)"), aux_bank(n, 4 * P), ACT.Copy, scale=-1.0)
            else:
                ins = act.activation(ktks[b].rearrange("p i t -> p (i t)"), aux_bank(n, 4 * P), ACT.Copy)
            ins.then_inc(aux_act, 1)

        def exps_act(act, c, b):
            act.wait_ge(tot_ok, c + 2)
            act.activation(e_halfs[b], tot, ACT.Exp, scale=0.5 * NEG_C).then_inc(ehalf_ok, 1)
            act.wait_ge(exp_in, c + 2)
            for dst, src, sc in ((e_m, csm, NEG_C), (e_p, cs, NEG_C), (e_i, cs, -NEG_C)):
                act.activation(dst, src, ACT.Exp, scale=sc).then_inc(exp_ok, 1)

        def tail_act(act, c, n):
            aux_there(act, c, n)
            act.activation(ysq_c, aux_bank(n, T), ACT.Sqrt, scale=1.0 / 64, bias=eps_gn[:, 0:1]).then_inc(aux_act, 1)

        def round_act(act, c, b, prev, nxt):
            for l in range(1, 7):
                for s in range(3):
                    act.wait_ge(yl_ps, c * 18 + (3 * l - 3 + s + 1))
                    act.activation(ys[s].rearrange("p a b q -> p (a b q)"), ps[:, 2 * s, :], ACT.Copy).then_inc(yl_ok, 1)
                if l == 1 and prev:
                    tail_act(act, c, VAR)
                if nxt:
                    for n in {1: (KSQ,), 2: (W_UP, W_UP + 1), 3: (A_UP, A_UP + 1), 4: (V_T, G_UP)}.get(l, ()):
                        prep_act(act, c, 1 - b, n)
                    if l == 4:
                        exps_act(act, c, 1 - b)

            def rhs_copy(s):
                act.wait_ge(rhs_ps, c * 3 + (s + 1))
                act.activation(rhs_s[s].rearrange("p (h d) v -> p h (d v)", h=2), ps[:, 2 * s:2 * s + 2, 0:128],
                               ACT.Copy).then_inc(rhs_ok, 1)

            def u_copy(s):
                act.wait_ge(u_ps, c * 3 + (s + 4))
                act.activation(us[s].rearrange("p i v -> p (i v)"), ps[:, 2 * s + 1, 128:384],
                               ACT.Copy).then_inc(u_ok, 1)
            rhs_copy(0)
            rhs_copy(1)
            u_copy(0)
            u_copy(1)
            rhs_copy(2)
            u_copy(2)
            if nxt:
                prep_act(act, c, 1 - b, BE_T)
                prep_act(act, c, 1 - b, KAP_T)

        def tile_of(i):
            return um_a[:, ds(i, 1), :].rearrange("p a t -> p (a t)")

        def wcol_of(name, c):
            return pv1[:, ds(c + V1[name], 1)]

        def both(ap):
            return ap.unsqueeze(1).to_broadcast([P, 2, T])

        def tiles(ap):
            return ap.rearrange("p d (j t) -> p d j t", j=NTILE)

        def tiles2(ap):
            return ap.rearrange("p (j t) -> p j t", j=NTILE).unsqueeze(1).to_broadcast([P, 2, NTILE, P])

        def prep_dve(dve, c, b, lc, part):
            k = tile_of(c + 9)
            if part == 0:
                lc.do(dve.tensor_scalar(kk, k, wcol_of("k_k", c + 1), None, ALU.mult))
                dve.tensor_tensor(kroot, kk, kk, ALU.mult).then_inc(ksq_ok, 1)
            elif part == 1:
                dve.wait_ge(aux_act, c * 10 + (10 + KSQ))
                lc.do(dve.tensor_scalar(kroot, kroot, 1e-12, None, ALU.max))
                lc.do(dve.reciprocal(kroot, kroot))
                lc.do(dve.tensor_tensor(kk, kk, kroot, ALU.mult))
            elif part == 2:
                dve.wait_ge(aux_act, c * 10 + (10 + W_UP + 1))
                dve.tensor_tensor_scan(cs[:, 0, :], rst[:, 0, :], sg[:, 0, :], 0.0, ALU.mult, ALU.add)
                lc.do(dve.tensor_tensor_scan(cs[:, 1, ::-1], rst[:, 1, ::-1], sg[:, 1, ::-1], 0.0, ALU.mult, ALU.add))
                dve.tensor_copy(tot[:, 0, :], cs[:, 0, P - 1::P])
                dve.tensor_copy(tot[:, 1, :], cs[:, 1, 0::P]).then_inc(tot_ok, 1)
                dve.wait_ge(tot_ok, c + 2)
                cs6 = cs.rearrange("p d (j t) -> p (d j) t", j=NTILE)
                lc.do(dve.scalar_tensor_tensor(cs6, tot.rearrange("p d j -> p (d j)").unsqueeze(2).to_broadcast([P, 6, P]),
                                               -0.5, cs6, ALU.mult, ALU.add))
                dve.tensor_tensor(csm, cs, sg, ALU.subtract).then_inc(exp_in, 1)
            elif part == 3:
                dve.wait_ge(aux_act, c * 10 + (10 + A_UP + 1))
                lc.do(dve.tensor_scalar(kd, am, wcol_of("k_a", c + 1), kam[:, ds(c + 1, 1)], ALU.mult, ALU.add))
                dve.tensor_tensor(am, am, both(kk), ALU.mult)
                lc.do(dve.tensor_tensor(kd, kd, both(k), ALU.mult))
            elif part == 4:
                dve.wait_ge(exp_ok, c * 3 + 6)
                dve.tensor_tensor(arrs[b][:, :, :, 0, :], tiles2(kk), tiles(e_m), ALU.mult)
                dve.tensor_tensor(arrs[b][:, :, :, 1, :], tiles2(tile_of(c + 1)), tiles(e_p), ALU.mult)
            elif part == 5:
                dve.tensor_tensor(be, tiles(am), tiles(e_i), ALU.mult).then_inc(ab_ok, 1)
                dve.tensor_tensor(kap, tiles(kd), tiles(e_i), ALU.mult).then_inc(ab_ok, 1)
                lc.do(dve.tensor_tensor(rb, kd[:, 0, :], kd[:, 1, :], ALU.add))
                dve.scalar_tensor_tensor(rb, rb, wcol_of("r_k", c + 1), tile_of(c + 1), ALU.mult, ALU.mult).then_inc(rb_ok, 1)
            else:
                dve.wait_ge(ehalf_ok, c + 2)
                for d in range(2):
                    j = TJ[0][d]
                    ins = dve.tensor_scalar(r0ps[b][:, 0, d, :], r0all[:, ds(c + 1, 1), d, :].rearrange("p a v -> p (a v)"),
                                      e_halfs[b][:, d, j:j + 1], None, ALU.mult)
                ins.then_inc(r0_ok, 1)
                aux_there(dve, c, BONUS)
                dve.wait_ge(v_ok, c + 2)
                dve.tensor_tensor(vbs[b], aux_bank(BONUS, T), v_c, ALU.mult).then_inc(aux_dve, 1)

        def tail_dve(dve, c, n, p, b, lc, part):
            if part == 0:
                aux_there(dve, c, n)
                dve.scalar_tensor_tensor(yc0, aux_bank(n, T), -1.0 / 64, y_c, ALU.mult, ALU.add).then_inc(aux_dve, 1)
                dve.wait_ge(aux_dve, c * 2 + (3 if n == 0 else 4))
                dve.tensor_tensor(ysq_c, yc0, yc0, ALU.mult).then_inc(ysq_ok, 1)
            else:
                dve.wait_ge(aux_act, c * 10 + (11 if n == 0 else 12))
                lc.do(dve.reciprocal(ysq_c, ysq_c))
                lc.do(dve.tensor_tensor(yc0, yc0, ysq_c, ALU.mult))
                lc.do(dve.tensor_scalar(yc0, yc0, wcol_of("ln_w", p), wcol_of("ln_b", p), ALU.mult, ALU.add))
                lc.do(dve.tensor_tensor(yc0, yc0, vbs[b], ALU.add))
                dve.tensor_tensor(tile_of(p), yc0, g_cs[b], ALU.mult).then_inc(pair_ok, 1)

        def round_dve(dve, c, b, prev, nxt):
            lc = LoopChain(dve, dve_w, c, 19)
            pc = LoopChain(dve, dve_p, c + 1, 9)
            tc = LoopChain(dve, dve_q, c - 1, 4)
            r0p, e_half = r0ps[b], e_halfs[b]
            for g in range(2):
                for s in range(3):
                    dve.wait_ge(gram_ps, c * 6 + (3 * g + s + 1))
                    dst = (gb, gk)[g][s].rearrange("p h a b q -> p h (a b q)")
                    m = (trin, tri)[g][:, :, :].rearrange("p i q -> p (i q)").unsqueeze(1).to_broadcast([P, 2, 512])
                    ins = dve.tensor_tensor(dst, ps[:, 2 * s:2 * s + 2, :], m, ALU.mult)
                    ins.then_inc(gram_rd, 1)
                    if g == 0:
                        dve.wait_ge(gram_rd, c * 6 + (s + 1))
                        dve.wait_ge(i4_ok, c * 3 + (s + 1))
                        dve.sem_inc(idle_dve, 1)
                        for h in range(2):
                            ins = dve.copy_predicated(xinvT[s][:, h], lvl[:, 0, ::-1, :].bitcast(I32), gb[s][:, h, :, 0, :])
                        lc.do(ins)
                        dve.transpose(xinv[s].rearrange("p a b q -> p (a b q)"),
                                      xinvT[s].rearrange("p a b q -> p (a b q)")).then_inc(x_ok, 1)
                if g == 0:
                    if prev:
                        tail_dve(dve, c, MEAN, c - 1, 1 - b, tc, 0)
                    if nxt:
                        prep_dve(dve, c, 1 - b, pc, 0)
            for l in range(1, 7):
                for s in range(3):
                    dve.wait_ge(zl_ps, c * 18 + (3 * l - 3 + s + 1))
                    dve.sem_inc(idle_dve, 1)
                    z = ps[:, 2 * s + 1, :].rearrange("p (h d q) -> p h d q", h=2, d=2)
                    zt = ps[:, 2 * s + (l == 6), :].rearrange("p (h d q) -> p h d q", h=2, d=2)
                    for h in range(2):
                        if l < 6:
                            ins = dve.copy_predicated(xinv[s][:, h], lvl[:, l, :, :].bitcast(I32), z[:, h])
                        if l >= 5:
                            ins = dve.copy_predicated(xinvT[s][:, h], lvl[:, l, ::-1, :].bitcast(I32), zt[:, h])
                    if l < 5:
                        lc.do(ins)
                        ins = dve.transpose(xinvT[s].rearrange("p a b q -> p (a b q)"),
                                            xinv[s].rearrange("p a b q -> p (a b q)"))
                    ins.then_inc(x_ok, 1)
                if l == 1 and prev:
                    tail_dve(dve, c, MEAN, c - 1, 1 - b, tc, 1)
                elif l > 1 and nxt:
                    prep_dve(dve, c, 1 - b, pc, l - 1)
            dve.wait_ge(ws_ps, c * 2 + 1)
            for d in range(2):
                j, j2 = TJ[0][d], TJ[2][d]
                lc.do(dve.tensor_tensor(r0p[:, 1, d, :], ps[:, 1, 384 + 64 * d:448 + 64 * d], r0p[:, 0, d, :], ALU.add))
                ins = dve.tensor_scalar(r0p[:, 1, d, :], r0p[:, 1, d, :], e_half[:, d, j:j + 1],
                                        e_half[:, d, j2:j2 + 1], ALU.mult, ALU.mult)
            ins.then_inc(r0_ok, 1)
            dve.wait_ge(yo_ps, c * 3 + 1)
            dve.tensor_copy(y_c[:, P:T], ps[:, 0, 256:512]).then_inc(yo_rd, 1)
            dve.wait_ge(ws_ps, c * 2 + 2)
            for d in range(2):
                lc.do(dve.tensor_scalar(sall[:, ds(c, 1), d, :].rearrange("p a v -> p (a v)"),
                                        ps[:, 3, 384 + 64 * d:448 + 64 * d], e_half[:, d, 0:1], None, ALU.mult))
            dve.wait_ge(yo_ps, c * 3 + 2)
            dve.tensor_copy(y_c[:, 0:P], ps[:, 2, 256:384]).then_inc(yo_rd, 1)
            dve.wait_ge(yo_ps, c * 3 + 3)
            dve.wait_ge(yo_rd, c * 3 + 4)
            dve.tensor_tensor(y_c[:, 2 * P:T], y_c[:, 2 * P:T], ps[:, 4, 256:384], ALU.add)
            dve.tensor_tensor(y_c[:, P:2 * P], y_c[:, P:2 * P], ps[:, 4, 384:512], ALU.add).then_inc(yo_rd, 1)
            dve.wait_ge(yo_rd, c * 3 + 6)
            dve.sem_inc(yc_ok, 1)
            if nxt:
                prep_dve(dve, c, 1 - b, pc, 6)
                pc.end()
            if prev:
                tc.end()
            lc.end()

        x1 = at(misc, 0, NTILE, D)
        g1 = at(misc, 3072, 2, D)
        g2 = at(misc, 5120, 2, D)
        h2 = at(misc, 7168, NTILE, D)
        brow = misc[0:2, 10240:12288]
        um_f = um_a[:, :, :].rearrange("p i t -> p (i t)")
        xg = at(um_f, 0, 2, D)
        xgT = at(um_f, 2048, 2, KT, P)
        yg = at(um_f, 4096, 2, D)
        hs = at(um_f, 6144, 2, DE)
        hid = at(um_f, 6656, 2, DE)
        hidT = at(um_f, 7168, 2, 2, P)
        wr = at(um_f, 7680, KT, 36)
        h2sq = at(um_f, 0, D)
        mx_f = mixm[:, :, :].rearrange("p i t -> p (i t)")
        fnw = at(mx_f, 0, D)
        ymoe = misc[:, 10240:10240 + D]
        lg = at(scratch, 0, NTILE, 36)
        msk = at(scratch, 108, NTILE, 32)
        tmp = at(scratch, 204, NTILE, 32)
        oh = at(scratch, 300, 2, NTILE, 32)
        both_oh = at(scratch, 492, NTILE, 32)
        slot_v = at(scratch, 588, NTILE, 32)
        ghot = at(scratch, 684, NTILE, 4)
        grp2 = at(scratch, 696, NTILE, 4)
        s3 = at(scratch, 708, 10, NTILE)
        cnt = at(scratch, 738, 4, 32)
        slots = at(scratch, 866, 2, NTILE)
        rowsT = scratch[0:N_GROUPS, 880:1008]
        tokid = at(scratch, 1008, NTILE)
        erow = at(scratch, 1011, 32)
        down = at(scratch, 1043, 36)
        brt = at(scratch, 1079, 36)
        fst = mstat[:, 0:12]
        wcol = at(scratch, 1127, 2, NTILE)
        meta = at(scratch, 1136, 1 + N_CHUNKS)
        mq = at(scratch, 1184, N_CHUNKS - NE, NE)
        mq2 = at(scratch, 1568, N_CHUNKS - NE, NE)
        wdt_f = wdt[:, :, :].rearrange("p k c -> p (k c)")
        slots_i = wdt_f[:, 0:6].bitcast(U32)
        idx = wdt_f[:, 16:16 + N_GROUPS].bitcast(U32)
        idx1 = wdt_f[:, 56:58].bitcast(U32)
        meta_i = wdt_f[:, 64:65 + N_CHUNKS].bitcast(I32)
        zrow = vrows[0:N_GROUPS, 0, :]
        cmb = at(um_f, 0, 2, 2, D)
        zero_z = sem("zeros_made")
        rconst = sem("router_constants")
        half = [ring_a[:, 6144 * i:6144 * (i + 1)] for i in range(2)]
        wgu = [[[(at(h, 0, KT, 2 * DE), 0, KT)] for h in half],
               [[(at(misc, 7168, KT, 2 * DE), 0, KT)],
                [(at(misc, 3072, 4, 2 * DE), 0, 4), (at(mx_f, D, 4, 2 * DE), 4, 4)]]]
        wdn = [[at(h, 4096, 2, D) for h in half], [at(hT_flat, 0, 2, D), at(um_f, 7968, 2, D)]]
        GU_LOADS, DN_LOADS = (4, 6), 2

        def gate_up_tile(b, x, k):
            return next(v[:, k - k0, :] for v, k0, n in wgu[b][x] if k0 <= k < k0 + n)

        h_dram = nc.dram_tensor("h_rows", [T, D], F32).ap()
        slot_dram = nc.dram_tensor("slot_tokens", [N_GROUPS * P, 1], F32).ap()
        y_dram = nc.dram_tensor("expert_rows", [N_GROUPS * P, D], F32).ap()

        x_again = sem("x_loaded_again")
        brow_in = sem("gate_bias_loaded")
        gate_ps = sem("gate_rows_in_psum")
        gate_ok = sem("gates_ready")
        bias_ok = sem("gate_rows_biased")
        out_ps = sem("mix_product_in_psum")
        x1_ok = sem("x1_ready")
        late_in = sem("router_and_norm_loaded")
        sq2_ok = sem("x1_squared")
        xn2_ok = sem("x1_normalised")
        h2T_ps = sem("x1_transposed")
        h2T_ok = sem("h2_channel_major_ready")
        h2_ps = sem("h2_transposed_back")
        h2_ok = sem("h2_token_major_ready")
        h2_out = sem("h2_rows_stored")
        lg_ps = sem("logits_in_psum")
        rt_act = sem("router_exps")
        rt_dve = sem("router_steps_for_act")
        a_ok = sem("assignments_ready")
        rank_ps = sem("ranks_in_psum")
        slots_ok = sem("slots_ready")
        zero_ok = sem("slot_table_zeroed")
        scat = sem("tokens_scattered")
        rows_in = sem("slot_rows_loaded")
        rows_ps = sem("slot_rows_transposed")
        idx_ok = sem("gather_indices_ready")
        idc = sem("index_column_ready")
        xg_in = [sem("rows_gathered_0"), sem("rows_gathered_1")]
        gu_in = [sem("gate_up_loaded_0"), sem("gate_up_loaded_1")]
        dn_in = [sem("down_loaded_0"), sem("down_loaded_1")]
        yst = [sem("expert_rows_stored_0"), sem("expert_rows_stored_1")]
        xt_ps = sem("rows_transposed")
        xt_rd = sem("rows_ready")
        gu_ps = sem("gate_up_in_psum")
        silu_ok = sem("silu_ready")
        hid_ok = sem("hidden_ready")
        ht_ps = sem("hidden_transposed")
        ht_rd = sem("hidden_channel_major_ready")
        dn_ps = sem("down_in_psum")
        yg_ok = sem("expert_rows_ready")
        comb = [sem("combined_rows_0"), sem("combined_rows_1")]
        moe_ok = sem("moe_summed")
        y_ok = sem("y_ready")

        def wout_block(n):
            return ring[:, n % RING].rearrange("p k c -> p (k c)").rearrange("p (k c) -> p k c", k=4)

        def gate_rows(pe, i):
            pe.wait_ge(bias_ok, i + 1)
            for v in range(2):
                if i:
                    pe.wait_ge(gate_ok, 2 * i - 1 + v)
                pe.matmul(ps[:, 6 + v, :], selb[:, v, :], adas[:, i % 2, :], start=True, stop=True).then_inc(gate_ps, 1)

        def late(n, at_least):
            return not isinstance(n, int) or n >= at_least

        def gather(pool, n, b):
            if late(n, 2):
                pool.wait_ge(xt_ps, n - 1)
            pool.sem_inc(idle_pool, 1)
            pool.tensor_copy(idx1[:, b:b + 1], idx[:, ds(n, 1)]).then_inc(idc, 1)
            pool.wait_ge(idc, n + 1)
            pool.sem_inc(idle_pool, 1)
            pool.indirect_dma_start(out=xg[:, b, :], out_offset=None, in_=h_dram,
                                    in_offset=bass.IndirectOffsetOnAxis(ap=idx1[:, b:b + 1], axis=0)
                                    ).then_inc(xg_in[b], 16)

        def expert_weights(sp, n, b, experts):
            if late(n, 2):
                sp.wait_ge(gu_ps, n - 1)
            for x in range(2):
                for i, name in enumerate(("moe_w_gate", "moe_w_up")):
                    for v, k0, kn in wgu[b][x]:
                        sp.dma_start(v[:, :, DE * i:DE * i + DE],
                                     a[name][0, ds(experts[x], 1), P * k0:P * (k0 + kn)].rearrange("a (k p) f -> p (a k) f", p=P)
                                     ).then_inc(gu_in[b], 16)
            if late(n, 2):
                sp.wait_ge(dn_ps, n - 1)
            for x in range(2):
                sp.dma_start(wdn[b][x], a["moe_w_down"][0, ds(experts[x], 1)].rearrange("a (k p) c -> p (a k) c", p=P)
                             ).then_inc(dn_in[b], 16)

        def rows_T(pe, n, b):
            if late(n, 1):
                pe.wait_ge(xt_rd, n)
            for k in range(KT):
                mm = pe.transpose(ps[:, k // 4, P * (k % 4):P * (k % 4) + P], xg[:, b, P * k:P * k + P], ident[:, :])
            mm.then_inc(xt_ps, 1)

        def gate_up(pe, n, b):
            pe.wait_ge(xt_rd, n + 1)
            if late(n, 2):
                pe.wait_ge(hid_ok, n - 1)
            for k in range(KT):
                for x in range(2):
                    h = slice(CH * x, CH * x + CH)
                    mm = pe.matmul(ps[h, 2 + b, :], xgT[:, b, k, h], gate_up_tile(b, x, k), start=(k == 0),
                                   stop=(k == KT - 1), tile_position=(0, CH * x), skip_group_check=True)
            mm.then_inc(gu_ps, 1)

        def down_proj(pe, m, b):
            pe.wait_ge(hid_ok, m + 1)
            if late(m, 1):
                pe.wait_ge(ht_rd, m)
            for k in range(2):
                mm = pe.transpose(ps[:, 4, P * k:P * k + P], hid[:, b, P * k:P * k + P], ident[:, :])
            mm.then_inc(ht_ps, 1)
            pe.wait_ge(ht_rd, m + 1)
            if late(m, 1):
                pe.wait_ge(yg_ok, m)
            for c in range(2):
                for k in range(2):
                    for x in range(2):
                        h = slice(CH * x, CH * x + CH)
                        mm = pe.matmul(ps[h, 5 + c, :], hidT[:, b, k, h], wdn[b][x][:, k, BLK * c:BLK * c + BLK],
                                       start=(k == 0), stop=(k == 1), tile_position=(0, CH * x), skip_group_check=True)
            mm.then_inc(dn_ps, 1)

        def rows_copy(dve, n, b):
            dve.wait_ge(xt_ps, n + 1)
            if late(n, 2):
                dve.wait_ge(gu_ps, n - 1)
            dve.tensor_copy(xgT[:, b, :, :].rearrange("p (g k) t -> p g (k t)", g=2), ps[:, 0:2, :]).then_inc(xt_rd, 1)

        def hidden(dve, m, b):
            dve.wait_ge(silu_ok, m + 1)
            if late(m, 2):
                dve.wait_ge(ht_ps, m - 1)
            dve.tensor_tensor(hid[:, b, :], hs[:, b, :], ps[:, 2 + b, DE:2 * DE], ALU.mult).then_inc(hid_ok, 1)
            dve.wait_ge(ht_ps, m + 1)
            if late(m, 2):
                dve.wait_ge(dn_ps, m - 1)
            dve.tensor_copy(hidT[:, b, :, :].rearrange("p k t -> p (k t)"), ps[:, 4, 0:256]).then_inc(ht_rd, 1)

        def silu_gate(act, n, b):
            act.wait_ge(gu_ps, n + 1)
            if late(n, 2):
                act.wait_ge(hid_ok, n - 1)
            act.activation(hs[:, b, :], ps[:, 2 + b, 0:DE], ACT.Silu).then_inc(silu_ok, 1)

        def expert_out(act, m, b):
            act.wait_ge(dn_ps, m + 1)
            if late(m, 2):
                act.wait_ge(yst[b], (m - b) * 8)
            act.activation(yg[:, b, :].rearrange("p (c n) -> p c n", c=2), ps[:, 5:7, :], ACT.Copy).then_inc(yg_ok, 1)
            act.wait_ge(yg_ok, m + 1)
            act.dma_start(y_dram[ds(m * P, P), :], yg[:, b, :]).then_inc(yst[b], 16)

        def turns(eng):
            return eng.value_load(meta_i[0:1, 0:1], min_val=0, max_val=OV_TURNS) + NG // 2

        block = ctx.enter_context(nc.Block())

        @block.sync
        def _(sp):
            rows = [(vrows[0:48, 0, :], a["b_ada"].rearrange("a (t p) -> (a t) p", p=P)),
                    (vrows[48:56, 0, :], a["norm1_w"].rearrange("a (t p) -> (a t) p", p=P)),
                    (vrows[56:116, 0, :], a["m_conv_w"].rearrange("a j (t p) -> (a j t) p", p=P)),
                    (vrows[116:128, 0, :], a["m_conv_b"].rearrange("a (t p) -> (a t) p", p=P)),
                    (vrows[0:27, 1, :], a["r_mu"].rearrange("a (t p) -> (a t) p", p=P)),
                    (vrows[27:43, 1, :], a["r_w0"].rearrange("a d (t p) -> (a d t) p", p=P)),
                    (vrows[43:59, 1, :], a["r_a0"].rearrange("a d (t p) -> (a d t) p", p=P)),
                    (vrows[59:67, 1, :], a["r_k_k"].rearrange("a (t p) -> (a t) p", p=P)),
                    (vrows[67:75, 1, :], a["r_k_a"].rearrange("a (t p) -> (a t) p", p=P)),
                    (vrows[75:83, 1, :], a["r_r_k"].rearrange("a (t h) n -> (a t) (h n)", h=2)),
                    (vrows[83:91, 1, :], a["r_ln_w"].rearrange("a (t p) -> (a t) p", p=P)),
                    (vrows[91:99, 1, :], a["r_ln_b"].rearrange("a (t p) -> (a t) p", p=P)),
                    (vrows[99:107, 1, :], a["norm2_w"].rearrange("a (t p) -> (a t) p", p=P)),
                    (vrows[107:115, 1, :], a["m_norm_w"].rearrange("a (t p) -> (a t) p", p=P)),
                    (crows[0:8, :], a["c_ctx"].rearrange("(t p) -> t p", p=P)),
                    (crows[8:16, :], a["c"].rearrange("a (t p) -> (a t) p", p=P)),
                    (drow[:, 0:32], a["m_dt_bias"].rearrange("a d h -> a (d h)").broadcast_to([P, 32])),
                    (drow[:, 32:64], a["m_a_log"].rearrange("a d h -> a (d h)").broadcast_to([P, 32])),
                    (drow[:, 64:80], a["m_d_skip"].broadcast_to([P, 16]))]
            assert len(rows) == N_SMALL
            for dst, src in rows:
                sp.dma_start(dst, src).then_inc(s_small, 16)
            sp.dma_start(xt[:, 0, :], a["x_prompt"][0]).then_inc(s_x, 16)
            sp.dma_start(xt[:, 1:3, :], a["x_sample"][0].rearrange("(j p) c -> p j c", p=P)).then_inc(s_x, 16)
            for n in range(GATES):
                if n >= RING:
                    block_used(sp, n - RING)
                src = block_source(n)
                sp.dma_start(slot(n)[:, :, 0:src.shape[2]], src).then_inc(w_in_slot[n % RING], 16)
                if n == XB:
                    sp.dma_start(wdt[:, :, :], w_in_v[:, :, DTC:DTC + 32]).then_inc(s_wdt, 16)
            sp.wait_ge(zero_z, 1)
            zsrc = zrow[0:16, :].unsqueeze(1)
            sp.dma_start(y_dram[NG * P:N_GROUPS * P, :].rearrange("(p r) (s c) -> p (r s) c", p=16, c=P),
                         zsrc.to_broadcast([16, (N_GROUPS - NG) * D // 16, P])).then_inc(zero_ok, 16)
            sp.dma_start(slot_dram.rearrange("(n p) a -> n (p a)", p=P), zrow[:, :]).then_inc(zero_ok, 16)
            sp.wait_ge(ada_ps, 6)
            for d, name in enumerate(("state_ssm_fwd", "state_ssm_bwd")):
                sp.dma_start(st_in[:, d], a[name][0, 0].rearrange("(i h) p n -> (h p) i n", h=2)).then_inc(st_loaded, 16)
            for d in range(2):
                sp.wait_ge(cst_out, d + 1)
                sp.dma_start(out[2 + d][0, 0].rearrange("(i h) p n -> (h p) i n", h=2), st_out[:, d]).then_inc(out_done, 16)
            sp.wait_ge(conv_tm, 10)
            sp.wait_ge(conv_out, XBC)
            for d, name in enumerate(("state_wkv_fwd", "state_wkv_bwd")):
                sp.dma_start(wkv_in[:, d, :].rearrange("v (h n) -> v h n", h=16),
                             a[name][0, 0].rearrange("h v n -> v h n")).then_inc(wkv_loaded, 16)

            ups = [a["r_w_up"][0].rearrange("d r c -> (d r) c"), a["r_a_up"][0].rearrange("d r c -> (d r) c"),
                   a["r_g_up"][0]]
            for i, w in enumerate(ups):
                sp.dma_start(stw[:, i, :], w[:, 0:P]).then_inc(up_loaded, 16)
            with sp.Fori(0, 7) as c:
                sp.wait_ge(aux_ps, c * 12 + 9)
                for i, w in enumerate(ups):
                    sp.dma_start(stw[:, i, :], w[:, ds(c * P + P, P)]).then_inc(up_loaded, 16)
            sp.wait_ge(pair_ok, 9)
            x_row = [(x1[:, 0, :], a["x_prompt"][0]),
                     (x1[:, 1:3, :], a["x_sample"][0].rearrange("(j p) c -> p j c", p=P))]
            for v in range(2):
                for i, c in enumerate((2, 5)):
                    sp.dma_start(brow[v:v + 1, D * i:D * i + D], a["b_ada"][:, D * c:D * c + D]).then_inc(brow_in, 16)
            for n in range(GATES, WOUT + 4):
                if n >= GATES + RING:
                    block_used(sp, n - RING)
                if n < WOUT:
                    c = (4, 5, 10, 11)[n - GATES]
                    sp.dma_start(slot(n), w_ada_v[:, :, BLK * c:BLK * (c + 1)]).then_inc(w_in_slot[n % RING], 16)
                else:
                    q = n - WOUT
                    sp.dma_start(wout_block(n), a["w_out"][0, BLK * q:BLK * (q + 1)].rearrange("(k p) c -> p k c", p=P)
                                 ).then_inc(w_in_slot[n % RING], 16)
                if n == GATES + 2:
                    for dst, src in x_row:
                        sp.dma_start(dst, src).then_inc(x_again, 16)
            sp.wait_ge(fin_sb, 2)
            for d in range(2):
                sp.dma_start(out[4 + d][0, 0].rearrange("h v n -> v h n"),
                             wkv_in[:, d, :].rearrange("v (h n) -> v h n", h=16)).then_inc(out_done, 16)
            sp.wait_ge(out_done, 16 * 4)
            sp.wait_ge(out_ps, 4)
            sp.dma_start(brt[:, 0:4], a["moe_b_grp"].broadcast_to([P, 4])).then_inc(late_in, 16)
            sp.dma_start(brt[:, 4:36], a["moe_b_exp"].broadcast_to([P, 32])).then_inc(late_in, 16)
            sp.dma_start(wr[:, :, 0:4], a["moe_w_grp"][0].rearrange("(k p) c -> p k c", p=P)).then_inc(late_in, 16)
            sp.dma_start(wr[:, :, 4:36], a["moe_w_exp"][0].rearrange("(k p) c -> p k c", p=P)).then_inc(late_in, 16)
            sp.dma_start(fnw, a["final_norm_w"].rearrange("(a c) -> a c", a=1).broadcast_to([P, D])).then_inc(late_in, 16)
            expert_weights(sp, 0, 0, (0, 1))
            sp.wait_ge(h2_ok, 3)
            sp.dma_start(h_dram.rearrange("(j p) c -> p j c", p=P), h2).then_inc(h2_out, 16)
            sp.wait_ge(scat, 16 * 6)
            sp.dma_start(rowsT, slot_dram.rearrange("(n p) a -> n (p a)", p=P)).then_inc(rows_in, 16)
            sp.wait_ge(h2_out, 16)
            expert_weights(sp, 1, 1, (2, 3))
            sp.wait_ge(idx_ok, 1)
            with sp.Fori(1, turns(sp)) as i:
                for b in range(2):
                    experts = [sp.value_load(meta_i[0:1, ds(i * 4 + (2 * b + x + 1), 1)], min_val=0, max_val=NE - 1)
                               for x in range(2)]
                    expert_weights(sp, i * 2 + b, b, experts)
            for j in range(NTILE):
                sp.wait_ge(y_ok, j + 1)
                dst = out[0][0] if j == 0 else out[1][0, P * (j - 1):P * j, :]
                sp.dma_start(dst, x1[:, j, :]).then_inc(out_done, 16)
            sp.wait_ge(out_done, 16 * 7)
            if dump:
                for eng_sem, v in dump["after"](s_bufs):
                    sp.wait_ge(eng_sem, v)
                nd = 0
                for name, (ap, _) in dump["what"](s_bufs).items():
                    sp.dma_start(dump["to"][name], ap).then_inc(out_done, 16)
                    nd += 1
                sp.wait_ge(out_done, 16 * (nd + N_OUT))

        @block.gpsimd
        def _(pool):
            g = Chain(pool, pool_c)
            pool.memset(ident[:, :], 0.0)
            pool.memset(ones[:, :], 1.0)
            pool.memset(tri[:, :, :], 1.0)
            pool.memset(lvl[:, :, :, :], 0.0)
            pool.memset(rst[:, :, :], 1.0)
            pool.memset(cond[:, :, :], 0.0)
            g.do(pool.memset(raw[:, :, :], 0.0))
            pool.affine_select(out=ident[:, :], in_=ident[:, :], compare_op=ALU.not_equal, fill=1.0, base=0,
                               pattern=[[-1, P]], channel_multiplier=1)
            for i, (step, cm, base) in enumerate([(1, -1, -1), (1, -1, 0), (-1, 1, -1), (-1, 1, 0)]):
                ins = pool.affine_select(out=tri[:, i, :], in_=tri[:, i, :], compare_op=ALU.is_ge, fill=0.0, base=base,
                                   pattern=[[step, P]], channel_multiplier=cm)
            g.did(ins)
            pool.memset(rst[:, 0, :].rearrange("p (j t) -> p j t", j=NTILE)[:, :, 0:1], 0.0)
            pool.memset(rst[:, 1, :].rearrange("p (j t) -> p j t", j=NTILE)[:, :, P - 1:P], 0.0)
            g.wait()
            pool.tensor_scalar(trin[:, :, :], tri[:, :, :], -1.0, None, ALU.mult).then_inc(const_ready, 1)
            for l in range(7):
                b = 1 << l
                for up in range(2):
                    v = lvl[:, l, up, :].rearrange("p (n h b) -> p n h b", h=2, b=b)[:, :, up, :]
                    g.do(pool.memset(v, 1.0))
                    lo = 0 if up else -b
                    g.do(pool.affine_select(out=v, in_=v, compare_op=ALU.is_ge, fill=0.0, base=lo,
                                            pattern=[[-2 * b, P // (2 * b)], [0, b]], channel_multiplier=1))
                    g.do(pool.affine_select(out=v, in_=v, compare_op=ALU.is_ge, fill=0.0, base=-lo + b - 1,
                                            pattern=[[2 * b, P // (2 * b)], [0, b]], channel_multiplier=-1))
            pool.nop().then_inc(masks_ready, 1)
            pool.wait_ge(vec_t, 1)
            pool.memset(zrow[:, :], 0.0).then_inc(zero_z, 1)
            pool.wait_ge(la_ready, 1)
            pool.wait_ge(proj, XBC + 6 + RT)
            with pool.Fori(0, NTILE) as j:
                for i in range(4):
                    pool.wait_ge(seg_ps, j * 4 + (i + 1))
                    for d in range(2):
                        h0 = 16 * d + 4 * i
                        ins = pool.tensor_tensor(
                            lam[:, i % 2, 4 * d:4 * d + 4, :],
                            tri[:, 2 - 2 * d, :].unsqueeze(1).to_broadcast([P, 4, P]),
                            la[:, ds(j, 1), h0:h0 + 4].rearrange("p a h -> p (a h)").unsqueeze(2).to_broadcast([P, 4, P]),
                            ALU.mult)
                    ins.then_inc(lam_ok, 1)

            pool.wait_ge(off_ps, 8)
            pool.wait_ge(cst_out, 2)
            pool.wait_ge(seg_ps, 14)
            pool.sem_inc(idle_pool, 1)
            pool.tensor_copy(v_c, um_a[:, 16, :]).then_inc(v_ok, 1)

            def identities(c):
                for s in range(3):
                    pool.wait_ge(u_ps, c * 3 + (s + 1))
                    pool.sem_inc(idle_pool, 1)
                    pool.tensor_copy(xinvT[s].rearrange("p a b q -> p (a b) q"),
                                     ident[:, :].unsqueeze(1).to_broadcast([P, 4, P])).then_inc(i4_ok, 1)

            with pool.Fori(0, 7) as c:
                identities(c)
                pool.wait_ge(aux_dve, c * 2 + 2)
                pool.sem_inc(idle_pool, 1)
                pool.tensor_copy(v_c, um_a[:, ds(c + 17, 1), :].rearrange("p a t -> p (a t)")).then_inc(v_ok, 1)
            identities(7)

            pool.wait_ge(out_done, 16 * 4)
            pool.iota(tokid, pattern=[[P, NTILE]], base=0, channel_multiplier=1, allow_small_or_imprecise_dtypes=True)
            pool.iota(erow, pattern=[[1, 32]], base=0, channel_multiplier=0, allow_small_or_imprecise_dtypes=True)
            pool.iota(down[:, 0:4], pattern=[[-1, 4]], base=4, channel_multiplier=0, allow_small_or_imprecise_dtypes=True)
            pool.iota(down[:, 4:36], pattern=[[-1, 32]], base=32, channel_multiplier=0,
                      allow_small_or_imprecise_dtypes=True).then_inc(rconst, 1)
            pool.wait_ge(rconst, 1)
            pool.wait_ge(zero_ok, 32)
            pool.wait_ge(slots_ok, 1)
            for i in range(6):
                pool.indirect_dma_start(out=slot_dram, out_offset=bass.IndirectOffsetOnAxis(ap=slots_i[:, i:i + 1], axis=0),
                                        in_=tokid[:, i % 3:i % 3 + 1], in_offset=None).then_inc(scat, 16)
            pool.wait_ge(h2_out, 16)
            pool.wait_ge(idx_ok, 1)
            for n in range(2):
                gather(pool, n, n)
            n_turns = turns(pool)
            with pool.Fori(1, n_turns) as i:
                for b in range(2):
                    gather(pool, i * 2 + b, b)
            for b in range(2):
                pool.wait_ge(yst[b], n_turns * 16)
            pool.sem_inc(idle_pool, 1)
            for j in range(NTILE):
                if j == 2:
                    pool.wait_ge(moe_ok, 1)
                for k in range(2):
                    pool.indirect_dma_start(out=cmb[:, j % 2, k, :], out_offset=None, in_=y_dram,
                                            in_offset=bass.IndirectOffsetOnAxis(ap=slots_i[:, 3 * k + j:3 * k + j + 1], axis=0)
                                            ).then_inc(comb[j % 2], 16)

        @block.tensor
        def _(pe):
            pe.wait_ge(const_ready, 1)
            pe.wait_ge(s_small, 16 * N_SMALL)
            pe.transpose(ps[:, 0, 0:16], crows[:, :], ident[0:16, 0:16])
            pe.transpose(ps[:, 1, 0:P], vrows[:, 0, :], ident[:, :])
            pe.transpose(ps[:, 2, 0:V1N], vrows[0:V1N, 1, :], ident[0:V1N, 0:V1N]).then_inc(vec_t, 1)

            def ada_block(n, i):
                block_ready(pe, n)
                if i >= 2:
                    pe.wait_ge(ada_sb, i - 1)
                for k2 in range(2):
                    for q in range(4):
                        mm = pe.matmul(ps[32 * q:32 * q + 32, 4 + i % 2, :], cond[:, 2 * q + k2, :],
                                       slot(n)[:, 2 * q + k2, :], start=(k2 == 0), stop=(k2 == 1),
                                       tile_position=(0, 32 * q), skip_group_check=True)
                mm.then_inc(ada_ps, 1)

            def ada_columns(i):
                pe.wait_ge(ada_sb, i + 1)
                for c in range(4):
                    o = 8 * i + 2 * c
                    mm = pe.matmul(ps[:, 6, o:o + 2], adas[:, i % 2, P * c:P * c + P], sel32[:, 0:2],
                                   start=True, stop=True)
                mm.then_inc(ada_cols, 1)

            pe.wait_ge(cond_ready, 1)
            for i in range(4):
                ada_block(ADA_A + i, i)
                if i:
                    ada_columns(i - 1)
            ada_columns(3)

            pe.wait_ge(xn_ready, 1)
            for k in range(KT):
                if k >= 4:
                    pe.wait_ge(hT_ready, k - 3)
                for j in range(NTILE):
                    mm = pe.transpose(ps[:, k % 4, P * j:P * j + P], xt[:, j, P * k:P * k + P], ident[:, :])
                mm.then_inc(xT_ps, 1)

            def project(n, c, t):
                for k in range(KT):
                    mm = pe.matmul(ps[:, t % 4 if isinstance(t, int) else t, 0:T],
                                   slot(n)[:, k, P * c:P * c + P], hT[:, k, :],
                                   start=(k == 0), stop=(k == KT - 1))
                return mm

            def conv_transpose(t):
                pe.wait_ge(conv_out, t + 1)
                if t >= 2:
                    pe.wait_ge(conv_tm, t - 1)
                src = bct[:, t - 8, :] if t >= 8 else acc[:, t % 2, :]
                for j in range(NTILE):
                    if t >= 8:
                        v = src[:, P * j:P * j + P]
                    else:
                        v = src[:, P * j + (2 if j else 0):P * j + (2 if j else 0) + P]
                    mm = pe.transpose(ps[:, 4 + t % 2, P * j:P * j + P], v, ident[:, :])
                mm.then_inc(conv_T, 1)

            pe.wait_ge(hT_ready, KT)
            for t in range(XBC):
                if t % 4 == 0:
                    block_ready(pe, XB + t // 4)
                if t >= 4:
                    pe.wait_ge(proj_read, t - 3)
                mm = project(XB + t // 4, t % 4, t)
                mm.then_inc(proj, 1)
                if 2 <= t < 12:
                    conv_transpose(t - 2)
            for i in range(6):
                n, j = Z + i // 3, i % 3
                if j == 0:
                    block_ready(pe, n)
                pe.wait_ge(proj_read, XBC - 3 + i)
                for k in range(KT):
                    mm = pe.matmul(ps[:, i % 4, :], hT[:, k, P * j:P * j + P], slot(n)[:, k, :],
                                   start=(k == 0), stop=(k == KT - 1))
                mm.then_inc(proj, 1)
            pe.wait_ge(s_wdt, 16)
            for j in range(NTILE):
                for k in range(KT):
                    mm = pe.matmul(ps[:, 7, 32 * j:32 * j + 32], hT[:, k, P * j:P * j + P], wdt[:, k, :],
                                   start=(k == 0), stop=(k == KT - 1))
            mm.then_inc(dt_ps, 1)
            with pe.Fori(0, 2) as r:
                for n in range(RING):
                    pe.wait_ge(w_in_slot[n], 64 + 16 * r)
                    for c in range(4):
                        pe.wait_ge(proj_read, r * 12 + (XBC + 6 + 4 * n + c - 3))
                        mm = project(R + n, c, (XBC + 6 + 4 * n + c) % 4)
                        mm.then_inc(proj, 1)
            block_ready(pe, R + 6)
            for c in range(3):
                pe.wait_ge(proj_read, XBC + 6 + 24 + c - 3)
                mm = project(R + 6, c, XBC + 6 + 24 + c)
                mm.then_inc(proj, 1)

            pe.wait_ge(proj_read, XBC + 6 + RT)
            pe.wait_ge(conv_tm, 10)
            for i in range(4, 8):
                ada_block(ADA_B + i - 4, i)
                if i > 4:
                    ada_columns(i - 1)
            ada_columns(7)

            pe.sem_inc(seg_ps, 2)
            pe.sem_inc(y_ps, 2)
            pe.wait_ge(la_ready, 1)
            for i, (m, lo) in enumerate(((1, 0), (3, 16), (2, 0), (0, 16))):
                pe.matmul(ps[:, 7, 48 * i:48 * i + 48], tri[:, m, :], la[:, :, lo:lo + 16], start=True, stop=True)
            pe.matmul(ps[:, 7, 192:288], ones[:, :], la[:, :, :], start=True, stop=True).then_inc(cs_ps, 1)
            for i in range(6):
                j, grp = i // 2, i % 2
                mm = pe.matmul(ps[:, 4 + i // 4, P * (i % 4):P * (i % 4) + P], bct[:, grp, P * j:P * j + P],
                               bct[:, 2 + grp, P * j:P * j + P], start=True, stop=True)
            mm.then_inc(score_ps, 1)
            pe.wait_ge(st_loaded, 32)
            for d in range(2):
                for i in range(8):
                    mm = pe.transpose(ps[:, 2 * d + i // 4, P * (i % 4):P * (i % 4) + P], st_in[:, d, i, :], ident[:, :])
            mm.then_inc(st_T, 1)
            for job in range(4):
                d, j = job % 2, (0, 0, 1, 2)[job]
                pe.wait_ge(xdw_ok, job + 1)
                if job == 0:
                    pe.wait_ge(st0_ok, 1)
                if job >= 2:
                    pe.wait_ge(cst_out, job - 1)
                b = 2 * d
                if job < 2:
                    for i in range(8):
                        grp = i // 4
                        mm = pe.matmul(ps[:, b + i // 4, P * (i % 4):P * (i % 4) + P], xdw[:, job % 2, P * i:P * i + P],
                                       btm[:, j, P * grp:P * grp + P], start=True, stop=True)
                else:
                    for grp in range(2):
                        mm = pe.matmul(ps[:, b + grp, :], btm[:, j, P * grp:P * grp + P],
                                       xdw[:, job % 2, BLK * grp:BLK * grp + BLK], start=True, stop=True)
                mm.then_inc(cst_ps, 1)
            pe.wait_ge(st1_ok, 1)
            pe.wait_ge(score_ok, 1)

            def seg_sums(j, i):
                pe.wait_ge(lam_ok, j * 4 + (i + 1))
                pe.wait_ge(seg_exp, j * 4 + (i + 1))
                for d in range(2):
                    for h in range(4):
                        mm = pe.matmul(ps[:, 2 * (i % 2) + d, P * h:P * h + P], lam[:, i % 2, 4 * d + h, :],
                                       tri[:, 1 + 2 * d, :], start=True, stop=True)
                mm.then_inc(seg_ps, 1)

            def y_heads(j, i):
                pe.wait_ge(g_ok, j * 4 + (i + 1))
                if i % 2 == 0:
                    pe.wait_ge(y_sb, j * 2 + (i // 2 + 1))
                for h in range(4):
                    o = 64 * (4 * (i % 2) + h)
                    for d in range(2):
                        mm = pe.matmul(ps[:, 4 + i // 2, o:o + 64], seg[:, i % 2, 4 * d + h, :],
                                       xs[:, ds(j, 1), 64 * (4 * i + h):64 * (4 * i + h) + 64].rearrange("p a c -> p (a c)"),
                                       start=(d == 0), stop=(d == 1))
                mm.then_inc(y_ps, 1)

            with pe.Fori(0, NTILE) as j:
                seg_sums(j, 0)
                for i in range(1, 4):
                    seg_sums(j, i)
                    y_heads(j, i - 1)
                y_heads(j, 3)

            pe.wait_ge(seg_exp, 12 + 2)
            for o, (j, d, src) in enumerate(OFF):
                pe_src = (st0, st1)[src]
                for grp in range(2):
                    i = 2 * o + grp
                    if i >= 4:
                        pe.wait_ge(off_rd, i - 3)
                    pe.matmul(ps[:, i % 4, :], bct[:, 2 + grp, P * j:P * j + P], pe_src[:, d, BLK * grp:BLK * grp + BLK],
                              start=True, stop=True).then_inc(off_ps, 1)
            pe.wait_ge(ynorm, 1)
            for t in range(8):
                if t >= 2:
                    pe.wait_ge(yT_sb, t - 1)
                for j in range(NTILE):
                    mm = pe.transpose(ps[:, 6 + t % 2, P * j:P * j + P], xs[:, j, P * t:P * t + P], ident[:, :])
                mm.then_inc(yT_ps, 1)

            pe.wait_ge(yT_sb, 8)
            pe.wait_ge(wkv_loaded, 32)
            for d in range(2):
                for i in range(8):
                    mm = pe.transpose(ps[:, 6 + d, 64 * i:64 * i + 64], wkv_in[:, d, P * i:P * i + P], ident[0:64, 0:64])
            mm.then_inc(wkv_T, 1)
            pe.wait_ge(wkv_ok, 1)
            pe.wait_ge(wd_ok, 1)
            pe.sem_inc(u_ps, 3)
            pe.sem_inc(aux_ps, 2)
            for n in range(KSQ, BONUS + 1):
                prep_pe(pe, -1, n)
            pe.wait_ge(aux_act, 10)
            pe.wait_ge(aux_dve, 2)
            pe.sem_inc(aux_ps, 2)
            round_pe(pe, 0, 0, False, True)
            with pe.Fori(0, 3) as i:
                round_pe(pe, i * 2 + 1, 1, True, True)
                round_pe(pe, i * 2 + 2, 0, True, True)
            round_pe(pe, 7, 1, True, False)
            tail_pe(pe, 7, 2, 7)
            tail_pe(pe, 7, 3, 7)
            pe.wait_ge(pair_ok, 9)
            for d in range(2):
                for i in range(8):
                    mm = pe.transpose(ps[0:64, 2 * d + i // 4, P * (i % 4):P * (i % 4) + P], sall[:, i, d, :], ident[:, :])
                mm.then_inc(fin_T, 1)

            for i in range(4):
                ada_block(GATES + i, 8 + i)
                if i:
                    gate_rows(pe, i - 1)
            gate_rows(pe, 3)

            pe.wait_ge(fin_sb, 2)
            pe.wait_ge(gate_ok, 8)
            for q in range(4):
                block_ready(pe, WOUT + q)
                w = wout_block(WOUT + q)
                for k in range(4):
                    kk_ = 4 * q + k
                    src = mixm[:, kk_, :] if kk_ < 8 else um_a[:, kk_ - 8, :]
                    for j in range(NTILE):
                        for c in range(2):
                            mm = pe.matmul(ps[:, 2 * j + c, :], src[:, P * j:P * j + P], w[:, k, BLK * c:BLK * c + BLK],
                                           start=(kk_ == 0), stop=(kk_ == 15))
                mm.then_inc(out_ps, 1)
            pe.wait_ge(xn2_ok, 1)
            for k in range(KT):
                if k >= 2:
                    pe.wait_ge(h2T_ok, k - 1)
                for j in range(NTILE):
                    mm = pe.transpose(ps[:, 6 + k % 2, P * j:P * j + P], h2[:, j, P * k:P * k + P], ident[:, :])
                mm.then_inc(h2T_ps, 1)
            pe.wait_ge(h2T_ok, 8)
            pe.wait_ge(late_in, 16 * 5)
            for j in range(NTILE):
                for k in range(KT):
                    mm = pe.matmul(ps[:, 6, 36 * j:36 * j + 36], hT[:, k, P * j:P * j + P], wr[:, k, :],
                                   start=(k == 0), stop=(k == KT - 1))
            mm.then_inc(lg_ps, 1)
            for j in range(NTILE):
                for k in range(KT):
                    mm = pe.transpose(ps[:, 2 * j + k // 4, P * (k % 4):P * (k % 4) + P], hT[:, k, P * j:P * j + P], ident[:, :])
                mm.then_inc(h2_ps, 1)
            pe.wait_ge(a_ok, 1)
            for j in range(NTILE):
                for i in range(j + 1):
                    mm = pe.matmul(ps[:, 7, 32 * j:32 * j + 32], tri[:, 0, :] if i == j else ones[:, :], both_oh[:, i, :],
                                   start=(i == 0), stop=(i == j))
            for i in range(NTILE):
                mm = pe.matmul(ps[:, 7, 96:128], ones[:, :], both_oh[:, i, :], start=(i == 0), stop=(i == 2))
            mm.then_inc(rank_ps, 1)
            pe.wait_ge(rows_in, 16)
            pe.wait_ge(h2_ok, 3)
            pe.transpose(ps[:, 6, 0:N_GROUPS], rowsT, ident[0:N_GROUPS, 0:N_GROUPS]).then_inc(rows_ps, 1)

            def pe_group(i, b, first=False, last=False):
                n = i * 2 + b
                pe.wait_ge(gu_in[b], i * (16 * GU_LOADS[b]) + 16 * GU_LOADS[b])
                gate_up(pe, n, b)
                if not first:
                    pe.wait_ge(dn_in[1 - b], i * (16 * DN_LOADS) + 16 * DN_LOADS * b)
                    down_proj(pe, n - 1, 1 - b)
                if not last:
                    pe.wait_ge(xg_in[1 - b], i * 16 + (32 if b else 16))
                    rows_T(pe, n + 1, 1 - b)

            pe.wait_ge(xg_in[0], 16)
            rows_T(pe, 0, 0)
            for b in range(2):
                pe_group(0, b, first=(b == 0))
            n_turns = turns(pe)
            with pe.Fori(1, n_turns - 1) as i:
                for b in range(2):
                    pe_group(i, b)
            for b in range(2):
                pe_group(n_turns - 1, b, last=(b == 1))
            pe.wait_ge(dn_in[1], n_turns * (16 * DN_LOADS))
            down_proj(pe, n_turns * 2 - 1, 1)

        @block.scalar
        def _(act):
            g = Chain(act, act_c)
            act.wait_ge(s_x, 32)
            act.wait_ge(const_ready, 1)
            for j in range(NTILE):
                g.did(act.activation(zs[:, j, :], xt[:, j, :], ACT.Square, accum_out=stat[:, j:j + 1]))
            act.wait_ge(meansq, 1)
            act.activation(stat[:, 12:15], stat[:, 4:7], ACT.Sqrt).then_inc(rstd, 1)
            act.wait_ge(vec_t, 1)
            act.activation(cond[:, :, 0:2], ps[:, 0, 0:16].rearrange("p (v k) -> p k v", v=2),
                           ACT.Silu).then_inc(cond_ready, 1)
            for i in range(4):
                act.wait_ge(ada_ps, i + 1)
                if i >= 2:
                    act.wait_ge(ada_cols, i - 1)
                ins = act.activation(adas[:, i % 2, :], ps[:, 4 + i % 2, :], ACT.Copy)
                ins.then_inc(ada_sb, 1)
            def conv_in(t):
                act.wait_ge(proj, t + 1)
                if t >= 2:
                    act.wait_ge(conv_acc, t - 1)
                act.activation(raw[:, t % 2, 2:2 + P], ps[:, t % 4, 0:P], ACT.Copy)
                ins = act.activation(raw[:, t % 2, 4 + P:4 + T], ps[:, t % 4, P:T], ACT.Copy)
                ins.then_inc(proj_read, 1)

            def conv_silu(t):
                act.wait_ge(conv_acc, t + 1)
                bias = pv0[:, V0["conv_b"] + t:V0["conv_b"] + t + 1]
                for o, i, n in ((0, 0, P), (P, P + 2, T - P)):
                    src = acc[:, t % 2, i:i + n]
                    dst = bct[:, t - 8, o:o + n] if t >= 8 else src
                    ins = act.activation(dst, src, ACT.Silu, bias=bias)
                ins.then_inc(conv_out, 1)

            for t in range(XBC):
                conv_in(t)
                if t:
                    conv_silu(t - 1)
            conv_silu(XBC - 1)
            for i in range(6):
                act.wait_ge(proj, XBC + i + 1)
                n, j = i // 3, i % 3
                ins = act.activation(zs[:, j, BLK * n:BLK * n + BLK], ps[:, i % 4, :], ACT.Silu)
                ins.then_inc(proj_read, 1)
            act.wait_ge(vec_ready, 1)
            with act.Fori(0, 6) as r:
                for c in range(4):
                    t = r * 4 + c
                    act.wait_ge(proj, r * 4 + (XBC + 6 + c + 1))
                    act.activation(um_a[:, ds(t, 1), :], ps[:, (XBC + 6 + c) % 4, 0:T], ACT.Copy,
                                   scale=mum[:, 0, ds(t, 1)]).then_inc(mix0, 1)
            for t in range(24, RT):
                act.wait_ge(proj, XBC + 6 + t + 1)
                act.activation(um_a[:, t, :], ps[:, (XBC + 6 + t) % 4, 0:T], ACT.Copy,
                               scale=mum[:, 0, t:t + 1]).then_inc(mix0, 1)

            act.wait_ge(dt_in, 1)
            act.activation(drow[:, 32:64], drow[:, 32:64], ACT.Exp)
            act.activation(dtmp[:, :, :], dtmp[:, :, :], ACT.Exp).then_inc(act_m, 1)
            act.wait_ge(act_m, 1)
            act.activation(dtl[:, :, :], dtmp[:, :, :], ACT.Ln, bias=1.0).then_inc(dt_ln, 1)

            for i in range(4, 8):
                act.wait_ge(ada_ps, i + 1)
                act.wait_ge(ada_cols, i - 1)
                act.activation(adas[:, i % 2, :], ps[:, 4 + i % 2, :], ACT.Copy).then_inc(ada_sb, 1)

            act.sem_inc(seg_exp, 2)
            act.wait_ge(cs_ps, 1)
            act.activation(ecs[:, :], ps[:, 7, 0:288], ACT.Exp).then_inc(cs_exp, 1)
            act.wait_ge(st_T, 1)
            for d in range(2):
                ins = act.activation(st0[:, d, :].rearrange("p (b c) -> p b c", b=2), ps[:, 2 * d:2 * d + 2, :], ACT.Copy)
            ins.then_inc(st0_ok, 1)
            for d in range(2):
                act.wait_ge(cst_ps, d + 1)
                act.activation(st_out[:, d, :, :].rearrange("p (b i) n -> p b (i n)", b=2), ps[:, 2 * d:2 * d + 2, :],
                               ACT.Copy).then_inc(cst_out, 1)
            act.wait_ge(xn_ready, 1)
            with act.Fori(0, NTILE) as j:
                for i in range(4):
                    act.wait_ge(seg_ps, j * 4 + (i + 3))
                    act.wait_ge(y_ps, j * 4 + (i + 1))
                    act.activation(seg[:, i % 2, :, :].rearrange("p (d h) q -> p d (h q)", d=2),
                                   ps[:, 2 * (i % 2):2 * (i % 2) + 2, :], ACT.Exp).then_inc(seg_exp, 1)
            for j in range(NTILE):
                act.wait_ge(gated, j + 1)
                for grp in range(2):
                    ins = act.activation(sq[:, :], xs[:, j, BLK * grp:BLK * grp + BLK], ACT.Square,
                                         accum_out=mstat[:, 2 * j + grp:2 * j + grp + 1])
                    ins.then_inc(ysq, 1)
                    act.wait_ge(ysq, 2 * j + grp + 1)
            act.wait_ge(meansq, 2)
            act.activation(mstat[:, 12:18], mstat[:, 6:12], ACT.Sqrt).then_inc(rstd, 1)

            act.activation(um_a[:, 24, :], um_a[:, 24, :], ACT.Tanh)
            act.activation(um_a[:, 26, :], um_a[:, 26, :], ACT.Sigmoid).then_inc(wd_ok, 1)
            act.wait_ge(wkv_T, 1)
            for d in range(2):
                ins = act.activation(r0all[:, :, d, :], ps[:, 6 + d, :].rearrange("p (i v) -> p i v", v=64), ACT.Copy)
            ins.then_inc(wkv_ok, 1)
            act.wait_ge(yT_sb, 8)
            act.sem_inc(aux_act, 1)
            for n in range(KSQ, G_UP + 1):
                prep_act(act, -1, 0, n)
            exps_act(act, -1, 0)
            prep_act(act, -1, 0, BE_T)
            prep_act(act, -1, 0, KAP_T)
            act.wait_ge(aux_ps, 14)
            act.sem_inc(aux_act, 1)
            round_act(act, 0, 0, False, True)
            with act.Fori(0, 3) as i:
                round_act(act, i * 2 + 1, 1, True, True)
                round_act(act, i * 2 + 2, 0, True, True)
            round_act(act, 7, 1, True, False)
            tail_act(act, 7, 3)
            for d in range(2):
                act.wait_ge(fin_T, d + 1)
                act.activation(wkv_in[:, d, :].rearrange("p (b c) -> p b c", b=2), ps[0:64, 2 * d:2 * d + 2, :],
                               ACT.Copy).then_inc(fin_sb, 1)
            for i in range(4):
                act.wait_ge(ada_ps, 8 + i + 1)
                if i >= 2:
                    act.wait_ge(gate_ps, 2 * i - 2)
                act.activation(adas[:, i % 2, :], ps[:, 4 + i % 2, :], ACT.Copy).then_inc(ada_sb, 1)
                for v in range(2):
                    act.wait_ge(gate_ps, 2 * i + v + 1)
                    dst = (g1, g2)[i // 2][:, v, BLK * (i % 2):BLK * (i % 2) + BLK]
                    act.activation(dst, ps[:, 6 + v, :], ACT.Copy).then_inc(gate_ok, 1)
            act.wait_ge(x1_ok, 3)
            for j in range(NTILE):
                act.activation(h2sq, x1[:, j, :], ACT.Square, accum_out=fst[:, j:j + 1]).then_inc(sq2_ok, 1)
                act.wait_ge(sq2_ok, j + 1)
            act.wait_ge(meansq, 3)
            act.activation(fst[:, 6:9], fst[:, 3:6], ACT.Sqrt).then_inc(rstd, 1)
            for j in range(NTILE):
                act.wait_ge(h2_ps, j + 1)
                act.activation(h2[:, j, :].rearrange("p (b c) -> p b c", b=2), ps[:, 2 * j:2 * j + 2, :],
                               ACT.Copy).then_inc(h2_ok, 1)
            act.wait_ge(rt_dve, 1)
            act.activation(grp2, grp2, ACT.Exp).then_inc(rt_act, 1)
            act.wait_ge(rt_dve, 2)
            act.activation(s3[:, 5, :], s3[:, 4, :], ACT.Exp).then_inc(rt_act, 1)
            for n in range(2):
                silu_gate(act, n, n)
                if n:
                    expert_out(act, n - 1, 1 - n)
            silu_gate(act, 2, 0)
            expert_out(act, 1, 1)
            n_turns = turns(act)
            with act.Fori(1, n_turns - 1) as i:
                silu_gate(act, i * 2 + 1, 1)
                expert_out(act, i * 2, 0)
                silu_gate(act, i * 2 + 2, 0)
                expert_out(act, i * 2 + 1, 1)
            silu_gate(act, n_turns * 2 - 1, 1)
            expert_out(act, n_turns * 2 - 2, 0)
            expert_out(act, n_turns * 2 - 1, 1)
            for j in range(NTILE):
                act.wait_ge(x1_ok, j + 4)
                act.activation(h2[:, j, :], x1[:, j, :], ACT.Square, accum_out=fst[:, j:j + 1]).then_inc(sq2_ok, 1)
            act.wait_ge(meansq, 4)
            act.activation(fst[:, 6:9], fst[:, 3:6], ACT.Sqrt).then_inc(rstd, 1)

        @block.vector
        def _(dve):
            g = Chain(dve, dve_c)
            dve.memset(eps_gn[:, :], 64e-5)
            g.do(dve.memset(bones[:, :], 0.0))
            dve.memset(bones[0:64, 0:64], 1.0)
            dve.memset(bones[64:P, 64:P], 1.0)
            dve.wait_ge(const_ready, 1)
            dve.tensor_reduce(sel32[:, :], ident[:, :].rearrange("p (q v) -> p v q", v=32), AX.X, ALU.add)
            g.do(dve.tensor_reduce(par[:, 0:4], ident[:, :].rearrange("p (q v) -> p v q", v=4), AX.X, ALU.add))
            dve.tensor_copy(selb[:, :, :], sel32[:, 0:2].unsqueeze(2).to_broadcast([P, 2, P]))
            dve.tensor_tensor(par[:, 4:6], par[:, 0:2], par[:, 2:4], ALU.add)
            dve.wait_ge(vec_t, 1)
            dve.tensor_copy(pv0[:, :], ps[:, 1, 0:P])
            g.do(dve.tensor_copy(pv1[:, 0:V1N], ps[:, 2, 0:V1N]))
            mu = pv1[:, 0:RT]
            dve.tensor_scalar(mum[:, 0, :], mu, -1.0, 1.0, ALU.mult, ALU.add)
            for i in range(6):
                dve.tensor_scalar(mum[:, 1 + i, :], mu, par[:, i:i + 1], None, ALU.mult)
            dve.tensor_scalar(kam[:, :], pv1[:, V1["k_a"]:V1["k_a"] + 8], -1.0, 1.0, ALU.mult,
                              ALU.add).then_inc(vec_ready, 1)
            dve.wait_ge(act_c, 3)
            dve.tensor_scalar(stat[:, 4:7], stat[:, 0:3], 1.0 / D, 1e-6, ALU.mult, ALU.add).then_inc(meansq, 1)
            dve.wait_ge(rstd, 1)
            g.do(dve.reciprocal(stat[:, 8:11], stat[:, 12:15]))
            for j in range(NTILE):
                ins = dve.tensor_scalar(xt[:, j, :], xt[:, j, :], stat[:, 8 + j:9 + j], None, ALU.mult)
            ins.then_inc(xn_ready, 1)
            dve.wait_ge(ada_cols, 4)
            g.do(dve.tensor_tensor(mod[:, 0:16, :], ps[:, 6, 0:32].rearrange("p (t v) -> p t v", v=2),
                                   pv0[:, 0:16].unsqueeze(2).to_broadcast([P, 16, 2]), ALU.add))
            g.do(dve.tensor_scalar(aff1[:, :, :], mod[:, 8:16, :], 1.0, None, ALU.add))
            g.do(dve.tensor_tensor(aff1[:, :, :], aff1[:, :, :],
                                   pv0[:, V0["norm1"]:V0["norm1"] + 8].unsqueeze(2).to_broadcast([P, 8, 2]), ALU.mult))
            for k in range(KT):
                dve.wait_ge(xT_ps, k + 1)
                for v, (lo, hi) in enumerate(((0, P), (P, T))):
                    ins = dve.tensor_scalar(hT[:, k, lo:hi], ps[:, k % 4, lo:hi], aff1[:, k, v:v + 1],
                                            mod[:, k, v:v + 1], ALU.mult, ALU.add)
                ins.then_inc(hT_ready, 1)
            W = T + 2

            def taps(t):
                dve.wait_ge(proj_read, t + 1)
                if t >= 2 and t < 10:
                    dve.wait_ge(conv_T, t - 1)
                elif t >= 10:
                    dve.wait_ge(conv_out, t - 1)
                for j in range(5):
                    w = pv0[:, V0["conv_w"] + 12 * j + t:V0["conv_w"] + 12 * j + t + 1]
                    src = raw[:, t % 2, j:j + W]
                    if j == 0:
                        ins = dve.tensor_scalar(acc[:, t % 2, 0:W], src, w, None, ALU.mult)
                    else:
                        ins = dve.scalar_tensor_tensor(acc[:, t % 2, 0:W], src, w, acc[:, t % 2, 0:W],
                                                       ALU.mult, ALU.add)
                    if j < 4:
                        g.do(ins)
                ins.then_inc(conv_acc, 1)

            def token_major(t):
                if t >= 10:
                    return
                dve.wait_ge(conv_T, t + 1)
                dst = xs[:, :, P * t:P * t + P] if t < 8 else btm[:, :, P * (t - 8):P * (t - 8) + P]
                dve.tensor_copy(dst, ps[:, 4 + t % 2, 0:T].rearrange("p (j c) -> p j c", j=NTILE)).then_inc(conv_tm, 1)

            for t in range(XBC):
                taps(t)
                if t >= 3:
                    token_major(t - 3)
            token_major(9)

            def mix(c, t, mus, step):
                u = ps[:, c, 0:T]
                o = um_a[:, t, :] if isinstance(t, int) else um_a[:, ds(t, 1), :].rearrange("p a t -> p (a t)")
                ug = u[:, P:T].rearrange("p (r w) -> p r w", w=GRID)
                og = o[:, P:T].rearrange("p (r w) -> p r w", w=GRID)
                parts = [(o[:, 1:P], u[:, 0:P - 1], 5), (o[:, 0:P - 1], u[:, 1:P], 6),
                         (og[:, :, 1:], ug[:, :, :-1], 1), (og[:, :, :-1], ug[:, :, 1:], 2),
                         (o[:, P + GRID:T], u[:, P:T - GRID], 3), (o[:, P:T - GRID], u[:, P + GRID:T], 4)]
                for i, (dst, src, m) in enumerate(parts):
                    step(dve.scalar_tensor_tensor(dst, src, mus(m), dst, ALU.mult, ALU.add), i)

            with dve.Fori(0, 6) as r:
                lc = LoopChain(dve, dve_r, r, 20)
                for c in range(4):
                    t = r * 4 + c
                    dve.wait_ge(mix0, r * 4 + (c + 1))

                    def step(ins, i):
                        if i < 5:
                            lc.do(ins)
                        else:
                            ins.then_inc(proj_read, 1)
                    mix((XBC + 6 + c) % 4, t, lambda m: mum[:, m, ds(t, 1)], step)
                lc.end()
            for t in range(24, RT):
                dve.wait_ge(mix0, t + 1)

                def step(ins, i):
                    if i < 5:
                        g.do(ins)
                    else:
                        ins.then_inc(proj_read, 1)
                mix((XBC + 6 + t) % 4, t, lambda m: mum[:, m, t:t + 1], step)

            m = g
            dve.wait_ge(dt_ps, 1)
            m.do(dve.tensor_tensor(dt[:, :, :], ps[:, 7, 0:96].rearrange("p (j h) -> p j h", j=NTILE),
                                   drow[:, 0:32].unsqueeze(1).to_broadcast([P, NTILE, 32]), ALU.add))
            dve.scalar_tensor_tensor(dtmp[:, :, :], dt[:, :, :], -1.0, dt[:, :, :], ALU.mult,
                                     ALU.min).then_inc(dt_in, 1)
            dve.wait_ge(dt_ln, 1)
            m.do(dve.tensor_scalar(la[:, :, :], dtmp[:, :, :], 1.0, None, ALU.add))
            m.do(dve.reciprocal(dtr[:, :, :], la[:, :, :]))
            m.do(dve.tensor_scalar(la[:, :, :], la[:, :, :], 1.0, None, ALU.subtract))
            m.do(dve.tensor_tensor(dtmp[:, :, :], dtmp[:, :, :], la[:, :, :], ALU.subtract))
            m.do(dve.tensor_tensor(dtmp[:, :, :], dtmp[:, :, :], dtr[:, :, :], ALU.mult))
            m.do(dve.tensor_tensor(dtl[:, :, :], dtl[:, :, :], dtmp[:, :, :], ALU.add))
            m.do(dve.scalar_tensor_tensor(dt[:, :, :], dt[:, :, :], 0.0, dtl[:, :, :], ALU.max, ALU.add))
            dve.scalar_tensor_tensor(la[:, :, :], dt[:, :, :], -1.0,
                                     drow[:, 32:64].unsqueeze(1).to_broadcast([P, NTILE, 32]),
                                     ALU.mult, ALU.mult).then_inc(la_ready, 1)
            dve.wait_ge(ada_cols, 8)
            m.do(dve.tensor_tensor(mod[:, 16:32, :], ps[:, 6, 32:64].rearrange("p (t v) -> p t v", v=2),
                                   pv0[:, 24:40].unsqueeze(2).to_broadcast([P, 16, 2]), ALU.add))
            m.do(dve.tensor_scalar(aff2[:, :, :], mod[:, 24:32, :], 1.0, None, ALU.add))
            m.do(dve.tensor_tensor(aff2[:, :, :], aff2[:, :, :],
                                   pv1[:, V1["norm2"]:V1["norm2"] + 8].unsqueeze(2).to_broadcast([P, 8, 2]), ALU.mult))

            dve.sem_inc(y_sb, 2)
            dve.wait_ge(cs_exp, 1)
            for d in range(2):
                w = ecs[:, 96 + 48 * d:144 + 48 * d].rearrange("p (j h) -> p j h", j=NTILE)
                ins = dve.tensor_tensor(w, w, dt[:, :, 16 * d:16 * d + 16], ALU.mult)
            m.do(ins)
            dve.wait_ge(ada_ps, 8)
            dve.wait_ge(score_ps, 1)
            for d in range(2):
                for b, n in ((0, 4), (1, 2)):
                    ins = dve.tensor_tensor(msc[:, d, 4 * b:4 * b + n, :],
                                            ps[:, 4 + b, 0:P * n].rearrange("p (i q) -> p i q", i=n),
                                            tri[:, 1 + 2 * d, :].unsqueeze(1).to_broadcast([P, n, P]), ALU.mult)
            ins.then_inc(score_ok, 1)

            def heads(ap):
                return ap.rearrange("p (h c) -> p h c", c=PM)

            for job in range(4):
                d, j = job % 2, (0, 0, 1, 2)[job]
                if job >= 2:
                    dve.wait_ge(cst_ps, job - 1)
                w = ecs[:, 96 + 48 * d + 16 * j:96 + 48 * d + 16 * j + 16]
                dve.tensor_tensor(heads(xdw[:, job % 2, :]), heads(xs[:, j, :]),
                                  w.unsqueeze(2).to_broadcast([P, HM, PM]), ALU.mult).then_inc(xdw_ok, 1)
            dve.wait_ge(st0_ok, 1)
            for d in range(2):
                j = 1 + d
                dec = ecs[:, 192 + 32 * j + 16 * d:192 + 32 * j + 16 * d + 16]
                m.do(dve.tensor_tensor(heads(st1[:, d, :]), heads(st0[:, d, :]),
                                       dec.unsqueeze(2).to_broadcast([P, HM, PM]), ALU.mult))
                dve.wait_ge(cst_ps, 3 + d)
                st1v = st1[:, d, :].rearrange("p (b c) -> p b c", b=2)
                ins = dve.tensor_tensor(st1v, st1v, ps[:, 2 * d:2 * d + 2, :], ALU.add)
            ins.then_inc(st1_ok, 1)

            with dve.Fori(0, NTILE) as j:
                lc = LoopChain(dve, dve_l, j, 2)
                for i in range(4):
                    grp = i // 2
                    dve.wait_ge(seg_exp, j * 4 + (i + 3))
                    for d in range(2):
                        for h in range(4):
                            gb = seg[:, i % 2, 4 * d + h, :]
                            hh = 16 * d + 4 * i + h
                            ins = dve.scalar_tensor_tensor(
                                gb, gb, dt[:, ds(j, 1), hh:hh + 1].rearrange("p a b -> p (a b)"),
                                msc[:, d, ds(j * 2 + grp, 1), :].rearrange("p a q -> p (a q)"), ALU.mult, ALU.mult)
                    ins.then_inc(g_ok, 1)
                    if i % 2:
                        dve.wait_ge(y_ps, j * 4 + (i + 3))
                        xv = xs[:, ds(j, 1), BLK * grp:BLK * grp + BLK].rearrange("p a c -> p (a c)")
                        lc.do(dve.tensor_tensor(heads(xv), heads(xv),
                                                drow[:, 64 + 8 * grp:72 + 8 * grp].unsqueeze(2).to_broadcast([P, 8, PM]),
                                                ALU.mult))
                        ins = dve.tensor_tensor(xv, xv, ps[:, 4 + grp, :], ALU.add)
                        ins.then_inc(y_sb, 1)
                        dve.wait_ge(y_sb, j * 2 + (grp + 3))
                lc.end()

            for o, (j, d, _) in enumerate(OFF):
                for grp in range(2):
                    i = 2 * o + grp
                    dve.wait_ge(off_ps, i + 1)
                    f = ecs[:, 48 * d + 16 * j + 8 * grp:48 * d + 16 * j + 8 * grp + 8]
                    dve.tensor_tensor(heads(yoff[:, :]), heads(ps[:, i % 4, :]),
                                      f.unsqueeze(2).to_broadcast([P, 8, PM]), ALU.mult).then_inc(off_rd, 1)
                    dve.wait_ge(off_rd, i + 1)
                    xv = xs[:, j, BLK * grp:BLK * grp + BLK]
                    m.do(dve.tensor_tensor(xv, xv, yoff[:, :], ALU.add))
            for j in range(NTILE):
                dve.tensor_tensor(xs[:, j, :], xs[:, j, :], zs[:, j, :], ALU.mult).then_inc(gated, 1)
            dve.wait_ge(ysq, 6)
            dve.tensor_scalar(mstat[:, 6:12], mstat[:, 0:6], 1.0 / BLK, 1e-6, ALU.mult, ALU.add).then_inc(meansq, 1)
            dve.wait_ge(rstd, 2)
            m.do(dve.reciprocal(mstat[:, 18:24], mstat[:, 12:18]))
            for i in range(6):
                xv = xs[:, i // 2, BLK * (i % 2):BLK * (i % 2) + BLK]
                ins = dve.tensor_scalar(xv, xv, mstat[:, 18 + i:19 + i], None, ALU.mult)
            ins.then_inc(ynorm, 1)
            for t in range(8):
                dve.wait_ge(yT_ps, t + 1)
                c = V1["m_norm"] + t
                dve.tensor_scalar(mixm[:, t, :], ps[:, 6 + t % 2, 0:T], pv1[:, c:c + 1], None, ALU.mult).then_inc(yT_sb, 1)

            dve.sem_inc(aux_dve, 1)
            dve.sem_inc(yo_rd, 3)
            dve.sem_inc(pair_ok, 1)
            dve.wait_ge(wkv_ok, 1)
            pc = LoopChain(dve, dve_p, 0, 9)
            for part in range(7):
                prep_dve(dve, -1, 0, pc, part)
            dve.wait_ge(aux_ps, 14)
            dve.sem_inc(aux_dve, 1)
            round_dve(dve, 0, 0, False, True)
            with dve.Fori(0, 3) as i:
                round_dve(dve, i * 2 + 1, 1, True, True)
                round_dve(dve, i * 2 + 2, 0, True, True)
            round_dve(dve, 7, 1, True, False)
            tc = LoopChain(dve, dve_q, 7, 4)
            tail_dve(dve, 7, 2, 7, 1, tc, 0)
            tail_dve(dve, 7, 2, 7, 1, tc, 1)

            t = g
            dve.wait_ge(brow_in, 64)
            for i in range(4):
                dve.wait_ge(ada_sb, 9 + i)
                ab = adas[0:2, i % 2, :]
                dve.tensor_tensor(ab, ab, brow[:, BLK * i:BLK * i + BLK], ALU.add).then_inc(bias_ok, 1)
            dve.wait_ge(out_ps, 4)
            dve.wait_ge(x_again, 32)
            dve.wait_ge(gate_ok, 8)
            for j in range(NTILE):
                v = min(j, 1)
                t.do(dve.tensor_tensor(h2[:, j, :].rearrange("p (b c) -> p b c", b=2), ps[:, 2 * j:2 * j + 2, :],
                                       g1[:, v, :].rearrange("p (b c) -> p b c", b=2), ALU.mult))
                dve.tensor_tensor(x1[:, j, :], x1[:, j, :], h2[:, j, :], ALU.add).then_inc(x1_ok, 1)
            dve.wait_ge(sq2_ok, 3)
            dve.tensor_scalar(fst[:, 3:6], fst[:, 0:3], 1.0 / D, 1e-6, ALU.mult, ALU.add).then_inc(meansq, 1)
            dve.wait_ge(rstd, 3)
            t.do(dve.reciprocal(fst[:, 9:12], fst[:, 6:9]))
            for j in range(NTILE):
                ins = dve.tensor_scalar(h2[:, j, :], x1[:, j, :], fst[:, 9 + j:10 + j], None, ALU.mult)
            ins.then_inc(xn2_ok, 1)
            for k in range(KT):
                dve.wait_ge(h2T_ps, k + 1)
                for v, (lo, hi) in enumerate(((0, P), (P, T))):
                    ins = dve.tensor_scalar(hT[:, k, lo:hi], ps[:, 6 + k % 2, lo:hi], aff2[:, k, v:v + 1],
                                            mod[:, 16 + k, v:v + 1], ALU.mult, ALU.add)
                ins.then_inc(h2T_ok, 1)
            def cols(ap, n):
                return ap.unsqueeze(2).to_broadcast([P, NTILE, n])

            def row(ap, n):
                return ap.unsqueeze(1).to_broadcast([P, NTILE, n])

            def one_hot(dst, vals, top, places, n, scr):
                t.do(dve.tensor_tensor(scr, vals, cols(top, n), ALU.is_equal))
                t.do(dve.tensor_tensor(scr, scr, row(places, n), ALU.mult))
                t.do(dve.tensor_reduce(s3[:, 9, :], scr, AX.X, ALU.max))
                t.do(dve.tensor_tensor(dst, scr, cols(s3[:, 9, :], n), ALU.is_equal))

            dve.wait_ge(lg_ps, 1)
            dve.wait_ge(rconst, 1)
            t.do(dve.tensor_tensor(lg, ps[:, 6, 0:108].rearrange("p (j c) -> p j c", j=NTILE), row(brt, 36), ALU.add))
            gl, el = lg[:, :, 0:4], lg[:, :, 4:36]
            t.do(dve.tensor_reduce(s3[:, 0, :], gl, AX.X, ALU.max))
            dve.tensor_tensor(grp2, gl, cols(s3[:, 0, :], 4), ALU.subtract).then_inc(rt_dve, 1)
            one_hot(ghot, gl, s3[:, 0, :], down[:, 0:4], 4, ghot)
            g4 = [x.rearrange("p j (g e) -> p j g e", g=EG) for x in (msk, el, tmp)]
            gb8 = ghot.unsqueeze(3).to_broadcast([P, NTILE, EG, EPG])
            t.do(dve.tensor_tensor(g4[0], g4[1], gb8, ALU.mult))
            t.do(dve.tensor_scalar(ghot, ghot, 1e30, -1e30, ALU.mult, ALU.add))
            t.do(dve.tensor_tensor(g4[0], g4[0], gb8, ALU.add))
            t.do(dve.tensor_reduce(s3[:, 2, :], msk, AX.X, ALU.max))
            one_hot(oh[:, 0], msk, s3[:, 2, :], down[:, 4:36], 32, tmp)
            t.do(dve.scalar_tensor_tensor(msk, oh[:, 0], -3e30, msk, ALU.mult, ALU.add))
            t.do(dve.tensor_reduce(s3[:, 3, :], msk, AX.X, ALU.max))
            one_hot(oh[:, 1], msk, s3[:, 3, :], down[:, 4:36], 32, tmp)
            dve.tensor_tensor(both_oh, oh[:, 0], oh[:, 1], ALU.add).then_inc(a_ok, 1)
            dve.tensor_tensor(s3[:, 4, :], s3[:, 3, :], s3[:, 2, :], ALU.subtract).then_inc(rt_dve, 1)
            dve.wait_ge(rt_act, 1)
            t.do(dve.tensor_reduce(s3[:, 1, :], grp2, AX.X, ALU.add))
            dve.wait_ge(rt_act, 2)
            t.do(dve.tensor_scalar(s3[:, 6, :], s3[:, 5, :], 1.0, None, ALU.add))
            t.do(dve.tensor_tensor(s3[:, 6, :], s3[:, 6, :], s3[:, 1, :], ALU.mult))
            t.do(dve.reciprocal(wcol[:, 0, :], s3[:, 6, :]))
            t.do(dve.tensor_tensor(wcol[:, 1, :], wcol[:, 0, :], s3[:, 5, :], ALU.mult))
            dve.wait_ge(rank_ps, 1)
            n_e = ps[:, 7, 96:128]
            t.do(dve.tensor_scalar(cnt[:, 0, :], n_e, CH + 0.5, None, ALU.is_gt))
            for m in range(2, T // CH):
                t.do(dve.scalar_tensor_tensor(cnt[:, 0, :], n_e, m * CH + 0.5, cnt[:, 0, :], ALU.is_gt, ALU.add))
            t.do(dve.tensor_tensor_scan(cnt[:, 1, :], ones[:, 0:32], cnt[:, 0, :], 0.0, ALU.mult, ALU.add))
            t.do(dve.tensor_tensor(cnt[:, 2, :], cnt[:, 1, :], cnt[:, 0, :], ALU.subtract))
            t.do(dve.tensor_tensor(cnt[:, 3, :], cnt[:, 2, :], erow, ALU.subtract))
            t.do(dve.tensor_scalar(cnt[:, 3, :], cnt[:, 3, :], float(CH), float(CH * (NE - 1)), ALU.mult, ALU.add))
            rank = ps[:, 7, 0:96].rearrange("p (j e) -> p j e", j=NTILE)
            t.do(dve.tensor_scalar(tmp, rank, CH - 0.5, None, ALU.is_gt))
            t.do(dve.tensor_tensor(tmp, tmp, row(cnt[:, 3, :], 32), ALU.mult))
            t.do(dve.tensor_tensor(slot_v, rank, tmp, ALU.add))
            t.do(dve.scalar_tensor_tensor(slot_v, row(erow, 32), float(CH), slot_v, ALU.mult, ALU.add))
            for k in range(2):
                t.do(dve.tensor_tensor(tmp, slot_v, oh[:, k], ALU.mult))
                t.do(dve.tensor_reduce(slots[:, k, :], tmp, AX.X, ALU.add))
            dve.tensor_copy(slots_i[:, :], slots.rearrange("p k j -> p (k j)")).then_inc(slots_ok, 1)
            n_ov = N_CHUNKS - NE
            q_col = erow[:, 0:n_ov].unsqueeze(2).to_broadcast([P, n_ov, NE])

            def by_chunk(v):
                return v.unsqueeze(1).to_broadcast([P, n_ov, NE])
            dve.tensor_tensor(mq, by_chunk(cnt[:, 2, :]), q_col, ALU.is_le)
            t.do(dve.tensor_tensor(mq2, by_chunk(cnt[:, 1, :]), q_col, ALU.is_gt))
            t.do(dve.tensor_tensor(mq, mq, mq2, ALU.mult))
            t.do(dve.tensor_tensor(mq, mq, by_chunk(erow), ALU.mult))
            dve.tensor_copy(meta[:, 1:1 + NE], erow)
            dve.tensor_scalar(meta[:, 0:1], cnt[:, 1, 31:32], 0.5, None, ALU.is_gt)
            t.do(dve.tensor_reduce(meta[:, 1 + NE:1 + N_CHUNKS], mq, AX.X, ALU.add))
            for m in range(1, OV_TURNS):
                t.do(dve.scalar_tensor_tensor(meta[:, 0:1], cnt[:, 1, 31:32], 4.0 * m + 0.5, meta[:, 0:1], ALU.is_gt, ALU.add))
            t.do(dve.tensor_copy(meta_i[:, :], meta))
            dve.wait_ge(rows_ps, 1)
            dve.tensor_copy(idx[:, :], ps[:, 6, 0:N_GROUPS]).then_inc(idx_ok, 1)
            rows_copy(dve, 0, 0)
            rows_copy(dve, 1, 1)
            for n in (1, 2):
                hidden(dve, n - 1, 1 - n % 2)
                rows_copy(dve, n + 1, 1 - n % 2)
            n_turns = turns(dve)
            with dve.Fori(1, n_turns - 1) as i:
                hidden(dve, i * 2, 0)
                rows_copy(dve, i * 2 + 2, 0)
                hidden(dve, i * 2 + 1, 1)
                rows_copy(dve, i * 2 + 3, 1)
            hidden(dve, n_turns * 2 - 2, 0)
            hidden(dve, n_turns * 2 - 1, 1)
            for j in range(NTILE):
                b, v = j % 2, min(j, 1)
                dve.wait_ge(comb[b], 32 * (j // 2 + 1))
                if j:
                    dve.wait_ge(x1_ok, j + 3)
                t.do(dve.tensor_scalar(ymoe, cmb[:, b, 0, :], wcol[:, 0, j:j + 1], None, ALU.mult))
                dve.scalar_tensor_tensor(ymoe, cmb[:, b, 1, :], wcol[:, 1, j:j + 1], ymoe, ALU.mult,
                                         ALU.add).then_inc(moe_ok, 1)
                dve.wait_ge(moe_ok, j + 1)
                t.do(dve.tensor_tensor(ymoe, ymoe, g2[:, v, :], ALU.mult))
                dve.tensor_tensor(x1[:, j, :], x1[:, j, :], ymoe, ALU.add).then_inc(x1_ok, 1)
            dve.wait_ge(sq2_ok, 6)
            dve.tensor_scalar(fst[:, 3:6], fst[:, 0:3], 1.0 / D, 1e-6, ALU.mult, ALU.add).then_inc(meansq, 1)
            dve.wait_ge(rstd, 4)
            t.do(dve.reciprocal(fst[:, 9:12], fst[:, 6:9]))
            for j in range(NTILE):
                dve.scalar_tensor_tensor(x1[:, j, :], x1[:, j, :], fst[:, 9 + j:10 + j], fnw, ALU.mult,
                                         ALU.mult).then_inc(y_ok, 1)


N_SMALL = 19
N_OUT = 7


_OUTS = [(1, P, D), (1, 2 * P, D), (1, 1, HM, PM, NS), (1, 1, HM, PM, NS), (1, 1, 16, 64, 64), (1, 1, 16, 64, 64)]


def kernel(**inputs):
    import numpy as np
    import concourse.bacc as bacc
    from concourse.bass_utils import run_bass_kernel_spmd

    nc = bacc.Bacc("TRN2", target_bir_lowering=False, num_devices=1)
    arrays, aps = {}, {}
    for name, value in inputs.items():
        arr = np.ascontiguousarray(value)
        arrays["in_" + name] = arr
        aps[name] = nc.dram_tensor("in_" + name, arr.shape, mybir.dt.from_np(arr.dtype), kind="ExternalInput").ap()
    outs = [nc.dram_tensor(f"out_{i}", shape, F32, kind="ExternalOutput").ap() for i, shape in enumerate(_OUTS)]
    program(nc, aps, outs)
    got = run_bass_kernel_spmd(nc, [arrays], core_ids=[0]).results[0]
    return tuple(got[f"out_{i}"] for i in range(len(_OUTS)))
```

```python
from contextlib import ExitStack

import concourse.bass as bass
from concourse import mybir

ALU = mybir.AluOpType
ACT = mybir.ActivationFunctionType
AX = mybir.AxisListType
F32 = mybir.dt.float32
I32 = mybir.dt.int32
U32 = mybir.dt.uint32
ds = bass.ds

P = 128
D = 1024
KT = D // P
NTILE = 3
T = NTILE * P
GRID = 64
BLK = 512
HM, PM, NS = 16, 64, 128
XBC = 12
DTC = 2560
RC = 2592
RT = 27
RING = 3
NEG_C = -0.6065306597126334
NE, EG, EPG, DE = 32, 4, 8, 256
CH = 64
NG = NE * CH // P
N_OVER = (2 * T - 1) // CH
OV_TURNS = -(-N_OVER * CH // (2 * P))
N_GROUPS = NG + 2 * OV_TURNS
N_CHUNKS = N_GROUPS * P // CH

V0 = dict(b_ada=0, norm1=48, conv_w=56, conv_b=116)
V1 = dict(mu=0, w0=27, a0=43, k_k=59, k_a=67, r_k=75, ln_w=83, ln_b=91, norm2=99, m_norm=107)
V1N = 115

ADA_N = [0, 1, 2, 3, 5, 7, 9, 10, 12, 13, 15, 16]
ADA_COLS = [0, 1, 2, 3, 6, 7, 8, 9, 4, 5, 10, 11]
X_N, Z_N, R = [4, 6, 8], [11, 14], 17
N_BLOCKS = R + 7


OFF = ((1, 0, 0), (1, 1, 1), (2, 1, 0), (2, 0, 1))


class Chain:

    def __init__(self, eng, sem):
        self.eng, self.sem, self.n = eng, sem, 0

    def did(self, ins):
        ins.then_inc(self.sem, 1)
        self.n += 1
        return self.n

    def wait(self, n=None):
        self.eng.wait_ge(self.sem, self.n if n is None else n)

    def do(self, ins):
        self.did(ins)
        self.wait()


class LoopChain:

    def __init__(self, eng, sem, i, per):
        self.eng, self.sem, self.i, self.per, self.n = eng, sem, i, per, 0

    def did(self, ins):
        ins.then_inc(self.sem, 1)
        self.n += 1
        return self.n

    def wait(self, n=None):
        self.eng.wait_ge(self.sem, self.i * self.per + (self.n if n is None else n))

    def do(self, ins):
        self.did(ins)
        self.wait()

    def end(self):
        assert self.n == self.per, (self.n, self.per)


def program(nc, a, out):
    ctx = ExitStack()
    with ctx:
        def sb(name, shape, dt=F32):
            return ctx.enter_context(nc.sbuf_tensor(name, shape, dt))

        def sem(name):
            return ctx.enter_context(nc.semaphore(name))

        ps = ctx.enter_context(nc.psum_tensor("ps", [P, 8, 512], F32))

        ident = sb("ident", [P, P])
        ones = sb("ones", [P, P])
        bones = sb("bones", [P, P])
        tri = sb("tri", [P, 4, P])
        trin = sb("trin", [P, 4, P])
        lvl = sb("lvl", [P, 7, 2, P])
        sel32 = sb("sel32", [P, 32])
        par = sb("par", [P, 6])
        rst = sb("rst", [P, 2, T])
        vrows = sb("vrows", [P, 2, P])
        crows = sb("crows", [16, P])
        pv0 = sb("pv0", [P, P])
        pv1 = sb("pv1", [P, P])
        cond = sb("cond", [P, KT, 32])
        mod = sb("mod", [P, 32, 2])
        aff1 = sb("aff1", [P, KT, 2])
        aff2 = sb("aff2", [P, KT, 2])
        mum = sb("mum", [P, 7, RT])
        kam = sb("kam", [P, KT])
        drow = sb("drow", [P, 32 + 32 + 16])
        stat = sb("stat", [P, 16])
        dt = sb("dt", [P, NTILE, 32])
        dtmp = sb("dtmp", [P, NTILE, 32])
        dtl = sb("dtl", [P, NTILE, 32])
        dtr = sb("dtr", [P, NTILE, 32])
        la = sb("la", [P, NTILE, 32])
        ecs = sb("ecs", [P, 288])
        wdt = sb("wdt", [P, KT, 32])

        ring_a = sb("ring_a", [P, RING * KT * BLK])
        um_a = sb("um_a", [P, RT, T])
        mixm = sb("mixm", [P, KT, T])
        hT = sb("hT", [P, KT, T])
        misc = sb("misc", [P, 12288])

        ring = ring_a[:, :].rearrange("p (s k c) -> p s k c", s=RING, k=KT)
        xt = misc[:, 0:3072].rearrange("p (j c) -> p j c", j=NTILE)
        zs = misc[:, 3072:6144].rearrange("p (j c) -> p j c", j=NTILE)
        xs = misc[:, 6144:9216].rearrange("p (j c) -> p j c", j=NTILE)
        btm = misc[:, 9216:9984].rearrange("p (j c) -> p j c", j=NTILE)
        bct = misc[:, 9984:11520].rearrange("p (i t) -> p i t", i=4)
        scratch = sb("scratch", [P, 2048 + 2 * BLK])
        raw = scratch[:, 0:784].rearrange("p (b t) -> p b t", b=2)
        acc = scratch[:, 784:1568].rearrange("p (b t) -> p b t", b=2)
        adas = scratch[:, 2048:3072].rearrange("p (b c) -> p b c", b=2)

        ring_s = [ring_a[:, 4096 * i:4096 * (i + 1)] for i in range(RING)]
        st_in = ring_s[2][:, 0:2048].rearrange("p (d i n) -> p d i n", d=2, i=8)
        st0 = ring_s[2][:, 2048:4096].rearrange("p (d c) -> p d c", d=2)
        st1 = ring_s[0][:, 0:2048].rearrange("p (d c) -> p d c", d=2)
        xdw = ring_s[0][:, 2048:4096].rearrange("p (b c) -> p b c", b=2)
        msc = ring_s[1][:, 0:1536].rearrange("p (d i q) -> p d i q", d=2, i=6)
        yoff = ring_s[1][:, 1536:2048]
        st_out = ring_s[1][:, 2048:4096].rearrange("p (d i n) -> p d i n", d=2, i=8)
        hT_flat = hT[:, :, :].rearrange("p k t -> p (k t)")
        lam = hT_flat.rearrange("p (b i s) -> p b i s", b=NTILE, i=8)
        seg = misc[:, 0:3072].rearrange("p (b i s) -> p b i s", b=NTILE, i=8)
        sq = misc[:, 2048:2560]
        mstat = sb("mstat", [P, 24])

        def at(flat, o, *shape):
            names = "abcd"[:len(shape)]
            n = 1
            for x in shape:
                n *= x
            v = flat[:, o:o + n]
            return v if len(shape) == 1 else v.rearrange(
                f"p ({' '.join(names)}) -> p {' '.join(names)}", **dict(zip(names, shape)))

        gb = [at(r, 0, 2, 2, 2, P) for r in ring_s]
        gk = [at(r, 1024, 2, 2, 2, P) for r in ring_s]
        xinvT = [at(r, 2048, 2, 2, P) for r in ring_s]
        xinv = [at(r, 2560, 2, 2, P) for r in ring_s]
        ys = [at(r, 3072, 2, 2, P) for r in ring_s]
        rhs_s = [at(r, 3584, 4, 64) for r in ring_s]
        us = [at(r, 3840, 2, 2, 64) for r in ring_s]
        sg = at(misc, 0, 2, T)
        am = at(misc, 768, 2, T)
        cs = at(misc, 1536, 2, T)
        csm = at(misc, 2304, 2, T)
        e_m = csm
        e_p = at(misc, 3072, 2, T)
        e_i = at(misc, 4608, 2, T)
        kd = at(misc, 5376, 2, T)
        be = at(misc, 6144, 2, NTILE, P)
        kap = at(misc, 6912, 2, NTILE, P)
        arrs = [at(misc, 7680, 2, NTILE, 2, P), at(scratch, 0, 2, NTILE, 2, P)]
        kk = at(misc, 9600, T)
        kroot = at(misc, 9984, T)
        rb = at(misc, 10368, T)
        eps_gn = sb("eps_gn", [P, 1])
        eps_rms = sb("eps_rms", [P, 1])
        tiny = sb("tiny", [P, 1])
        btks = [at(misc, 10752, 4, P), at(scratch, 1536, 4, P)]
        ktks = [at(misc, 11264, 4, P), at(scratch, 2048, 4, P)]
        vtks = [at(misc, 11776, NTILE, P), at(scratch, 2560, NTILE, P)]
        y_c = at(hT_flat, 0, T)
        yc0 = at(hT_flat, 384, T)
        ysq_c = at(hT_flat, 768, T)
        v_c = at(hT_flat, 1152, T)
        g_cs = [at(hT_flat, 1536, T), at(misc, 3840, T)]
        vbs = [at(hT_flat, 1920, T), at(misc, 4224, T)]
        tot = at(hT_flat, 2304, 2, NTILE)
        e_halfs = [at(hT_flat, 2310 + 6 * i, 2, NTILE) for i in range(2)]
        r0ps = [at(hT_flat, 2322 + 256 * i, 2, 2, 64) for i in range(2)]
        stw = sb("stw", [P, 3, P])
        r0all = sb("r0all", [P, 8, 2, 64])
        sall = sb("sall", [P, 8, 2, 64])
        wkv_in = scratch[0:64, 0:2048].rearrange("p (d c) -> p d c", d=2)

        s_small = sem("small_loads")
        s_x = sem("x_loaded")
        w_in_slot = [sem(f"block_in_slot_{i}") for i in range(RING)]
        s_wdt = sem("wdt_loaded")
        pool_c = sem("pool_steps")
        const_ready = sem("constants_ready")
        vec_t = sem("vectors_transposed")
        vec_ready = sem("vectors_ready")
        cond_ready = sem("cond_ready")
        ada_ps = sem("ada_in_psum")
        ada_sb = sem("ada_copied")
        ada_cols = sem("ada_columns_in_psum")
        s_cond = sem("conditions_loaded")
        cond_T = sem("conditions_transposed")
        ident_ok = sem("identity_ready")
        sel32_ok = sem("selector_ready")
        rstd = sem("roots_ready")
        xn_ready = sem("x_normalised")
        xT_ps = sem("x_transposed")
        hT_ready = sem("h_ready")
        proj = sem("projection_in_psum")
        proj_read = sem("projection_read")
        conv_acc = sem("conv_summed")
        conv_out = sem("conv_silu_done")
        conv_T = sem("conv_transposed")
        conv_tm = sem("conv_token_major")
        mix0 = sem("mix_started")
        dve_c = sem("dve_steps")
        dve_r = sem("dve_mix_steps")
        act_c = sem("act_steps")
        dt_ps = sem("dt_in_psum")
        out_done = sem("outputs_written")
        masks_ready = sem("level_masks_ready")
        dt_in = sem("softplus_input_ready")
        dt_ln = sem("softplus_log_ready")
        la_ready = sem("la_ready")
        cs_ps = sem("cumulated_la_in_psum")
        cs_exp = sem("decay_factors_ready")
        score_ps = sem("scores_in_psum")
        score_ok = sem("scores_masked")
        st_loaded = sem("ssm_states_loaded")
        st_T = sem("ssm_states_transposed")
        st0_ok = sem("ssm_states_ready")
        xdw_ok = sem("weighted_x_ready")
        cst_ps = sem("chunk_states_in_psum")
        cst_out = sem("prompt_states_copied")
        st1_ok = sem("carried_states_ready")
        lam_ok = sem("masked_la_ready")
        seg_ps = sem("segment_sums_in_psum")
        seg_exp = sem("segment_decays_ready")
        g_ok = sem("decayed_scores_ready")
        y_ps = sem("mamba_y_in_psum")
        y_sb = sem("mamba_y_read")
        off_ps = sem("state_y_in_psum")
        off_rd = sem("state_y_read")
        gated = sem("mamba_y_gated")
        ysq = sem("mamba_squares_and_roots")
        mroot = sem("mamba_roots_ready")
        ynorm = sem("mamba_y_normalised")
        ynorm_d = sem("mamba_y_last_half_normalised")
        yT_ps = sem("mamba_y_transposed")
        yT_sb = sem("mamba_mix_ready")
        act_m = sem("act_mamba_steps")
        dve_l = sem("dve_mamba_loop_steps")
        up_loaded = sem("up_projections_loaded")
        wkv_loaded = sem("wkv_states_loaded")
        wkv_T = sem("wkv_states_transposed")
        wkv_ok = sem("wkv_states_ready")
        wd_ok = sem("low_rank_activated")
        aux_ps = sem("aux_in_psum")
        aux_act = sem("aux_read_by_act")
        aux_dve = sem("aux_read_by_dve")
        ksq_ok = sem("k_squared")
        exp_in = sem("decay_sums_ready")
        exp_ok = sem("decays_ready")
        tot_ok = sem("tile_sums_ready")
        ehalf_ok = sem("half_decays_ready")
        v_ok = sem("v_copied")
        ab_ok = sem("alpha_beta_ready")
        rb_ok = sem("bonus_ready")
        i4_ok = sem("identities_ready")
        gram_ps = sem("grams_in_psum")
        gram_rd = sem("grams_masked")
        x_ok = sem("inverse_level_ready")
        yl_ps = sem("level_y_in_psum")
        yl_ok = sem("level_y_ready")
        zl_ps = sem("level_z_in_psum")
        r0_ok = sem("wkv_start_states_ready")
        rhs_ps = sem("rhs_in_psum")
        rhs_ok = sem("rhs_ready")
        u_ps = sem("u_in_psum")
        u_ok = sem("u_ready")
        yo_ps = sem("wkv_y_in_psum")
        yo_rd = sem("wkv_y_read")
        ws_ps = sem("wkv_state_in_psum")
        yc_ok = sem("wkv_y_ready")
        ysq_ok = sem("wkv_y_squared")
        kr_ok = sem("key_lengths_inverted")
        yr_ok = sem("wkv_deviations_inverted")
        pair_ok = sem("wkv_pair_done")
        fin_T = sem("wkv_final_transposed")
        fin_sb = sem("wkv_final_copied")
        dve_w = sem("dve_wkv_steps")
        dve_p = sem("dve_preparation_steps")
        dve_q = sem("dve_group_norm_steps")
        idle_dve = sem("idle_dve")
        idle_pool = sem("idle_pool")


        def slot(n):
            return ring[:, n % RING]

        def block_ready(eng, n):
            eng.wait_ge(w_in_slot[n % RING], 16 * (n // RING + 1))

        def block_used(eng, n):
            if n in ADA_N:
                eng.wait_ge(ada_ps, ADA_N.index(n) + 1)
            elif n in X_N:
                eng.wait_ge(proj, 4 * (X_N.index(n) + 1))
            elif n in Z_N:
                eng.wait_ge(proj, XBC + 3 * (Z_N.index(n) + 1))
            else:
                eng.wait_ge(proj, XBC + 6 + min(4 * (n - R + 1), RT))

        def ada_bank(i):
            return 4 + i % 2 if i < 4 else 7

        w_in_v = a["w_in"][0].rearrange("(k p) c -> p k c", p=P)
        w_ada_v = a["w_ada"][0].rearrange("(k p) c -> p k c", p=P)

        def block_source(n):
            if n in ADA_N:
                c = ADA_COLS[ADA_N.index(n)]
                return w_ada_v[:, :, BLK * c:BLK * (c + 1)]
            if n in X_N:
                c = D + BLK * X_N.index(n)
            elif n in Z_N:
                c = BLK * Z_N.index(n)
            else:
                c = RC + BLK * (n - R)
                return w_in_v[:, :, c:min(c + BLK, RC + RT * P)]
            return w_in_v[:, :, c:c + BLK]

        QUADS = [(q, j) for q in range(2) for j in range(NTILE)]

        def y_place(n):
            return ps[:, 6 + n % 2, 0:256]

        TJ = ((1, 2), (0, 0), (2, 1))
        UNITS = ((0, 1), (1, 2), (0, 0), (1, 0))

        MEAN, VAR, KSQ, W_UP, A_UP, V_T, G_UP, BE_T, KAP_T, BONUS = 0, 1, 2, 3, 5, 7, 8, 9, 10, 11

        def aux_bank(n, width):
            return ps[:, 6 + n % 2, 0:width]

        def aux_free(pe, c, n):
            if n == MEAN:
                pe.wait_ge(aux_act, c * 10 + 10)
            elif n == VAR:
                pe.wait_ge(aux_dve, c * 2 + 2)
            elif n == KSQ:
                pe.wait_ge(aux_dve, c * 2 + 3)
            else:
                pe.wait_ge(aux_act, c * 10 + (10 + n - 2))
            return aux_bank(n, T)

        def keep_warm(pe, place, n):
            for _ in range(n):
                pe.matmul(place, ident[:, :], ident[:, :], start=True, stop=True)

        def aux_there(eng, c, n):
            eng.wait_ge(aux_ps, c * 12 + (12 + n + 1))

        def prep_pe(pe, c, n):
            o = aux_free(pe, c, n)
            if n == KSQ:
                pe.wait_ge(ksq_ok, c + 2)
                pe.matmul(o, bones[:, :], kroot, start=True, stop=True).then_inc(aux_ps, 1)
            elif n < V_T:
                if n == W_UP:
                    pe.wait_ge(up_loaded, c * 48 + 96)
                i, d = (n - W_UP) // 2, (n - W_UP) % 2
                pe.matmul(o, stw[64 * d:64 * d + 64, i, :], um_a[64 * d:64 * d + 64, 24 + i, :],
                          start=True, stop=True).then_inc(aux_ps, 1)
            elif n == V_T:
                pe.wait_ge(v_ok, c + 2)
                for j in range(NTILE):
                    mm = pe.transpose(o[:, P * j:P * j + P], v_c[:, P * j:P * j + P], ident[:, :])
                mm.then_inc(aux_ps, 1)
            elif n == G_UP:
                pe.matmul(o, stw[:, 2, :], um_a[:, 26, :], start=True, stop=True).then_inc(aux_ps, 1)
            elif n < BONUS:
                pe.wait_ge(ab_ok, c * 2 + (n - BE_T + 3))
                for i, (d, j) in enumerate(UNITS):
                    mm = pe.transpose(aux_bank(n, 4 * P)[:, P * i:P * i + P], (be, kap)[n - BE_T][:, d, j, :], ident[:, :])
                mm.then_inc(aux_ps, 1)
            else:
                pe.wait_ge(rb_ok, c + 2)
                pe.matmul(o, bones[:, :], rb, start=True, stop=True).then_inc(aux_ps, 1)

        def tail_pe(pe, c, n, p):
            o = aux_free(pe, c, n)
            src, done = ((y_c, yc_ok), (ysq_c, ysq_ok))[n % 2]
            pe.wait_ge(done, p + 1)
            pe.matmul(o, bones[:, :], src, start=True, stop=True).then_inc(aux_ps, 1)

        def round_pe(pe, c, b, prev, nxt):
            arr, btk, ktk, vtk, r0p = arrs[b], btks[b], ktks[b], vtks[b], r0ps[b]

            def fill(*numbers):
                for n in numbers:
                    if n >= KSQ and nxt:
                        prep_pe(pe, c, n)
                    elif n < KSQ and prev:
                        tail_pe(pe, c, n, c - 1)

            for g, src in enumerate((be, kap)):
                for s in range(3):
                    if g == 0:
                        pe.wait_ge(yo_rd, c * 3 + (s + 1))
                    else:
                        pe.wait_ge(gram_rd, c * 6 + (s + 1))
                    for d in range(2):
                        j = TJ[s][d]
                        for h in range(2):
                            mm = pe.matmul(ps[:, 2 * s + h, 256 * d:256 * d + 256], src[64 * h:64 * h + 64, d, j, :],
                                           arr[64 * h:64 * h + 64, d, j, :, :].rearrange("p a t -> p (a t)"),
                                           start=True, stop=True)
                    mm.then_inc(gram_ps, 1)
                if g == 0:
                    fill(MEAN)

            plan = {1: (VAR, KSQ), 2: (W_UP, W_UP + 1), 3: (A_UP, A_UP + 1), 4: (V_T, G_UP)}
            for l in range(1, 7):
                for s in range(3):
                    if s == 2 and l in plan:
                        fill(plan[l][0])
                    pe.wait_ge(x_ok, c * 21 + (3 * l - 3 + s + 1))
                    if l == 1:
                        pe.wait_ge(gram_rd, c * 6 + (3 + s + 1))
                    for h in range(2):
                        for d in range(2):
                            i = 2 * h + d
                            mm = pe.matmul(ps[:, 2 * s, P * i:P * i + P], gb[s][:, h, d, 0, :], xinv[s][:, h, d, :],
                                           start=True, stop=True)
                    mm.then_inc(yl_ps, 1)
                for s in range(3):
                    if s == 2 and l in plan:
                        fill(plan[l][1])
                    pe.wait_ge(yl_ok, c * 18 + (3 * l - 3 + s + 1))
                    for h in range(2):
                        for d in range(2):
                            o = P * (2 * h + d)
                            if l < 6:
                                mm = pe.matmul(ps[:, 2 * s + 1, o:o + P], xinvT[s][:, h, d, :], ys[s][:, h, d, :],
                                               start=True, stop=True)
                    if l >= 5:
                        bank = 2 * s + (l == 6)
                        for h in range(2):
                            for d in range(2):
                                o = P * (2 * h + d)
                                mm = pe.matmul(ps[:, bank, o:o + P], ys[s][:, h, d, :], xinvT[s][:, h, d, :],
                                               start=True, stop=True)
                    mm.then_inc(zl_ps, 1)

            def rhs(s):
                pe.wait_ge(x_ok, c * 21 + (18 + s + 1))
                if s != 1:
                    pe.wait_ge(r0_ok, c * 2 + (2 if s else 1))
                for h in range(2):
                    for d in range(2):
                        j, hp = TJ[s][d], slice(64 * h, 64 * h + 64)
                        o = ps[:, 2 * s + h, 64 * d:64 * d + 64]
                        mm = pe.matmul(o, gk[s][:, h, d, 0, :], vtk[:, j, hp], start=True, stop=(s == 1))
                        if s != 1:
                            mm = pe.matmul(o, arr[hp, d, j, 0, :], r0p[hp, s // 2, d, :], start=False, stop=True)
                mm.then_inc(rhs_ps, 1)

            def u(s):
                pe.wait_ge(rhs_ok, c * 3 + (s + 1))
                for i in range(4):
                    mm = pe.matmul(ps[:, 2 * s + 1, 128 + 64 * i:192 + 64 * i], xinvT[s][:, i // 2, i % 2, :], rhs_s[s][:, i, :],
                                   start=True, stop=True)
                mm.then_inc(u_ps, 1)

            def end_state(s):
                pe.wait_ge(u_ok, c * 3 + (s + 1))
                for d in range(2):
                    j, un = TJ[s][d], 2 * s + d
                    o = ps[:, 2 * s + 1, 384 * d:384 * d + P]
                    pe.matmul(o, ktk[:, un, :], vtk[:, j, :], start=True, stop=False)
                    mm = pe.matmul(o, btk[:, un, :], us[s][:, d].rearrange("p h v -> p (h v)"), start=False, stop=True)
                mm.then_inc(ws_ps, 1)

            def y_out(s):
                pe.wait_ge(u_ok, c * 3 + (s + 1))
                for h in range(2):
                    for d in range(2):
                        j, hp = TJ[s][d], slice(64 * h, 64 * h + 64)
                        o = ps[hp, 2 * s, 256 + P * (0 if s == 1 else d):256 + P * (0 if s == 1 else d) + P]
                        first, last = (d == 0 or s != 1), (d == 1 or s != 1)
                        pe.matmul(o, vtk[:, j, hp], gk[s][:, h, d, 1, :], start=first, stop=False)
                        mm = pe.matmul(o, us[s][:, d, h, :], gb[s][:, h, d, 1, :], start=False, stop=(last and s == 1))
                        if s != 1:
                            mm = pe.matmul(o, r0p[hp, s // 2, d, :], arr[hp, d, j, 1, :], start=False, stop=True)
                mm.then_inc(yo_ps, 1)

            rhs(0)
            rhs(1)
            u(0)
            u(1)
            end_state(0)
            y_out(0)
            end_state(1)
            rhs(2)
            y_out(1)
            u(2)
            fill(BE_T, KAP_T)
            y_out(2)
            fill(BONUS)

        def prep_act(act, c, b, n):
            aux_there(act, c, n)
            src = aux_bank(n, T)
            if n == KSQ:
                act.activation(kroot, src, ACT.Ln, bias=tiny[:, 0:1]).then_inc(aux_act, 1)
                return
            elif n < V_T:
                i, d = (n - W_UP) // 2, (n - W_UP) % 2
                bias = pv1[:, ds(c + (V1[("w0", "a0")[i]] + 8 * d + 1), 1)]
                ins = act.activation((sg, am)[i][:, d, :], src, ACT.Sigmoid, bias=bias)
            elif n == V_T:
                ins = act.activation(vtks[b].rearrange("p j t -> p (j t)"), src, ACT.Copy)
            elif n == G_UP:
                ins = act.activation(g_cs[b], src, ACT.Copy)
            elif n == BE_T:
                ins = act.activation(btks[b].rearrange("p i t -> p (i t)"), aux_bank(n, 4 * P), ACT.Copy, scale=-1.0)
            else:
                ins = act.activation(ktks[b].rearrange("p i t -> p (i t)"), aux_bank(n, 4 * P), ACT.Copy)
            ins.then_inc(aux_act, 1)

        def inverse_roots(act, c, prev, nxt):
            act.wait_ge(aux_act, c * 10 + (12 if nxt else 11))
            if prev:
                act.activation(ysq_c, ysq_c, ACT.Exp, scale=-0.5).then_inc(yr_ok, 1)
            if nxt:
                act.activation(kroot, kroot, ACT.Exp, scale=-0.5).then_inc(kr_ok, 1)

        def exps_act(act, c, b):
            act.wait_ge(tot_ok, c + 2)
            act.activation(e_halfs[b], tot, ACT.Exp, scale=0.5 * NEG_C).then_inc(ehalf_ok, 1)
            act.wait_ge(exp_in, c + 2)
            for dst, src, sc in ((e_m, csm, NEG_C), (e_p, cs, NEG_C), (e_i, cs, -NEG_C)):
                act.activation(dst, src, ACT.Exp, scale=sc).then_inc(exp_ok, 1)

        def tail_act(act, c, n):
            aux_there(act, c, n)
            act.activation(ysq_c, aux_bank(n, T), ACT.Ln, scale=1.0 / 64, bias=eps_gn[:, 0:1]).then_inc(aux_act, 1)

        def round_act(act, c, b, prev, nxt):
            for l in range(1, 7):
                for s in range(3):
                    act.wait_ge(yl_ps, c * 18 + (3 * l - 3 + s + 1))
                    act.activation(ys[s].rearrange("p a b q -> p (a b q)"), ps[:, 2 * s, :], ACT.Copy).then_inc(yl_ok, 1)
                if l == 1 and prev:
                    tail_act(act, c, VAR)
                if nxt:
                    for n in {1: (KSQ,), 2: (W_UP, W_UP + 1), 3: (A_UP, A_UP + 1), 4: (V_T, G_UP)}.get(l, ()):
                        prep_act(act, c, 1 - b, n)
                if l == 1:
                    inverse_roots(act, c, prev, nxt)
                if nxt:
                    if l == 4:
                        exps_act(act, c, 1 - b)

            def rhs_copy(s):
                act.wait_ge(rhs_ps, c * 3 + (s + 1))
                act.activation(rhs_s[s].rearrange("p (h d) v -> p h (d v)", h=2), ps[:, 2 * s:2 * s + 2, 0:128],
                               ACT.Copy).then_inc(rhs_ok, 1)

            def u_copy(s):
                act.wait_ge(u_ps, c * 3 + (s + 4))
                act.activation(us[s].rearrange("p d h v -> p h d v"), ps[:, 2 * s + 1, 128:384].rearrange("p (h d v) -> p h d v", h=2, d=2),
                               ACT.Copy).then_inc(u_ok, 1)

            def y_copy(s):
                if s == 1:
                    act.wait_ge(ws_ps, c * 2 + 2)
                    for d in range(2):
                        for h in range(2):
                            hp = slice(64 * h, 64 * h + 64)
                            act.activation(sall[hp, ds(c, 1), d, :].rearrange("p a v -> p (a v)"),
                                           ps[hp, 3, 384 * d + 64 * h:384 * d + 64 * h + 64], ACT.Copy, scale=e_halfs[b][hp, d, 0:1])
                act.wait_ge(yo_ps, c * 3 + (s + 1))
                act.activation(y_c[:, 0:P] if s else y_c[:, P:T], ps[:, 2 * s, 256:384 if s else 512], ACT.Copy).then_inc(yo_rd, 1)
            rhs_copy(0)
            rhs_copy(1)
            u_copy(0)
            u_copy(1)
            y_copy(0)
            rhs_copy(2)
            y_copy(1)
            u_copy(2)
            if nxt:
                prep_act(act, c, 1 - b, BE_T)
                prep_act(act, c, 1 - b, KAP_T)

        def tile_of(i):
            return um_a[:, ds(i, 1), :].rearrange("p a t -> p (a t)")

        def wcol_of(name, c):
            return pv1[:, ds(c + V1[name], 1)]

        def both(ap):
            return ap.unsqueeze(1).to_broadcast([P, 2, T])

        def tiles(ap):
            return ap.rearrange("p d (j t) -> p d j t", j=NTILE)

        def tiles2(ap):
            return ap.rearrange("p (j t) -> p j t", j=NTILE).unsqueeze(1).to_broadcast([P, 2, NTILE, P])

        def level_mask(l, transposed):
            m = lvl[:, l, ::-1, :] if transposed else lvl[:, l, :, :]
            return m.bitcast(I32).unsqueeze(1).to_broadcast([P, 2, 2, P])

        def prep_dve(dve, c, b, lc, part):
            k = tile_of(c + 9)
            if part == 0:
                lc.do(dve.tensor_scalar(kk, k, wcol_of("k_k", c + 1), None, ALU.mult))
                dve.tensor_tensor(kroot, kk, kk, ALU.mult).then_inc(ksq_ok, 1)
            elif part == 1:
                dve.wait_ge(kr_ok, c + 2)
                lc.do(dve.scalar_tensor_tensor(kk, kroot, 1e12, kk, ALU.min, ALU.mult))
            elif part == 2:
                dve.wait_ge(aux_act, c * 10 + (10 + W_UP + 1))
                dve.tensor_tensor_scan(cs[:, 0, :], rst[:, 0, :], sg[:, 0, :], 0.0, ALU.mult, ALU.add)
                lc.do(dve.tensor_tensor_scan(cs[:, 1, ::-1], rst[:, 1, ::-1], sg[:, 1, ::-1], 0.0, ALU.mult, ALU.add))
                dve.tensor_copy(tot[:, 0, :], cs[:, 0, P - 1::P])
                dve.tensor_copy(tot[:, 1, :], cs[:, 1, 0::P]).then_inc(tot_ok, 1)
                dve.wait_ge(tot_ok, c + 2)
                cs6 = cs.rearrange("p d (j t) -> p (d j) t", j=NTILE)
                lc.do(dve.scalar_tensor_tensor(cs6, tot.rearrange("p d j -> p (d j)").unsqueeze(2).to_broadcast([P, 6, P]),
                                               -0.5, cs6, ALU.mult, ALU.add))
                dve.tensor_tensor(csm, cs, sg, ALU.subtract).then_inc(exp_in, 1)
            elif part == 3:
                dve.wait_ge(aux_act, c * 10 + (10 + A_UP + 1))
                lc.do(dve.tensor_scalar(kd, am, wcol_of("k_a", c + 1), kam[:, ds(c + 1, 1)], ALU.mult, ALU.add))
                dve.tensor_tensor(am, am, both(kk), ALU.mult)
                lc.do(dve.tensor_tensor(kd, kd, both(k), ALU.mult))
            elif part == 4:
                dve.wait_ge(exp_ok, c * 3 + 6)
                dve.tensor_tensor(arrs[b][:, :, :, 0, :], tiles2(kk), tiles(e_m), ALU.mult)
                dve.tensor_tensor(arrs[b][:, :, :, 1, :], tiles2(tile_of(c + 1)), tiles(e_p), ALU.mult)
            elif part == 5:
                dve.tensor_tensor(be, tiles(am), tiles(e_i), ALU.mult).then_inc(ab_ok, 1)
                dve.tensor_tensor(kap, tiles(kd), tiles(e_i), ALU.mult).then_inc(ab_ok, 1)
                lc.do(dve.tensor_tensor(rb, kd[:, 0, :], kd[:, 1, :], ALU.add))
                dve.scalar_tensor_tensor(rb, rb, wcol_of("r_k", c + 1), tile_of(c + 1), ALU.mult, ALU.mult).then_inc(rb_ok, 1)
            else:
                dve.wait_ge(ehalf_ok, c + 2)
                for d in range(2):
                    j = TJ[0][d]
                    ins = dve.tensor_scalar(r0ps[b][:, 0, d, :], r0all[:, ds(c + 1, 1), d, :].rearrange("p a v -> p (a v)"),
                                      e_halfs[b][:, d, j:j + 1], None, ALU.mult)
                ins.then_inc(r0_ok, 1)
                aux_there(dve, c, BONUS)
                dve.wait_ge(v_ok, c + 2)
                dve.tensor_tensor(vbs[b], aux_bank(BONUS, T), v_c, ALU.mult).then_inc(aux_dve, 1)

        def tail_dve(dve, c, n, p, b, lc, part):
            if part == 0:
                aux_there(dve, c, n)
                dve.scalar_tensor_tensor(yc0, aux_bank(n, T), -1.0 / 64, y_c, ALU.mult, ALU.add).then_inc(aux_dve, 1)
                dve.wait_ge(aux_dve, c * 2 + (3 if n == 0 else 4))
                dve.tensor_tensor(ysq_c, yc0, yc0, ALU.mult).then_inc(ysq_ok, 1)
            else:
                dve.wait_ge(yr_ok, p + 1)
                lc.do(dve.tensor_tensor(yc0, yc0, ysq_c, ALU.mult))
                lc.do(dve.scalar_tensor_tensor(yc0, yc0, wcol_of("ln_w", p), vbs[b], ALU.mult, ALU.add))
                dve.scalar_tensor_tensor(tile_of(p), yc0, wcol_of("ln_b", p), g_cs[b], ALU.add, ALU.mult).then_inc(pair_ok, 1)

        def round_dve(dve, c, b, prev, nxt):
            lc = LoopChain(dve, dve_w, c, 16)
            pc = LoopChain(dve, dve_p, c + 1, 7)
            tc = LoopChain(dve, dve_q, c - 1, 2)
            r0p, e_half = r0ps[b], e_halfs[b]
            for g in range(2):
                for s in range(3):
                    dve.wait_ge(gram_ps, c * 6 + (3 * g + s + 1))
                    dst = (gb, gk)[g][s].rearrange("p h a b q -> p h (a b q)")
                    m = (trin, tri)[g][:, :, :].rearrange("p i q -> p (i q)").unsqueeze(1).to_broadcast([P, 2, 512])
                    ins = dve.tensor_tensor(dst, ps[:, 2 * s:2 * s + 2, :], m, ALU.mult)
                    ins.then_inc(gram_rd, 1)
                    if g == 0:
                        dve.wait_ge(gram_rd, c * 6 + (s + 1))
                        dve.wait_ge(i4_ok, c * 3 + (s + 1))
                        dve.sem_inc(idle_dve, 1)
                        lc.do(dve.copy_predicated(xinvT[s], level_mask(0, True), gb[s][:, :, :, 0, :]))
                        dve.transpose(xinv[s].rearrange("p a b q -> p (a b q)"),
                                      xinvT[s].rearrange("p a b q -> p (a b q)")).then_inc(x_ok, 1)
            if prev:
                tail_dve(dve, c, MEAN, c - 1, 1 - b, tc, 0)
            if nxt:
                prep_dve(dve, c, 1 - b, pc, 0)
            for l in range(1, 7):
                for s in range(3):
                    dve.wait_ge(zl_ps, c * 18 + (3 * l - 3 + s + 1))
                    dve.sem_inc(idle_dve, 1)
                    z = ps[:, 2 * s + 1, :].rearrange("p (h d q) -> p h d q", h=2, d=2)
                    zt = ps[:, 2 * s + (l == 6), :].rearrange("p (h d q) -> p h d q", h=2, d=2)
                    if l < 6:
                        ins = dve.copy_predicated(xinv[s], level_mask(l, False), z)
                    if l >= 5:
                        ins = dve.copy_predicated(xinvT[s], level_mask(l, True), zt)
                    if l < 5:
                        lc.do(ins)
                        ins = dve.transpose(xinvT[s].rearrange("p a b q -> p (a b q)"),
                                            xinv[s].rearrange("p a b q -> p (a b q)"))
                    ins.then_inc(x_ok, 1)
                if l == 1 and prev:
                    tail_dve(dve, c, MEAN, c - 1, 1 - b, tc, 1)
                elif l > 1 and nxt:
                    prep_dve(dve, c, 1 - b, pc, l - 1)
            dve.wait_ge(ws_ps, c * 2 + 1)
            for d in range(2):
                for h in range(2):
                    hp = slice(64 * h, 64 * h + 64)
                    ins = dve.tensor_tensor(r0p[hp, 1, d, :], ps[hp, 1, 384 * d + 64 * h:384 * d + 64 * h + 64], r0p[hp, 0, d, :], ALU.add)
            lc.do(ins)
            for d in range(2):
                j, j2 = TJ[0][d], TJ[2][d]
                ins = dve.tensor_scalar(r0p[:, 1, d, :], r0p[:, 1, d, :], e_half[:, d, j:j + 1],
                                        e_half[:, d, j2:j2 + 1], ALU.mult, ALU.mult)
            ins.then_inc(r0_ok, 1)
            dve.wait_ge(yo_ps, c * 3 + 3)
            dve.wait_ge(yo_rd, c * 3 + 5)
            dve.tensor_tensor(y_c[:, 2 * P:T], y_c[:, 2 * P:T], ps[:, 4, 256:384], ALU.add)
            dve.tensor_tensor(y_c[:, P:2 * P], y_c[:, P:2 * P], ps[:, 4, 384:512], ALU.add).then_inc(yo_rd, 1)
            dve.wait_ge(yo_rd, c * 3 + 6)
            dve.sem_inc(yc_ok, 1)
            if nxt:
                prep_dve(dve, c, 1 - b, pc, 6)
                pc.end()
            if prev:
                tc.end()
            lc.end()

        x1 = at(misc, 0, NTILE, D)
        g1 = at(misc, 3072, 2, D)
        g2 = at(misc, 5120, 2, D)
        h2 = at(misc, 7168, NTILE, D)
        um_f = um_a[:, :, :].rearrange("p i t -> p (i t)")
        xgT = at(um_f, 2048, 2, KT, P)
        yg = at(um_f, 4096, 2, D)
        hs = at(um_f, 6144, 2, DE)
        hid = at(um_f, 6656, 2, DE)
        hidT = at(um_f, 7168, 2, 2, P)
        wr = at(um_f, 7680, KT, 36)
        h2sq = at(um_f, 4096, D)
        mx_f = mixm[:, :, :].rearrange("p i t -> p (i t)")
        fnw = at(mx_f, 0, D)
        ymoe = misc[:, 10240:10240 + D]
        lg = at(scratch, 0, NTILE, 36)
        lgT = scratch[0:36, 2048:2048 + T]
        msk = at(scratch, 108, NTILE, 32)
        tmp = at(scratch, 204, NTILE, 32)
        oh = at(scratch, 300, 2, NTILE, 32)
        both_oh = at(scratch, 492, NTILE, 32)
        slot_v = at(scratch, 588, NTILE, 32)
        ghot = at(scratch, 684, NTILE, 4)
        grp2 = at(scratch, 696, NTILE, 4)
        s3 = at(scratch, 708, 10, NTILE)
        cnt = at(scratch, 738, 4, 32)
        slots = at(scratch, 866, 2, NTILE)
        irow = at(scratch, 880, P)
        srel = at(scratch, 872, 2, NTILE)
        pick = at(scratch, 2432, NTILE, P)
        erow = at(scratch, 1011, 32)
        down = at(scratch, 1043, 36)
        brt = at(scratch, 1079, 36)
        fst = mstat[:, 0:12]
        wcol = at(scratch, 1127, 2, NTILE)
        meta = at(scratch, 1136, 1 + N_CHUNKS)
        mq = at(scratch, 1184, N_CHUNKS - NE, NE)
        mq2 = at(scratch, 1568, N_CHUNKS - NE, NE)
        wdt_f = wdt[:, :, :].rearrange("p k c -> p (k c)")
        slots_i = wdt_f[:, 0:6].bitcast(U32)
        gcol = wdt_f[:, 112:144].rearrange("p (t v) -> p t v", v=2)
        meta_i = wdt_f[:, 64:65 + N_CHUNKS].bitcast(I32)
        zrow = vrows[0:16, 0, :]
        cmb = at(um_f, 0, 2, 2, D)
        zero_z = sem("zeros_made")
        rconst = sem("router_constants")
        half = [ring_a[:, 6144 * i:6144 * (i + 1)] for i in range(2)]
        wgu = [[[(at(h, 0, KT, 2 * DE), 0, KT)] for h in half],
               [[(at(misc, 3072, 4, 2 * DE), 0, 4), (at(um_f, 0, 4, 2 * DE), 4, 4)],
                [(at(mx_f, D, 4, 2 * DE), 0, 4), (at(misc, 10240, 4, 2 * DE), 4, 4)]]]
        wdn = [[at(h, 4096, 2, D) for h in half], [at(hT_flat, 0, 2, D), at(um_f, 7968, 2, D)]]
        GU_LOADS, DN_LOADS = (4, 8), 2

        def gate_up_tile(b, x, k):
            return next(v[:, k - k0, :] for v, k0, n in wgu[b][x] if k0 <= k < k0 + n)

        y_dram = nc.dram_tensor("expert_rows", [N_GROUPS * P, D], F32).ap()

        x_again = sem("x_loaded_again")
        wout0_in = sem("first_out_weights_loaded")
        gcol_ok = sem("gate_columns_ready")
        gate_ps = sem("gate_rows_in_psum")
        gate_ok = sem("gates_ready")
        out_ps = sem("mix_product_in_psum")
        x1_ok = sem("x1_ready")
        late_in = sem("router_and_norm_loaded")
        sq2_ok = sem("x1_squared")
        xn2_ok = sem("x1_normalised")
        h2T_ps = sem("x1_transposed")
        h2T_ok = sem("h2_channel_major_ready")
        h2_ps = sem("h2_transposed_back")
        h2_ok = sem("h2_token_major_ready")
        lg_ps = sem("logits_in_psum")
        lgT_ps = sem("expert_major_logits_in_psum")
        lgT_ok = sem("expert_major_logits_ready")
        rt_act = sem("router_exps")
        rt_dve = sem("router_steps_for_act")
        a_ok = sem("assignments_ready")
        rank_ps = sem("ranks_in_psum")
        slots_ok = sem("slots_ready")
        meta_ok = sem("loop_table_ready")
        zero_ok = sem("overflow_rows_zeroed")
        sel_c = sem("selection_steps")
        sel_ok = sem("selection_ready")
        gu_in = [sem("gate_up_loaded_0"), sem("gate_up_loaded_1")]
        dn_in = [sem("down_loaded_0"), sem("down_loaded_1")]
        yst = [sem("expert_rows_stored_0"), sem("expert_rows_stored_1")]
        xt_ps = sem("rows_transposed")
        xt_rd = sem("rows_ready")
        gu_ps = sem("gate_up_in_psum")
        silu_ok = sem("silu_ready")
        hid_ok = sem("hidden_ready")
        ht_ps = sem("hidden_transposed")
        ht_rd = sem("hidden_channel_major_ready")
        dn_ps = sem("down_in_psum")
        yg_ok = sem("expert_rows_ready")
        comb = [sem("combined_rows_0"), sem("combined_rows_1")]
        moe_ok = sem("moe_summed")
        cmb_w = sem("first_expert_row_weighed")
        y_ok = sem("y_ready")

        def wout_block(q):
            if q == 0:
                return at(um_f, 8 * T, 4, D)
            return ring[:, q - 1].rearrange("p k c -> p (k c)").rearrange("p (k c) -> p k c", k=4)

        def wout_ready(eng, q):
            if q == 0:
                eng.wait_ge(wout0_in, 16)
            else:
                eng.wait_ge(w_in_slot[q - 1], 16 * (N_BLOCKS // RING + 1))

        def gate_rows(pe, m):
            if m:
                pe.wait_ge(gate_ok, m)
            for t in range(8):
                mm = pe.matmul(ps[:, 6 + t // 4, P * (t % 4):P * (t % 4) + P],
                               gcol[:, 8 * (m // 2) + t, m % 2:m % 2 + 1].to_broadcast([P, P]), ident[:, :],
                               start=True, stop=True)
            mm.then_inc(gate_ps, 1)

        def late(n, at_least):
            return not isinstance(n, int) or n >= at_least

        def expert_weights(sp, n, b, experts):
            if late(n, 2):
                sp.wait_ge(gu_ps, n - 1)
            for x in range(2):
                for i, name in enumerate(("moe_w_gate", "moe_w_up")):
                    for v, k0, kn in wgu[b][x]:
                        sp.dma_start(v[:, :, DE * i:DE * i + DE],
                                     a[name][0, ds(experts[x], 1), P * k0:P * (k0 + kn)].rearrange("a (k p) f -> p (a k) f", p=P)
                                     ).then_inc(gu_in[b], 16)
            if late(n, 2):
                sp.wait_ge(dn_ps, n - 1)
            for x in range(2):
                sp.dma_start(wdn[b][x], a["moe_w_down"][0, ds(experts[x], 1)].rearrange("a (k p) c -> p (a k) c", p=P)
                             ).then_inc(dn_in[b], 16)

        def rows_T(pe, n):
            pe.wait_ge(sel_ok, n + 1)
            if late(n, 1):
                pe.wait_ge(xt_rd, n)
            for k in range(KT):
                for j in range(NTILE):
                    mm = pe.matmul(ps[:, k // 4, P * (k % 4):P * (k % 4) + P], h2[:, j, P * k:P * k + P], pick[:, j, :],
                                   start=(j == 0), stop=(j == NTILE - 1))
            mm.then_inc(xt_ps, 1)

        def gate_up(pe, n, b):
            pe.wait_ge(xt_rd, n + 1)
            if late(n, 2):
                pe.wait_ge(hid_ok, n - 1)
            for k in range(KT):
                for x in range(2):
                    h = slice(CH * x, CH * x + CH)
                    mm = pe.matmul(ps[h, 2 + b, :], xgT[:, b, k, h], gate_up_tile(b, x, k), start=(k == 0),
                                   stop=(k == KT - 1), tile_position=(0, CH * x), skip_group_check=True)
            mm.then_inc(gu_ps, 1)

        def down_proj(pe, m, b):
            pe.wait_ge(hid_ok, m + 1)
            if late(m, 1):
                pe.wait_ge(ht_rd, m)
            for k in range(2):
                mm = pe.transpose(ps[:, 4, P * k:P * k + P], hid[:, b, P * k:P * k + P], ident[:, :])
            mm.then_inc(ht_ps, 1)
            pe.wait_ge(ht_rd, m + 1)
            if late(m, 1):
                pe.wait_ge(yg_ok, m)
            for c in range(2):
                for k in range(2):
                    for x in range(2):
                        h = slice(CH * x, CH * x + CH)
                        mm = pe.matmul(ps[h, 5 + c, :], hidT[:, b, k, h], wdn[b][x][:, k, BLK * c:BLK * c + BLK],
                                       start=(k == 0), stop=(k == 1), tile_position=(0, CH * x), skip_group_check=True)
            mm.then_inc(dn_ps, 1)

        def select(dve, n):
            if late(n, 1):
                dve.tensor_scalar(srel, srel, float(P), None, ALU.subtract).then_inc(sel_c, 1)
            else:
                dve.tensor_copy(srel, slots).then_inc(sel_c, 1)
            dve.wait_ge(sel_c, n * 2 + 1)
            for j in range(NTILE):
                ins = dve.tensor_scalar(pick[:, j, :], irow, srel[:, 0, j:j + 1], None, ALU.is_equal)
            ins.then_inc(sel_c, 1)
            dve.wait_ge(sel_c, n * 2 + 2)
            for j in range(NTILE):
                ins = dve.scalar_tensor_tensor(pick[:, j, :], irow, srel[:, 1, j:j + 1], pick[:, j, :], ALU.is_equal, ALU.add)
            ins.then_inc(sel_ok, 1)

        def rows_copy(dve, n, b):
            dve.wait_ge(xt_ps, n + 1)
            if late(n, 2):
                dve.wait_ge(gu_ps, n - 1)
            dve.tensor_copy(xgT[:, b, :, :].rearrange("p (g k) t -> p g (k t)", g=2), ps[:, 0:2, :]).then_inc(xt_rd, 1)

        def hidden(dve, m, b):
            dve.wait_ge(silu_ok, m + 1)
            if late(m, 2):
                dve.wait_ge(ht_ps, m - 1)
            dve.tensor_tensor(hid[:, b, :], hs[:, b, :], ps[:, 2 + b, DE:2 * DE], ALU.mult).then_inc(hid_ok, 1)
            dve.wait_ge(ht_ps, m + 1)
            if late(m, 2):
                dve.wait_ge(dn_ps, m - 1)
            dve.tensor_copy(hidT[:, b, :, :].rearrange("p k t -> p (k t)"), ps[:, 4, 0:256]).then_inc(ht_rd, 1)

        def silu_gate(act, n, b):
            act.wait_ge(gu_ps, n + 1)
            if late(n, 2):
                act.wait_ge(hid_ok, n - 1)
            act.activation(hs[:, b, :], ps[:, 2 + b, 0:DE], ACT.Silu).then_inc(silu_ok, 1)

        def expert_out(act, m, b):
            act.wait_ge(dn_ps, m + 1)
            if late(m, 2):
                act.wait_ge(yst[b], (m - b) * 8)
            act.activation(yg[:, b, :].rearrange("p (c n) -> p c n", c=2), ps[:, 5:7, :], ACT.Copy).then_inc(yg_ok, 1)
            act.wait_ge(yg_ok, m + 1)
            act.dma_start(y_dram[ds(m * P, P), :], yg[:, b, :]).then_inc(yst[b], 16)

        def turns(eng):
            eng.wait_ge(meta_ok, 1)
            return eng.value_load(meta_i[0:1, 0:1], min_val=0, max_val=OV_TURNS) + NG // 2

        small_loads = [(vrows[0:48, 0, :], a["b_ada"].rearrange("a (t p) -> (a t) p", p=P)),
                (vrows[48:56, 0, :], a["norm1_w"].rearrange("a (t p) -> (a t) p", p=P)),
                (vrows[56:116, 0, :], a["m_conv_w"].rearrange("a j (t p) -> (a j t) p", p=P)),
                (vrows[116:128, 0, :], a["m_conv_b"].rearrange("a (t p) -> (a t) p", p=P)),
                (vrows[0:27, 1, :], a["r_mu"].rearrange("a (t p) -> (a t) p", p=P)),
                (vrows[27:43, 1, :], a["r_w0"].rearrange("a d (t p) -> (a d t) p", p=P)),
                (vrows[43:59, 1, :], a["r_a0"].rearrange("a d (t p) -> (a d t) p", p=P)),
                (vrows[59:67, 1, :], a["r_k_k"].rearrange("a (t p) -> (a t) p", p=P)),
                (vrows[67:75, 1, :], a["r_k_a"].rearrange("a (t p) -> (a t) p", p=P)),
                (vrows[75:83, 1, :], a["r_r_k"].rearrange("a (t h) n -> (a t) (h n)", h=2)),
                (vrows[83:91, 1, :], a["r_ln_w"].rearrange("a (t p) -> (a t) p", p=P)),
                (vrows[91:99, 1, :], a["r_ln_b"].rearrange("a (t p) -> (a t) p", p=P)),
                (vrows[99:107, 1, :], a["norm2_w"].rearrange("a (t p) -> (a t) p", p=P)),
                (vrows[107:115, 1, :], a["m_norm_w"].rearrange("a (t p) -> (a t) p", p=P)),
                (drow[:, 0:32], a["m_dt_bias"].rearrange("a d h -> a (d h)").broadcast_to([P, 32])),
                (drow[:, 32:64], a["m_a_log"].rearrange("a d h -> a (d h)").broadcast_to([P, 32])),
                (drow[:, 64:80], a["m_d_skip"].broadcast_to([P, 16]))]

        block = ctx.enter_context(nc.Block())

        @block.sync
        def _(sp):
            sp.dma_start(crows[0:8, :], a["c_ctx"].rearrange("(t p) -> t p", p=P)).then_inc(s_cond, 16)
            sp.dma_start(crows[8:16, :], a["c"].rearrange("a (t p) -> (a t) p", p=P)).then_inc(s_cond, 16)
            for n in range(N_BLOCKS):
                if n >= RING:
                    block_used(sp, n - RING)
                src = block_source(n)
                sp.dma_start(slot(n)[:, :, 0:src.shape[2]], src).then_inc(w_in_slot[n % RING], 16)
                if n == 2:
                    sp.dma_start(xt[:, 0, :], a["x_prompt"][0]).then_inc(s_x, 16)
                    sp.dma_start(xt[:, 1:3, :], a["x_sample"][0].rearrange("(j p) c -> p j c", p=P)).then_inc(s_x, 16)
                if n == X_N[0]:
                    sp.dma_start(wdt[:, :, :], w_in_v[:, :, DTC:DTC + 32]).then_inc(s_wdt, 16)
            sp.wait_ge(zero_z, 1)
            zsrc = zrow[0:16, :].unsqueeze(1)
            sp.dma_start(y_dram[NG * P:N_GROUPS * P, :].rearrange("(p r) (s c) -> p (r s) c", p=16, c=P),
                         zsrc.to_broadcast([16, (N_GROUPS - NG) * D // 16, P])).then_inc(zero_ok, 16)
            sp.wait_ge(proj, XBC + 6 + RT)
            for d, name in enumerate(("state_ssm_fwd", "state_ssm_bwd")):
                sp.dma_start(st_in[:, d], a[name][0, 0].rearrange("(i h) p n -> (h p) i n", h=2)).then_inc(st_loaded, 16)
            for d in range(2):
                sp.wait_ge(cst_out, d + 1)
                sp.dma_start(out[2 + d][0, 0].rearrange("(i h) p n -> (h p) i n", h=2), st_out[:, d]).then_inc(out_done, 16)
            sp.wait_ge(conv_tm, 10)
            sp.wait_ge(conv_out, XBC)
            for d, name in enumerate(("state_wkv_fwd", "state_wkv_bwd")):
                sp.dma_start(wkv_in[:, d, :].rearrange("v (h n) -> v h n", h=16),
                             a[name][0, 0].rearrange("h v n -> v h n")).then_inc(wkv_loaded, 16)

            ups = [a["r_w_up"][0].rearrange("d r c -> (d r) c"), a["r_a_up"][0].rearrange("d r c -> (d r) c"),
                   a["r_g_up"][0]]
            for i, w in enumerate(ups):
                sp.dma_start(stw[:, i, :], w[:, 0:P]).then_inc(up_loaded, 16)
            with sp.Fori(0, 7) as c:
                sp.wait_ge(aux_ps, c * 12 + 9)
                for i, w in enumerate(ups):
                    sp.dma_start(stw[:, i, :], w[:, ds(c * P + P, P)]).then_inc(up_loaded, 16)
            w_out_q = [a["w_out"][0, BLK * q:BLK * (q + 1)].rearrange("(k p) c -> p k c", p=P) for q in range(4)]
            sp.wait_ge(v_ok, 8)
            sp.wait_ge(ab_ok, 16)
            sp.dma_start(wout_block(0), w_out_q[0]).then_inc(wout0_in, 16)
            sp.wait_ge(yo_rd, 27)
            x_row = [(x1[:, 0, :], a["x_prompt"][0]),
                     (x1[:, 1:3, :], a["x_sample"][0].rearrange("(j p) c -> p j c", p=P))]
            for q in range(1, 4):
                sp.dma_start(wout_block(q), w_out_q[q]).then_inc(w_in_slot[q - 1], 16)
            for dst, src in x_row:
                sp.dma_start(dst, src).then_inc(x_again, 16)
            sp.wait_ge(fin_sb, 2)
            for d in range(2):
                sp.dma_start(out[4 + d][0, 0].rearrange("h v n -> v h n"),
                             wkv_in[:, d, :].rearrange("v (h n) -> v h n", h=16)).then_inc(out_done, 16)
            sp.wait_ge(out_done, 16 * 4)
            sp.wait_ge(out_ps, 6)
            sp.dma_start(brt[:, 0:4], a["moe_b_grp"].broadcast_to([P, 4])).then_inc(late_in, 16)
            sp.dma_start(brt[:, 4:36], a["moe_b_exp"].broadcast_to([P, 32])).then_inc(late_in, 16)
            sp.dma_start(wr[:, :, 0:4], a["moe_w_grp"][0].rearrange("(k p) c -> p k c", p=P)).then_inc(late_in, 16)
            sp.dma_start(wr[:, :, 4:36], a["moe_w_exp"][0].rearrange("(k p) c -> p k c", p=P)).then_inc(late_in, 16)
            sp.dma_start(fnw, a["final_norm_w"].rearrange("(a c) -> a c", a=1).broadcast_to([P, D])).then_inc(late_in, 16)
            def gate_up_piece(b, x, piece, e):
                v, k0, kn = wgu[b][x][piece]
                for i, name in enumerate(("moe_w_gate", "moe_w_up")):
                    sp.dma_start(v[:, :, DE * i:DE * i + DE],
                                 a[name][0, e:e + 1, P * k0:P * (k0 + kn)].rearrange("a (k p) f -> p (a k) f", p=P)
                                 ).then_inc(gu_in[b], 16)

            def down_weights(b, x, e):
                sp.dma_start(wdn[b][x], a["moe_w_down"][0, e:e + 1].rearrange("a (k p) c -> p (a k) c", p=P)
                             ).then_inc(dn_in[b], 16)

            for x in range(2):
                gate_up_piece(0, x, 0, x)
            for x in range(2):
                down_weights(0, x, x)
            for piece in range(2):
                gate_up_piece(1, 1, piece, 3)
            down_weights(1, 1, 3)
            gate_up_piece(1, 0, 1, 2)
            sp.wait_ge(x1_ok, 3)
            gate_up_piece(1, 0, 0, 2)
            sp.wait_ge(h2_ps, 3)
            down_weights(1, 0, 2)
            with sp.Fori(1, turns(sp)) as i:
                for b in range(2):
                    experts = [sp.value_load(meta_i[0:1, ds(i * 4 + (2 * b + x + 1), 1)], min_val=0, max_val=NE - 1)
                               for x in range(2)]
                    expert_weights(sp, i * 2 + b, b, experts)
            for j in range(NTILE):
                sp.wait_ge(y_ok, j + 1)
                dst = out[0][0] if j == 0 else out[1][0, P * (j - 1):P * j, :]
                sp.dma_start(dst, x1[:, j, :]).then_inc(out_done, 16)
            sp.wait_ge(out_done, 16 * 7)

        @block.gpsimd
        def _(pool):
            chain = Chain(pool, pool_c)
            chain.do(pool.memset(ident[:, :], 0.0))
            chain.do(pool.affine_select(out=ident[:, :], in_=ident[:, :], compare_op=ALU.not_equal, fill=1.0, base=0,
                                    pattern=[[-1, P]], channel_multiplier=1))
            chain.do(pool.memset(cond[:, :, :], 0.0))
            pool.nop().then_inc(ident_ok, 1)
            pool.memset(ones[:, :], 1.0)
            pool.memset(tri[:, :, :], 1.0)
            pool.memset(lvl[:, :, :, :], 0.0)
            pool.memset(rst[:, :, :], 1.0)
            chain.do(pool.memset(raw[:, :, :], 0.0))
            for i, (step, cm, base) in enumerate([(1, -1, -1), (1, -1, 0), (-1, 1, -1), (-1, 1, 0)]):
                ins = pool.affine_select(out=tri[:, i, :], in_=tri[:, i, :], compare_op=ALU.is_ge, fill=0.0, base=base,
                                   pattern=[[step, P]], channel_multiplier=cm)
            chain.did(ins)
            pool.memset(rst[:, 0, :].rearrange("p (j t) -> p j t", j=NTILE)[:, :, 0:1], 0.0)
            pool.memset(rst[:, 1, :].rearrange("p (j t) -> p j t", j=NTILE)[:, :, P - 1:P], 0.0)
            chain.wait()
            pool.tensor_scalar(trin[:, :, :], tri[:, :, :], -1.0, None, ALU.mult).then_inc(const_ready, 1)
            for l in range(7):
                b = 1 << l
                for up in range(2):
                    v = lvl[:, l, up, :].rearrange("p (n h b) -> p n h b", h=2, b=b)[:, :, up, :]
                    chain.do(pool.memset(v, 1.0))
                    lo = 0 if up else -b
                    chain.do(pool.affine_select(out=v, in_=v, compare_op=ALU.is_ge, fill=0.0, base=lo,
                                            pattern=[[-2 * b, P // (2 * b)], [0, b]], channel_multiplier=1))
                    chain.do(pool.affine_select(out=v, in_=v, compare_op=ALU.is_ge, fill=0.0, base=-lo + b - 1,
                                            pattern=[[2 * b, P // (2 * b)], [0, b]], channel_multiplier=-1))
            pool.nop().then_inc(masks_ready, 1)
            pool.wait_ge(vec_t, 1)
            pool.memset(zrow[:, :], 0.0).then_inc(zero_z, 1)
            pool.wait_ge(la_ready, 1)
            pool.wait_ge(proj, XBC + 6 + RT)
            with pool.Fori(0, 2) as grp:
                for n, (q, j) in enumerate(QUADS):
                    pool.wait_ge(seg_ps, grp * 6 + (n + 1))
                    for d in range(2):
                        ins = pool.tensor_tensor(
                            lam[:, j, 4 * d:4 * d + 4, :],
                            tri[:, 2 - 2 * d, :].unsqueeze(1).to_broadcast([P, 4, P]),
                            la[:, j, ds(grp * 8 + (16 * d + 4 * q), 4)].unsqueeze(2).to_broadcast([P, 4, P]),
                            ALU.mult)
                    ins.then_inc(lam_ok, 1)

            pool.wait_ge(off_ps, 8)
            pool.wait_ge(cst_out, 2)
            pool.wait_ge(seg_ps, 15)
            pool.sem_inc(idle_pool, 1)
            pool.tensor_copy(v_c, um_a[:, 16, :]).then_inc(v_ok, 1)

            def identities(c):
                for s in range(3):
                    pool.wait_ge(u_ps, c * 3 + (s + 1))
                    pool.sem_inc(idle_pool, 1)
                    pool.tensor_copy(xinvT[s].rearrange("p a b q -> p (a b) q"),
                                     ident[:, :].unsqueeze(1).to_broadcast([P, 4, P])).then_inc(i4_ok, 1)

            with pool.Fori(0, 7) as c:
                identities(c)
                pool.wait_ge(aux_dve, c * 2 + 2)
                pool.sem_inc(idle_pool, 1)
                pool.tensor_copy(v_c, um_a[:, ds(c + 17, 1), :].rearrange("p a t -> p (a t)")).then_inc(v_ok, 1)
            identities(7)

            pool.wait_ge(out_done, 16 * 4)
            pool.iota(irow, pattern=[[1, P]], base=0, channel_multiplier=0, allow_small_or_imprecise_dtypes=True)
            pool.iota(erow, pattern=[[1, 32]], base=0, channel_multiplier=0, allow_small_or_imprecise_dtypes=True)
            pool.iota(down[:, 0:4], pattern=[[-1, 4]], base=4, channel_multiplier=0, allow_small_or_imprecise_dtypes=True)
            pool.iota(down[:, 4:36], pattern=[[-1, 32]], base=32, channel_multiplier=0,
                      allow_small_or_imprecise_dtypes=True).then_inc(rconst, 1)
            n_turns = turns(pool)
            pool.wait_ge(zero_ok, 16)
            for b in range(2):
                pool.wait_ge(yst[b], n_turns * 16)
            pool.sem_inc(idle_pool, 1)
            for j in range(NTILE):
                if j == 2:
                    pool.wait_ge(moe_ok, 1)
                for k in range(2):
                    pool.indirect_dma_start(out=cmb[:, j % 2, k, :], out_offset=None, in_=y_dram,
                                            in_offset=bass.IndirectOffsetOnAxis(ap=slots_i[:, 3 * k + j:3 * k + j + 1], axis=0)
                                            ).then_inc(comb[j % 2], 16)

        @block.tensor
        def _(pe):
            pe.wait_ge(ident_ok, 1)
            pe.wait_ge(s_cond, 32)
            pe.transpose(ps[:, 0, 0:16], crows[:, :], ident[0:16, 0:16]).then_inc(cond_T, 1)

            def ada_block(i):
                n = ADA_N[i]
                block_ready(pe, n)
                if i >= 5:
                    pe.wait_ge(ada_sb, i)
                elif 2 <= i < 4:
                    pe.wait_ge(ada_sb, i - 1)
                for k2 in range(2):
                    for q in range(4):
                        mm = pe.matmul(ps[32 * q:32 * q + 32, ada_bank(i), :], cond[:, 2 * q + k2, :],
                                       slot(n)[:, 2 * q + k2, :], start=(k2 == 0), stop=(k2 == 1),
                                       tile_position=(0, 32 * q), skip_group_check=True)
                mm.then_inc(ada_ps, 1)

            def ada_columns(i):
                pe.wait_ge(ada_sb, i + 1)
                for c in range(4):
                    o = 8 * i + 2 * c
                    mm = pe.matmul(ps[:, 6, o:o + 2], adas[:, i % 2, P * c:P * c + P], sel32[:, 0:2],
                                   start=True, stop=True)
                mm.then_inc(ada_cols, 1)

            pe.wait_ge(cond_ready, 1)
            pe.wait_ge(sel32_ok, 1)
            for i in range(4):
                ada_block(i)
                if i:
                    ada_columns(i - 1)
                if i == 1:
                    pe.wait_ge(s_small, 16 * N_SMALL)
                    pe.transpose(ps[:, 1, 0:P], vrows[:, 0, :], ident[:, :])
                    pe.transpose(ps[:, 2, 0:V1N], vrows[0:V1N, 1, :], ident[0:V1N, 0:V1N]).then_inc(vec_t, 1)
            ada_columns(3)

            pe.wait_ge(xn_ready, 1)
            for k in range(KT):
                if k >= 4:
                    pe.wait_ge(hT_ready, k - 3)
                for j in range(NTILE):
                    mm = pe.transpose(ps[:, k % 4, P * j:P * j + P], xt[:, j, P * k:P * k + P], ident[:, :])
                mm.then_inc(xT_ps, 1)

            def project(n, c, t):
                for k in range(KT):
                    mm = pe.matmul(ps[:, t % 4 if isinstance(t, int) else t, 0:T],
                                   slot(n)[:, k, P * c:P * c + P], hT[:, k, :],
                                   start=(k == 0), stop=(k == KT - 1))
                return mm

            def conv_transpose(t):
                pe.wait_ge(conv_out, t + 1)
                if t >= 2:
                    pe.wait_ge(conv_tm, t - 1)
                src = bct[:, t - 8, :] if t >= 8 else acc[:, t % 2, :]
                for j in range(NTILE):
                    if t >= 8:
                        v = src[:, P * j:P * j + P]
                    else:
                        v = src[:, P * j + (2 if j else 0):P * j + (2 if j else 0) + P]
                    mm = pe.transpose(ps[:, 4 + t % 2, P * j:P * j + P], v, ident[:, :])
                mm.then_inc(conv_T, 1)

            pe.wait_ge(hT_ready, KT)
            for t in range(XBC):
                if t % 4 == 0:
                    block_ready(pe, X_N[t // 4])
                if t >= 4:
                    pe.wait_ge(proj_read, t - 3)
                mm = project(X_N[t // 4], t % 4, t)
                mm.then_inc(proj, 1)
                if 2 <= t < 12:
                    conv_transpose(t - 2)
                if t in (4, 8):
                    ada_columns(3 + t // 4)
                if t in (3, 7):
                    ada_block(4 + t // 4)
            ada_block(6)
            ada_block(7)
            ada_columns(6)
            for i in range(6):
                n, j = Z_N[i // 3], i % 3
                if j == 0:
                    block_ready(pe, n)
                pe.wait_ge(proj_read, XBC - 3 + i)
                for k in range(KT):
                    mm = pe.matmul(ps[:, i % 4, :], hT[:, k, P * j:P * j + P], slot(n)[:, k, :],
                                   start=(k == 0), stop=(k == KT - 1))
                mm.then_inc(proj, 1)
                if j == 0:
                    ada_columns(7 if i == 0 else 9)
                if j == 2:
                    ada_block(8 if i == 2 else 10)
                    ada_block(9 if i == 2 else 11)
                    ada_columns(8 if i == 2 else 10)
            ada_columns(11)
            pe.wait_ge(s_wdt, 16)
            for j in range(NTILE):
                for k in range(KT):
                    mm = pe.matmul(ps[:, 7, 32 * j:32 * j + 32], hT[:, k, P * j:P * j + P], wdt[:, k, :],
                                   start=(k == 0), stop=(k == KT - 1))
            mm.then_inc(dt_ps, 1)
            with pe.Fori(0, 2) as r:
                for n in range(RING):
                    pe.wait_ge(w_in_slot[(R + n) % RING], r * 16 + 16 * ((R + n) // RING + 1))
                    for c in range(4):
                        pe.wait_ge(proj_read, r * 12 + (XBC + 6 + 4 * n + c - 3))
                        mm = project(R + n, c, (XBC + 6 + 4 * n + c) % 4)
                        mm.then_inc(proj, 1)
            block_ready(pe, R + 6)
            for c in range(3):
                pe.wait_ge(proj_read, XBC + 6 + 24 + c - 3)
                mm = project(R + 6, c, XBC + 6 + 24 + c)
                mm.then_inc(proj, 1)

            pe.wait_ge(proj_read, XBC + 6 + RT)
            pe.wait_ge(conv_tm, 10)
            pe.sem_inc(seg_ps, 3)
            pe.sem_inc(y_ps, 3)
            pe.wait_ge(la_ready, 1)
            for i, (m, lo) in enumerate(((1, 0), (3, 16), (2, 0), (0, 16))):
                pe.matmul(ps[:, 7, 48 * i:48 * i + 48], tri[:, m, :], la[:, :, lo:lo + 16], start=True, stop=True)
            pe.matmul(ps[:, 7, 192:288], ones[:, :], la[:, :, :], start=True, stop=True).then_inc(cs_ps, 1)
            for i in range(6):
                j, grp = i // 2, i % 2
                mm = pe.matmul(ps[:, 4 + i // 4, P * (i % 4):P * (i % 4) + P], bct[:, grp, P * j:P * j + P],
                               bct[:, 2 + grp, P * j:P * j + P], start=True, stop=True)
            mm.then_inc(score_ps, 1)
            pe.wait_ge(st_loaded, 32)
            for d in range(2):
                for i in range(8):
                    mm = pe.transpose(ps[:, 2 * d + i // 4, P * (i % 4):P * (i % 4) + P], st_in[:, d, i, :], ident[:, :])
            mm.then_inc(st_T, 1)
            for job in range(4):
                d, j = job % 2, (0, 0, 1, 2)[job]
                pe.wait_ge(xdw_ok, job + 1)
                if job == 0:
                    pe.wait_ge(st0_ok, 1)
                if job >= 2:
                    pe.wait_ge(cst_out, job - 1)
                b = 2 * d
                if job < 2:
                    for i in range(8):
                        grp = i // 4
                        mm = pe.matmul(ps[:, b + i // 4, P * (i % 4):P * (i % 4) + P], xdw[:, job % 2, P * i:P * i + P],
                                       btm[:, j, P * grp:P * grp + P], start=True, stop=True)
                else:
                    for grp in range(2):
                        mm = pe.matmul(ps[:, b + grp, :], btm[:, j, P * grp:P * grp + P],
                                       xdw[:, job % 2, BLK * grp:BLK * grp + BLK], start=True, stop=True)
                mm.then_inc(cst_ps, 1)
            pe.wait_ge(st1_ok, 1)
            pe.wait_ge(score_ok, 1)

            def seg_sums(grp, n):
                j = QUADS[n][1]
                pe.wait_ge(lam_ok, grp * 6 + (n + 1))
                pe.wait_ge(seg_exp, grp * 6 + (n + 1))
                for d in range(2):
                    for h in range(4):
                        mm = pe.matmul(ps[:, 2 * j + d, P * h:P * h + P], lam[:, j, 4 * d + h, :],
                                       tri[:, 1 + 2 * d, :], start=True, stop=True)
                mm.then_inc(seg_ps, 1)

            def y_heads(grp, n):
                q, j = QUADS[n]
                pe.wait_ge(g_ok, grp * 6 + (n + 1))
                pe.wait_ge(y_sb, grp * 6 + (n + 1))
                for h in range(4):
                    mm = pe.matmul(y_place(n)[:, 64 * h:64 * h + 64], seg[:, j, h, :],
                                   xs[:, j, ds(grp * BLK + 64 * (4 * q + h), 64)], start=True, stop=True)
                mm.then_inc(y_ps, 1)

            with pe.Fori(0, 2) as grp:
                for n in range(len(QUADS)):
                    seg_sums(grp, n)
                    if n >= 2:
                        y_heads(grp, n - 2)
                y_heads(grp, 4)
                y_heads(grp, 5)

            pe.wait_ge(seg_exp, 12 + 3)
            for o, (j, d, src) in enumerate(OFF):
                pe_src = (st0, st1)[src]
                for grp in range(2):
                    i = 2 * o + grp
                    if i >= 4:
                        pe.wait_ge(off_rd, i - 3)
                    pe.matmul(ps[:, i % 4, :], bct[:, 2 + grp, P * j:P * j + P], pe_src[:, d, BLK * grp:BLK * grp + BLK],
                              start=True, stop=True).then_inc(off_ps, 1)
            pe.wait_ge(wkv_loaded, 32)
            for d in range(2):
                for i in range(8):
                    mm = pe.transpose(ps[:, 4 + d, 64 * i:64 * i + 64], wkv_in[:, d, P * i:P * i + P], ident[0:64, 0:64])
            mm.then_inc(wkv_T, 1)
            pe.wait_ge(y_sb, 14)
            keep_warm(pe, ps[:, 7, 384:512], 24)
            pe.wait_ge(off_rd, 8)
            pe.wait_ge(wkv_ok, 1)
            for j in range(NTILE):
                pe.wait_ge(ynorm, j + 1)
                if j == NTILE - 1:
                    pe.wait_ge(ynorm_d, 1)
                for t in range(8):
                    mm = pe.transpose(ps[:, t, P * j:P * j + P], xs[:, j, P * t:P * t + P], ident[:, :])
                    if j == NTILE - 1:
                        mm.then_inc(yT_ps, 1)
                if j < NTILE - 1:
                    keep_warm(pe, ps[:, 7, 384:512], 12)

            pe.wait_ge(yT_sb, 8)
            pe.wait_ge(wd_ok, 1)
            pe.sem_inc(u_ps, 3)
            pe.sem_inc(aux_ps, 2)
            for n in range(KSQ, BONUS + 1):
                keep_warm(pe, ps[:, 0, 0:P], {KSQ: 8, W_UP: 6, BE_T: 28, KAP_T: 3, BONUS: 3}.get(n, 0))
                prep_pe(pe, -1, n)
            keep_warm(pe, ps[:, 0, 0:P], 3)
            pe.wait_ge(aux_act, 10)
            pe.wait_ge(aux_dve, 2)
            pe.sem_inc(aux_ps, 2)
            round_pe(pe, 0, 0, False, True)
            with pe.Fori(0, 3) as i:
                round_pe(pe, i * 2 + 1, 1, True, True)
                round_pe(pe, i * 2 + 2, 0, True, True)
            round_pe(pe, 7, 1, True, False)
            tail_pe(pe, 7, 2, 7)
            pe.wait_ge(yo_rd, 27)
            for d in range(2):
                for i in range(8):
                    mm = pe.transpose(ps[0:64, 2 * d + i // 4, P * (i % 4):P * (i % 4) + P], sall[:, i, d, :], ident[:, :])
                mm.then_inc(fin_T, 1)

            tail_pe(pe, 7, 3, 7)

            pe.wait_ge(fin_sb, 2)
            pe.wait_ge(gcol_ok, 1)
            for q in range(4):
                if q == 1:
                    pe.wait_ge(pair_ok, 9)
                if q:
                    gate_rows(pe, q - 1)
                if q == 3:
                    gate_rows(pe, 3)
                wout_ready(pe, q)
                w = wout_block(q)
                steps = ([(k, j) for k in range(4) for j in range(NTILE)] if q < 3 else
                         [(k, j) for j in range(NTILE) for k in range(4)])
                for k, j in steps:
                    kk_ = 4 * q + k
                    src = mixm[:, kk_, :] if kk_ < 8 else um_a[:, kk_ - 8, :]
                    for c in range(2):
                        mm = pe.matmul(ps[:, 2 * j + c, :], src[:, P * j:P * j + P], w[:, k, BLK * c:BLK * c + BLK],
                                       start=(kk_ == 0), stop=(kk_ == 15))
                    if q == 3 and k == 3:
                        mm.then_inc(out_ps, 1)
                if q < 3:
                    mm.then_inc(out_ps, 1)
            pe.wait_ge(gate_ok, 4)
            keep_warm(pe, ps[:, 6, 0:P], 24)
            pe.wait_ge(xn2_ok, 3)
            for k in range(KT):
                if k >= 2:
                    pe.wait_ge(h2T_ok, k - 1)
                for j in range(NTILE):
                    mm = pe.transpose(ps[:, 6 + k % 2, P * j:P * j + P], h2[:, j, P * k:P * k + P], ident[:, :])
                mm.then_inc(h2T_ps, 1)
            pe.wait_ge(h2T_ok, 8)
            pe.wait_ge(late_in, 16 * 5)
            for k in range(KT):
                mm = pe.matmul(ps[0:36, 6, 0:T], wr[:, k, :], hT[:, k, :], start=(k == 0), stop=(k == KT - 1))
            mm.then_inc(lgT_ps, 1)
            pe.wait_ge(lgT_ok, 1)
            for j in range(NTILE):
                mm = pe.transpose(ps[:, 7, 128 + 36 * j:164 + 36 * j], lgT[:, P * j:P * j + P], ident[0:36, 0:36])
            mm.then_inc(lg_ps, 1)
            for j in range(NTILE):
                for k in range(KT):
                    mm = pe.transpose(ps[:, 2 * j + k // 4, P * (k % 4):P * (k % 4) + P], hT[:, k, P * j:P * j + P], ident[:, :])
                mm.then_inc(h2_ps, 1)
            keep_warm(pe, ps[:, 6, 0:P], 14)
            pe.wait_ge(a_ok, 1)
            for j in range(NTILE):
                for i in range(j + 1):
                    mm = pe.matmul(ps[:, 7, 32 * j:32 * j + 32], tri[:, 0, :] if i == j else ones[:, :], both_oh[:, i, :],
                                   start=(i == 0), stop=(i == j))
            for i in range(NTILE):
                mm = pe.matmul(ps[:, 7, 96:128], ones[:, :], both_oh[:, i, :], start=(i == 0), stop=(i == 2))
            mm.then_inc(rank_ps, 1)
            keep_warm(pe, ps[:, 6, 0:P], 28)
            pe.wait_ge(h2_ok, 3)

            def pe_group(i, b, first=False, last=False):
                n = i * 2 + b
                pe.wait_ge(gu_in[b], i * (16 * GU_LOADS[b]) + 16 * GU_LOADS[b])
                gate_up(pe, n, b)
                if not first:
                    pe.wait_ge(dn_in[1 - b], i * (16 * DN_LOADS) + 16 * DN_LOADS * b)
                    down_proj(pe, n - 1, 1 - b)
                if not last:
                    rows_T(pe, n + 1)

            rows_T(pe, 0)
            for b in range(2):
                pe_group(0, b, first=(b == 0))
            n_turns = turns(pe)
            with pe.Fori(1, n_turns - 1) as i:
                for b in range(2):
                    pe_group(i, b)
            for b in range(2):
                pe_group(n_turns - 1, b, last=(b == 1))
            pe.wait_ge(dn_in[1], n_turns * (16 * DN_LOADS))
            down_proj(pe, n_turns * 2 - 1, 1)

        @block.scalar
        def _(act):
            chain = Chain(act, act_c)
            act.wait_ge(cond_T, 1)
            act.activation(cond[:, :, 0:2], ps[:, 0, 0:16].rearrange("p (v k) -> p k v", v=2),
                           ACT.Silu).then_inc(cond_ready, 1)
            for dst, src in small_loads:
                act.dma_start(dst, src).then_inc(s_small, 16)
            for i in range(4):
                act.wait_ge(ada_ps, i + 1)
                if i >= 2:
                    act.wait_ge(ada_cols, i - 1)
                act.activation(adas[:, i % 2, :], ps[:, ada_bank(i), :], ACT.Copy).then_inc(ada_sb, 1)
                if i == 1:
                    act.wait_ge(s_x, 32)
                    for j in range(NTILE):
                        chain.did(act.activation(zs[:, j, :], xt[:, j, :], ACT.Square, accum_out=stat[:, j:j + 1]))
                    chain.wait()
                    act.activation(stat[:, 12:15], stat[:, 0:3], ACT.Sqrt, scale=1.0 / D, bias=eps_rms[:, 0:1]).then_inc(rstd, 1)

            def ada_copy(i):
                act.wait_ge(ada_ps, i + 1)
                act.wait_ge(ada_cols, i - 1)
                act.activation(adas[:, i % 2, :], ps[:, ada_bank(i), :], ACT.Copy).then_inc(ada_sb, 1)
            def conv_in(t):
                act.wait_ge(proj, t + 1)
                if t >= 2:
                    act.wait_ge(conv_acc, t - 1)
                act.activation(raw[:, t % 2, 2:2 + P], ps[:, t % 4, 0:P], ACT.Copy)
                ins = act.activation(raw[:, t % 2, 4 + P:4 + T], ps[:, t % 4, P:T], ACT.Copy)
                ins.then_inc(proj_read, 1)

            def conv_silu(t):
                act.wait_ge(conv_acc, t + 1)
                bias = pv0[:, V0["conv_b"] + t:V0["conv_b"] + t + 1]
                for o, i, n in ((0, 0, P), (P, P + 2, T - P)):
                    src = acc[:, t % 2, i:i + n]
                    dst = bct[:, t - 8, o:o + n] if t >= 8 else src
                    ins = act.activation(dst, src, ACT.Silu, bias=bias)
                ins.then_inc(conv_out, 1)

            for t in range(XBC):
                conv_in(t)
                if t:
                    conv_silu(t - 1)
                if t % 4 == 3:
                    ada_copy(4 + t // 4)
            ada_copy(7)
            conv_silu(XBC - 1)
            for i in range(6):
                act.wait_ge(proj, XBC + i + 1)
                n, j = i // 3, i % 3
                ins = act.activation(zs[:, j, BLK * n:BLK * n + BLK], ps[:, i % 4, :], ACT.Silu)
                ins.then_inc(proj_read, 1)
                if j == 2:
                    ada_copy(8 + 2 * n)
                    ada_copy(9 + 2 * n)
            act.wait_ge(dt_in, 1)
            act.activation(drow[:, 32:64], drow[:, 32:64], ACT.Exp)
            act.activation(dtmp[:, :, :], dtmp[:, :, :], ACT.Exp).then_inc(act_m, 1)
            act.wait_ge(act_m, 1)
            act.activation(dtl[:, :, :], dtmp[:, :, :], ACT.Ln, bias=1.0).then_inc(dt_ln, 1)

            act.wait_ge(vec_ready, 1)
            with act.Fori(0, 6) as r:
                for c in range(4):
                    t = r * 4 + c
                    act.wait_ge(proj, r * 4 + (XBC + 6 + c + 1))
                    act.activation(um_a[:, ds(t, 1), :], ps[:, (XBC + 6 + c) % 4, 0:T], ACT.Copy,
                                   scale=mum[:, 0, ds(t, 1)]).then_inc(mix0, 1)
            for t in range(24, RT):
                act.wait_ge(proj, XBC + 6 + t + 1)
                act.activation(um_a[:, t, :], ps[:, (XBC + 6 + t) % 4, 0:T], ACT.Copy,
                               scale=mum[:, 0, t:t + 1]).then_inc(mix0, 1)

            act.sem_inc(seg_exp, 3)
            act.wait_ge(cs_ps, 1)
            act.activation(ecs[:, :], ps[:, 7, 0:288], ACT.Exp).then_inc(cs_exp, 1)
            act.wait_ge(st_T, 1)
            for d in range(2):
                ins = act.activation(st0[:, d, :].rearrange("p (b c) -> p b c", b=2), ps[:, 2 * d:2 * d + 2, :], ACT.Copy)
            ins.then_inc(st0_ok, 1)
            for d in range(2):
                act.wait_ge(cst_ps, d + 1)
                act.activation(st_out[:, d, :, :].rearrange("p (b i) n -> p b (i n)", b=2), ps[:, 2 * d:2 * d + 2, :],
                               ACT.Copy).then_inc(cst_out, 1)
            act.wait_ge(xn_ready, 1)
            with act.Fori(0, 2) as grp:
                for n, (q, j) in enumerate(QUADS):
                    act.wait_ge(seg_ps, grp * 6 + (n + 4))
                    act.wait_ge(y_ps, grp * 6 + (n + 1))
                    act.activation(seg[:, j, :, :].rearrange("p (d h) q -> p d (h q)", d=2),
                                   ps[:, 2 * j:2 * j + 2, :], ACT.Exp).then_inc(seg_exp, 1)
            act.activation(um_a[:, 24, :], um_a[:, 24, :], ACT.Tanh)
            act.activation(um_a[:, 26, :], um_a[:, 26, :], ACT.Sigmoid).then_inc(wd_ok, 1)
            act.wait_ge(wkv_T, 1)
            for d in range(2):
                ins = act.activation(r0all[:, :, d, :], ps[:, 4 + d, :].rearrange("p (i v) -> p i v", v=64), ACT.Copy)
            ins.then_inc(wkv_ok, 1)
            for j in range(NTILE):
                for grp in range(2):
                    act.wait_ge(gated, 2 * j + grp + 1)
                    act.activation(sq[:, :], xs[:, j, BLK * grp:BLK * grp + BLK], ACT.Square,
                                   accum_out=mstat[:, 2 * j + grp:2 * j + grp + 1]).then_inc(ysq, 1)
                    act.wait_ge(ysq, 3 * j + grp + 1)
                act.activation(mstat[:, 6 + 2 * j:8 + 2 * j], mstat[:, 2 * j:2 * j + 2], ACT.Ln,
                               scale=1.0 / BLK, bias=eps_rms[:, 0:1]).then_inc(ysq, 1)
                act.wait_ge(ysq, 3 * j + 3)
                act.activation(mstat[:, 12 + 2 * j:14 + 2 * j], mstat[:, 6 + 2 * j:8 + 2 * j], ACT.Exp,
                               scale=-0.5).then_inc(mroot, 1)
                act.wait_ge(mroot, j + 1)
                for grp in range(2 if j < NTILE - 1 else 1):
                    xv = xs[:, j, BLK * grp:BLK * grp + BLK]
                    ins = act.activation(xv, xv, ACT.Copy, scale=mstat[:, 12 + 2 * j + grp:13 + 2 * j + grp])
                ins.then_inc(ynorm, 1)
            for t in range(1, 8, 2):
                act.wait_ge(yT_ps, t + 1)
                c = V1["m_norm"] + t
                act.activation(mixm[:, t, :], ps[:, t, 0:T], ACT.Copy, scale=pv1[:, c:c + 1]).then_inc(yT_sb, 1)
            act.wait_ge(yT_sb, 8)
            act.sem_inc(aux_act, 1)
            prep_act(act, -1, 0, KSQ)
            inverse_roots(act, -1, False, True)
            for n in range(W_UP, G_UP + 1):
                prep_act(act, -1, 0, n)
            exps_act(act, -1, 0)
            prep_act(act, -1, 0, BE_T)
            prep_act(act, -1, 0, KAP_T)
            act.wait_ge(aux_ps, 14)
            act.sem_inc(aux_act, 1)
            round_act(act, 0, 0, False, True)
            with act.Fori(0, 3) as i:
                round_act(act, i * 2 + 1, 1, True, True)
                round_act(act, i * 2 + 2, 0, True, True)
            round_act(act, 7, 1, True, False)
            for d in range(2):
                act.wait_ge(fin_T, d + 1)
                act.activation(wkv_in[:, d, :].rearrange("p (b c) -> p b c", b=2), ps[0:64, 2 * d:2 * d + 2, :],
                               ACT.Copy).then_inc(fin_sb, 1)
            tail_act(act, 7, 3)
            act.wait_ge(aux_act, 82)
            act.activation(ysq_c, ysq_c, ACT.Exp, scale=-0.5).then_inc(yr_ok, 1)
            for m in range(4):
                act.wait_ge(gate_ps, m + 1)
                act.activation((g1, g2)[m // 2][:, m % 2, :].rearrange("p (b c) -> p b c", b=2), ps[:, 6:8, :],
                               ACT.Copy).then_inc(gate_ok, 1)
            for j in range(NTILE):
                act.wait_ge(x1_ok, j + 1)
                act.activation(h2sq, x1[:, j, :], ACT.Square, accum_out=fst[:, j:j + 1]).then_inc(sq2_ok, 1)
                act.wait_ge(sq2_ok, j + 1)
                act.activation(fst[:, 6 + j:7 + j], fst[:, j:j + 1], ACT.Sqrt, scale=1.0 / D, bias=eps_rms[:, 0:1]).then_inc(rstd, 1)
            act.wait_ge(lgT_ps, 1)
            act.activation(lgT, ps[0:36, 6, 0:T], ACT.Copy).then_inc(lgT_ok, 1)
            for j in range(NTILE):
                act.wait_ge(h2_ps, j + 1)
                act.activation(h2[:, j, :].rearrange("p (b c) -> p b c", b=2), ps[:, 2 * j:2 * j + 2, :],
                               ACT.Copy).then_inc(h2_ok, 1)
            act.wait_ge(rt_dve, 1)
            act.activation(grp2, grp2, ACT.Exp).then_inc(rt_act, 1)
            act.wait_ge(rt_dve, 2)
            act.activation(s3[:, 5, :], s3[:, 4, :], ACT.Exp).then_inc(rt_act, 1)
            for n in range(2):
                silu_gate(act, n, n)
                if n:
                    expert_out(act, n - 1, 1 - n)
            silu_gate(act, 2, 0)
            expert_out(act, 1, 1)
            act.wait_ge(zero_ok, 16)
            n_turns = turns(act)
            with act.Fori(1, n_turns - 1) as i:
                silu_gate(act, i * 2 + 1, 1)
                expert_out(act, i * 2, 0)
                silu_gate(act, i * 2 + 2, 0)
                expert_out(act, i * 2 + 1, 1)
            silu_gate(act, n_turns * 2 - 1, 1)
            expert_out(act, n_turns * 2 - 2, 0)
            expert_out(act, n_turns * 2 - 1, 1)
            for j in range(2):
                act.wait_ge(comb[j], 32)
                act.activation(cmb[:, j, 0, :], cmb[:, j, 0, :], ACT.Copy, scale=wcol[:, 0, j:j + 1]).then_inc(cmb_w, 1)
            for j in range(NTILE):
                if j == 1:
                    act.wait_ge(comb[0], 64)
                    act.activation(cmb[:, 0, 0, :], cmb[:, 0, 0, :], ACT.Copy, scale=wcol[:, 0, 2:3]).then_inc(cmb_w, 1)
                act.wait_ge(x1_ok, j + 4)
                act.activation(h2[:, j, :], x1[:, j, :], ACT.Square, accum_out=fst[:, j:j + 1]).then_inc(sq2_ok, 1)
                act.wait_ge(sq2_ok, j + 4)
                act.activation(fst[:, 6 + j:7 + j], fst[:, j:j + 1], ACT.Sqrt, scale=1.0 / D, bias=eps_rms[:, 0:1]).then_inc(rstd, 1)

        @block.vector
        def _(dve):
            chain = Chain(dve, dve_c)
            dve.memset(eps_rms[:, :], 1e-6)
            dve.memset(tiny[:, :], 1e-30)
            dve.memset(eps_gn[:, :], 64e-5)
            chain.do(dve.memset(bones[:, :], 0.0))
            dve.memset(bones[0:64, 0:64], 1.0)
            dve.memset(bones[64:P, 64:P], 1.0)
            dve.wait_ge(const_ready, 1)
            dve.tensor_reduce(sel32[:, :], ident[:, :].rearrange("p (q v) -> p v q", v=32), AX.X, ALU.add).then_inc(sel32_ok, 1)
            chain.do(dve.tensor_reduce(par[:, 0:4], ident[:, :].rearrange("p (q v) -> p v q", v=4), AX.X, ALU.add))
            dve.tensor_tensor(par[:, 4:6], par[:, 0:2], par[:, 2:4], ALU.add)
            dve.wait_ge(vec_t, 1)
            dve.tensor_copy(pv0[:, :], ps[:, 1, 0:P])
            chain.do(dve.tensor_copy(pv1[:, 0:V1N], ps[:, 2, 0:V1N]))
            mu = pv1[:, 0:RT]
            dve.tensor_scalar(mum[:, 0, :], mu, -1.0, 1.0, ALU.mult, ALU.add)
            for i in range(6):
                dve.tensor_scalar(mum[:, 1 + i, :], mu, par[:, i:i + 1], None, ALU.mult)
            dve.tensor_scalar(kam[:, :], pv1[:, V1["k_a"]:V1["k_a"] + 8], -1.0, 1.0, ALU.mult,
                              ALU.add).then_inc(vec_ready, 1)
            dve.wait_ge(rstd, 1)
            chain.do(dve.reciprocal(stat[:, 8:11], stat[:, 12:15]))
            for j in range(NTILE):
                ins = dve.tensor_scalar(xt[:, j, :], xt[:, j, :], stat[:, 8 + j:9 + j], None, ALU.mult)
            ins.then_inc(xn_ready, 1)
            dve.wait_ge(ada_cols, 4)
            chain.do(dve.tensor_tensor(mod[:, 0:16, :], ps[:, 6, 0:32].rearrange("p (t v) -> p t v", v=2),
                                   pv0[:, 0:16].unsqueeze(2).to_broadcast([P, 16, 2]), ALU.add))
            chain.do(dve.tensor_scalar(aff1[:, :, :], mod[:, 8:16, :], 1.0, None, ALU.add))
            chain.do(dve.tensor_tensor(aff1[:, :, :], aff1[:, :, :],
                                   pv0[:, V0["norm1"]:V0["norm1"] + 8].unsqueeze(2).to_broadcast([P, 8, 2]), ALU.mult))
            for k in range(KT):
                dve.wait_ge(xT_ps, k + 1)
                for v, (lo, hi) in enumerate(((0, P), (P, T))):
                    ins = dve.tensor_scalar(hT[:, k, lo:hi], ps[:, k % 4, lo:hi], aff1[:, k, v:v + 1],
                                            mod[:, k, v:v + 1], ALU.mult, ALU.add)
                ins.then_inc(hT_ready, 1)
            W = T + 2

            def taps(t):
                dve.wait_ge(proj_read, t + 1)
                if t >= 2 and t < 10:
                    dve.wait_ge(conv_T, t - 1)
                elif t >= 10:
                    dve.wait_ge(conv_out, t - 1)
                for j in range(5):
                    w = pv0[:, V0["conv_w"] + 12 * j + t:V0["conv_w"] + 12 * j + t + 1]
                    src = raw[:, t % 2, j:j + W]
                    if j == 0:
                        ins = dve.tensor_scalar(acc[:, t % 2, 0:W], src, w, None, ALU.mult)
                    else:
                        ins = dve.scalar_tensor_tensor(acc[:, t % 2, 0:W], src, w, acc[:, t % 2, 0:W],
                                                       ALU.mult, ALU.add)
                    if j < 4:
                        chain.do(ins)
                ins.then_inc(conv_acc, 1)

            def token_major(t):
                if t >= 10:
                    return
                dve.wait_ge(conv_T, t + 1)
                dst = xs[:, :, P * t:P * t + P] if t < 8 else btm[:, :, P * (t - 8):P * (t - 8) + P]
                dve.tensor_copy(dst, ps[:, 4 + t % 2, 0:T].rearrange("p (j c) -> p j c", j=NTILE)).then_inc(conv_tm, 1)

            for t in range(XBC):
                taps(t)
                if t >= 3:
                    token_major(t - 3)
            token_major(9)

            dve.wait_ge(dt_ps, 1)
            chain.do(dve.tensor_tensor(dt[:, :, :], ps[:, 7, 0:96].rearrange("p (j h) -> p j h", j=NTILE),
                                   drow[:, 0:32].unsqueeze(1).to_broadcast([P, NTILE, 32]), ALU.add))
            dve.scalar_tensor_tensor(dtmp[:, :, :], dt[:, :, :], -1.0, dt[:, :, :], ALU.mult,
                                     ALU.min).then_inc(dt_in, 1)
            dve.wait_ge(dt_ln, 1)
            chain.do(dve.tensor_scalar(la[:, :, :], dtmp[:, :, :], 1.0, None, ALU.add))
            chain.do(dve.reciprocal(dtr[:, :, :], la[:, :, :]))
            chain.do(dve.tensor_scalar(la[:, :, :], la[:, :, :], 1.0, None, ALU.subtract))
            chain.do(dve.tensor_tensor(dtmp[:, :, :], dtmp[:, :, :], la[:, :, :], ALU.subtract))
            chain.do(dve.tensor_tensor(dtmp[:, :, :], dtmp[:, :, :], dtr[:, :, :], ALU.mult))
            chain.do(dve.tensor_tensor(dtl[:, :, :], dtl[:, :, :], dtmp[:, :, :], ALU.add))
            chain.do(dve.scalar_tensor_tensor(dt[:, :, :], dt[:, :, :], 0.0, dtl[:, :, :], ALU.max, ALU.add))
            dve.scalar_tensor_tensor(la[:, :, :], dt[:, :, :], -1.0,
                                     drow[:, 32:64].unsqueeze(1).to_broadcast([P, NTILE, 32]),
                                     ALU.mult, ALU.mult).then_inc(la_ready, 1)
            dve.wait_ge(ada_cols, 12)
            chain.do(dve.tensor_tensor(mod[:, 16:32, :], ps[:, 6, 32:64].rearrange("p (t v) -> p t v", v=2),
                                   pv0[:, 24:40].unsqueeze(2).to_broadcast([P, 16, 2]), ALU.add))
            chain.do(dve.tensor_scalar(aff2[:, :, :], mod[:, 24:32, :], 1.0, None, ALU.add))
            chain.do(dve.tensor_tensor(aff2[:, :, :], aff2[:, :, :],
                                   pv1[:, V1["norm2"]:V1["norm2"] + 8].unsqueeze(2).to_broadcast([P, 8, 2]), ALU.mult))

            for i, lo in enumerate((16, 40)):
                ins = dve.tensor_tensor(gcol[:, 8 * i:8 * i + 8, :], ps[:, 6, 64 + 16 * i:80 + 16 * i].rearrange("p (t v) -> p t v", v=2),
                                        pv0[:, lo:lo + 8].unsqueeze(2).to_broadcast([P, 8, 2]), ALU.add)
            ins.then_inc(gcol_ok, 1)

            def mix(c, t, mus, step):
                u = ps[:, c, 0:T]
                o = um_a[:, t, :] if isinstance(t, int) else um_a[:, ds(t, 1), :].rearrange("p a t -> p (a t)")
                ug = u[:, P:T].rearrange("p (r w) -> p r w", w=GRID)
                og = o[:, P:T].rearrange("p (r w) -> p r w", w=GRID)
                parts = [(o[:, 1:P], u[:, 0:P - 1], 5), (o[:, 0:P - 1], u[:, 1:P], 6),
                         (og[:, :, 1:], ug[:, :, :-1], 1), (og[:, :, :-1], ug[:, :, 1:], 2),
                         (o[:, P + GRID:T], u[:, P:T - GRID], 3), (o[:, P:T - GRID], u[:, P + GRID:T], 4)]
                for i, (dst, src, m) in enumerate(parts):
                    step(dve.scalar_tensor_tensor(dst, src, mus(m), dst, ALU.mult, ALU.add), i)

            with dve.Fori(0, 6) as r:
                lc = LoopChain(dve, dve_r, r, 20)
                for c in range(4):
                    t = r * 4 + c
                    dve.wait_ge(mix0, r * 4 + (c + 1))

                    def step(ins, i):
                        if i < 5:
                            lc.do(ins)
                        else:
                            ins.then_inc(proj_read, 1)
                    mix((XBC + 6 + c) % 4, t, lambda m: mum[:, m, ds(t, 1)], step)
                lc.end()
            for t in range(24, RT):
                dve.wait_ge(mix0, t + 1)

                def step(ins, i):
                    if i < 5:
                        chain.do(ins)
                    else:
                        ins.then_inc(proj_read, 1)
                mix((XBC + 6 + t) % 4, t, lambda m: mum[:, m, t:t + 1], step)

            dve.sem_inc(y_sb, 2)
            dve.wait_ge(cs_exp, 1)
            for d in range(2):
                w = ecs[:, 96 + 48 * d:144 + 48 * d].rearrange("p (j h) -> p j h", j=NTILE)
                ins = dve.tensor_tensor(w, w, dt[:, :, 16 * d:16 * d + 16], ALU.mult)
            chain.do(ins)
            dve.wait_ge(proj, XBC + 6 + RT)
            dve.wait_ge(score_ps, 1)
            for d in range(2):
                for b, n in ((0, 4), (1, 2)):
                    ins = dve.tensor_tensor(msc[:, d, 4 * b:4 * b + n, :],
                                            ps[:, 4 + b, 0:P * n].rearrange("p (i q) -> p i q", i=n),
                                            tri[:, 1 + 2 * d, :].unsqueeze(1).to_broadcast([P, n, P]), ALU.mult)
            ins.then_inc(score_ok, 1)

            def heads(ap):
                return ap.rearrange("p (h c) -> p h c", c=PM)

            for job in range(4):
                d, j = job % 2, (0, 0, 1, 2)[job]
                if job >= 2:
                    dve.wait_ge(cst_ps, job - 1)
                w = ecs[:, 96 + 48 * d + 16 * j:96 + 48 * d + 16 * j + 16]
                dve.tensor_tensor(heads(xdw[:, job % 2, :]), heads(xs[:, j, :]),
                                  w.unsqueeze(2).to_broadcast([P, HM, PM]), ALU.mult).then_inc(xdw_ok, 1)
            dve.wait_ge(st0_ok, 1)
            for d in range(2):
                j = 1 + d
                dec = ecs[:, 192 + 32 * j + 16 * d:192 + 32 * j + 16 * d + 16]
                chain.do(dve.tensor_tensor(heads(st1[:, d, :]), heads(st0[:, d, :]),
                                       dec.unsqueeze(2).to_broadcast([P, HM, PM]), ALU.mult))
                dve.wait_ge(cst_ps, 3 + d)
                st1v = st1[:, d, :].rearrange("p (b c) -> p b c", b=2)
                ins = dve.tensor_tensor(st1v, st1v, ps[:, 2 * d:2 * d + 2, :], ALU.add)
            ins.then_inc(st1_ok, 1)

            def decayed_scores(grp, n, lc):
                q, j = QUADS[n]
                dve.wait_ge(seg_exp, grp * 6 + (n + 4))
                for d in range(2):
                    for h in range(4):
                        ins = dve.scalar_tensor_tensor(
                            seg[:, j, 4 * d + h, :], seg[:, j, 4 * d + h, :], dt[:, j, ds(grp * 8 + (16 * d + 4 * q + h), 1)],
                            msc[:, d, ds(grp + 2 * j, 1), :].rearrange("p a q -> p (a q)"), ALU.mult, ALU.mult)
                lc.do(ins)
                both_dirs = seg[:, j, :, :].rearrange("p (d h) q -> p d (h q)", d=2)
                dve.tensor_tensor(both_dirs[:, 0], both_dirs[:, 0], both_dirs[:, 1], ALU.add).then_inc(g_ok, 1)

            def y_add(grp, n, lc):
                q, j = QUADS[n]
                dve.wait_ge(y_ps, grp * 6 + (n + 4))
                xv = xs[:, j, ds(grp * BLK + 256 * q, 256)]
                lc.do(dve.tensor_tensor(heads(xv), heads(xv),
                                        drow[:, ds(grp * 8 + (64 + 4 * q), 4)].unsqueeze(2).to_broadcast([P, 4, PM]), ALU.mult))
                dve.tensor_tensor(xv, xv, y_place(n), ALU.add).then_inc(y_sb, 1)

            with dve.Fori(0, 2) as grp:
                lc = LoopChain(dve, dve_l, grp, 12)
                for n in range(len(QUADS)):
                    decayed_scores(grp, n, lc)
                    if n >= 2:
                        y_add(grp, n - 2, lc)
                y_add(grp, 4, lc)
                y_add(grp, 5, lc)
                lc.end()
            dve.wait_ge(y_sb, 14)

            def gate(j):
                for grp in range(2):
                    xv = xs[:, j, BLK * grp:BLK * grp + BLK]
                    dve.tensor_tensor(xv, xv, zs[:, j, BLK * grp:BLK * grp + BLK], ALU.mult).then_inc(gated, 1)

            gate(0)
            for o, (j, d, _) in enumerate(OFF):
                for grp in range(2):
                    i = 2 * o + grp
                    dve.wait_ge(off_ps, i + 1)
                    f = ecs[:, 48 * d + 16 * j + 8 * grp:48 * d + 16 * j + 8 * grp + 8]
                    dve.tensor_tensor(heads(yoff[:, :]), heads(ps[:, i % 4, :]),
                                      f.unsqueeze(2).to_broadcast([P, 8, PM]), ALU.mult).then_inc(off_rd, 1)
                    dve.wait_ge(off_rd, i + 1)
                    xv = xs[:, j, BLK * grp:BLK * grp + BLK]
                    chain.do(dve.tensor_tensor(xv, xv, yoff[:, :], ALU.add))
                if o % 2:
                    gate(j)
            dve.wait_ge(mroot, 3)
            xv = xs[:, 2, BLK:2 * BLK]
            dve.tensor_scalar(xv, xv, mstat[:, 17:18], None, ALU.mult).then_inc(ynorm_d, 1)
            for t in range(0, 8, 2):
                dve.wait_ge(yT_ps, t + 1)
                c = V1["m_norm"] + t
                dve.tensor_scalar(mixm[:, t, :], ps[:, t, 0:T], pv1[:, c:c + 1], None, ALU.mult).then_inc(yT_sb, 1)

            dve.sem_inc(aux_dve, 1)
            dve.sem_inc(yo_rd, 3)
            dve.sem_inc(pair_ok, 1)
            dve.wait_ge(wkv_ok, 1)
            pc = LoopChain(dve, dve_p, 0, 7)
            for part in range(7):
                prep_dve(dve, -1, 0, pc, part)
            dve.wait_ge(aux_ps, 14)
            dve.sem_inc(aux_dve, 1)
            round_dve(dve, 0, 0, False, True)
            with dve.Fori(0, 3) as i:
                round_dve(dve, i * 2 + 1, 1, True, True)
                round_dve(dve, i * 2 + 2, 0, True, True)
            round_dve(dve, 7, 1, True, False)
            tc = LoopChain(dve, dve_q, 7, 2)
            tail_dve(dve, 7, 2, 7, 1, tc, 0)
            tail_dve(dve, 7, 2, 7, 1, tc, 1)

            dve.wait_ge(x_again, 32)
            dve.wait_ge(gate_ok, 4)

            def x1_tile(j):
                dve.wait_ge(out_ps, 4 + j)
                chain.do(dve.tensor_tensor(h2[:, j, :].rearrange("p (b c) -> p b c", b=2), ps[:, 2 * j:2 * j + 2, :],
                                       g1[:, min(j, 1), :].rearrange("p (b c) -> p b c", b=2), ALU.mult))
                dve.tensor_tensor(x1[:, j, :], x1[:, j, :], h2[:, j, :], ALU.add).then_inc(x1_ok, 1)

            def x1_norm(j):
                dve.wait_ge(rstd, 2 + j)
                chain.do(dve.reciprocal(fst[:, 9 + j:10 + j], fst[:, 6 + j:7 + j]))
                dve.tensor_scalar(h2[:, j, :], x1[:, j, :], fst[:, 9 + j:10 + j], None, ALU.mult).then_inc(xn2_ok, 1)

            x1_tile(0)
            x1_tile(1)
            x1_norm(0)
            x1_tile(2)
            x1_norm(1)
            x1_norm(2)
            for k in range(KT):
                dve.wait_ge(h2T_ps, k + 1)
                for v, (lo, hi) in enumerate(((0, P), (P, T))):
                    ins = dve.tensor_scalar(hT[:, k, lo:hi], ps[:, 6 + k % 2, lo:hi], aff2[:, k, v:v + 1],
                                            mod[:, 16 + k, v:v + 1], ALU.mult, ALU.add)
                ins.then_inc(h2T_ok, 1)
            def cols(ap, n):
                return ap.unsqueeze(2).to_broadcast([P, NTILE, n])

            def row(ap, n):
                return ap.unsqueeze(1).to_broadcast([P, NTILE, n])

            def one_hot(dst, vals, top, places, n, scr):
                chain.do(dve.tensor_tensor(scr, vals, cols(top, n), ALU.is_equal))
                chain.do(dve.tensor_tensor(scr, scr, row(places, n), ALU.mult))
                chain.do(dve.tensor_reduce(s3[:, 9, :], scr, AX.X, ALU.max))
                chain.do(dve.tensor_tensor(dst, scr, cols(s3[:, 9, :], n), ALU.is_equal))

            dve.wait_ge(lg_ps, 1)
            dve.wait_ge(rconst, 1)
            chain.do(dve.tensor_tensor(lg, ps[:, 7, 128:236].rearrange("p (j c) -> p j c", j=NTILE), row(brt, 36), ALU.add))
            gl, el = lg[:, :, 0:4], lg[:, :, 4:36]
            chain.do(dve.tensor_reduce(s3[:, 0, :], gl, AX.X, ALU.max))
            dve.tensor_tensor(grp2, gl, cols(s3[:, 0, :], 4), ALU.subtract).then_inc(rt_dve, 1)
            one_hot(ghot, gl, s3[:, 0, :], down[:, 0:4], 4, ghot)
            g4 = [x.rearrange("p j (g e) -> p j g e", g=EG) for x in (msk, el, tmp)]
            gb8 = ghot.unsqueeze(3).to_broadcast([P, NTILE, EG, EPG])
            chain.do(dve.tensor_tensor(g4[0], g4[1], gb8, ALU.mult))
            chain.do(dve.tensor_scalar(ghot, ghot, 1e30, -1e30, ALU.mult, ALU.add))
            chain.do(dve.tensor_tensor(g4[0], g4[0], gb8, ALU.add))
            chain.do(dve.tensor_reduce(s3[:, 2, :], msk, AX.X, ALU.max))
            one_hot(oh[:, 0], msk, s3[:, 2, :], down[:, 4:36], 32, tmp)
            chain.do(dve.scalar_tensor_tensor(msk, oh[:, 0], -3e30, msk, ALU.mult, ALU.add))
            chain.do(dve.tensor_reduce(s3[:, 3, :], msk, AX.X, ALU.max))
            one_hot(oh[:, 1], msk, s3[:, 3, :], down[:, 4:36], 32, tmp)
            dve.tensor_tensor(both_oh, oh[:, 0], oh[:, 1], ALU.add).then_inc(a_ok, 1)
            dve.tensor_tensor(s3[:, 4, :], s3[:, 3, :], s3[:, 2, :], ALU.subtract).then_inc(rt_dve, 1)
            dve.wait_ge(rt_act, 1)
            chain.do(dve.tensor_reduce(s3[:, 1, :], grp2, AX.X, ALU.add))
            dve.wait_ge(rt_act, 2)
            chain.do(dve.tensor_scalar(s3[:, 6, :], s3[:, 5, :], 1.0, None, ALU.add))
            chain.do(dve.tensor_tensor(s3[:, 6, :], s3[:, 6, :], s3[:, 1, :], ALU.mult))
            chain.do(dve.reciprocal(wcol[:, 0, :], s3[:, 6, :]))
            chain.do(dve.tensor_tensor(wcol[:, 1, :], wcol[:, 0, :], s3[:, 5, :], ALU.mult))
            dve.wait_ge(rank_ps, 1)
            n_e = ps[:, 7, 96:128]
            chain.do(dve.tensor_scalar(cnt[:, 0, :], n_e, CH + 0.5, None, ALU.is_gt))
            for m in range(2, T // CH):
                chain.do(dve.scalar_tensor_tensor(cnt[:, 0, :], n_e, m * CH + 0.5, cnt[:, 0, :], ALU.is_gt, ALU.add))
            chain.do(dve.tensor_tensor_scan(cnt[:, 1, :], ones[:, 0:32], cnt[:, 0, :], 0.0, ALU.mult, ALU.add))
            chain.do(dve.tensor_tensor(cnt[:, 2, :], cnt[:, 1, :], cnt[:, 0, :], ALU.subtract))
            chain.do(dve.tensor_tensor(cnt[:, 3, :], cnt[:, 2, :], erow, ALU.subtract))
            chain.do(dve.tensor_scalar(cnt[:, 3, :], cnt[:, 3, :], float(CH), float(CH * (NE - 1)), ALU.mult, ALU.add))
            rank = ps[:, 7, 0:96].rearrange("p (j e) -> p j e", j=NTILE)
            chain.do(dve.tensor_scalar(tmp, rank, CH - 0.5, None, ALU.is_gt))
            chain.do(dve.tensor_tensor(tmp, tmp, row(cnt[:, 3, :], 32), ALU.mult))
            chain.do(dve.tensor_tensor(slot_v, rank, tmp, ALU.add))
            chain.do(dve.scalar_tensor_tensor(slot_v, row(erow, 32), float(CH), slot_v, ALU.mult, ALU.add))
            for k in range(2):
                chain.do(dve.tensor_tensor(tmp, slot_v, oh[:, k], ALU.mult))
                chain.do(dve.tensor_reduce(slots[:, k, :], tmp, AX.X, ALU.add))
            dve.tensor_copy(slots_i[:, :], slots.rearrange("p k j -> p (k j)")).then_inc(slots_ok, 1)
            select(dve, 0)
            n_ov = N_CHUNKS - NE
            q_col = erow[:, 0:n_ov].unsqueeze(2).to_broadcast([P, n_ov, NE])

            def by_chunk(v):
                return v.unsqueeze(1).to_broadcast([P, n_ov, NE])
            dve.tensor_tensor(mq, by_chunk(cnt[:, 2, :]), q_col, ALU.is_le)
            chain.do(dve.tensor_tensor(mq2, by_chunk(cnt[:, 1, :]), q_col, ALU.is_gt))
            chain.do(dve.tensor_tensor(mq, mq, mq2, ALU.mult))
            chain.do(dve.tensor_tensor(mq, mq, by_chunk(erow), ALU.mult))
            dve.tensor_copy(meta[:, 1:1 + NE], erow)
            dve.tensor_scalar(meta[:, 0:1], cnt[:, 1, 31:32], 0.5, None, ALU.is_gt)
            chain.do(dve.tensor_reduce(meta[:, 1 + NE:1 + N_CHUNKS], mq, AX.X, ALU.add))
            for m in range(1, OV_TURNS):
                chain.do(dve.scalar_tensor_tensor(meta[:, 0:1], cnt[:, 1, 31:32], 4.0 * m + 0.5, meta[:, 0:1], ALU.is_gt, ALU.add))
            dve.tensor_copy(meta_i[:, :], meta).then_inc(meta_ok, 1)
            for n in range(2):
                rows_copy(dve, n, n)
                select(dve, n + 1)
            for n in (1, 2):
                hidden(dve, n - 1, 1 - n % 2)
                rows_copy(dve, n + 1, 1 - n % 2)
                select(dve, n + 2)
            n_turns = turns(dve)
            with dve.Fori(1, n_turns - 1) as i:
                for b in range(2):
                    hidden(dve, i * 2 + b, b)
                    rows_copy(dve, i * 2 + (b + 2), b)
                    select(dve, i * 2 + (b + 3))
            hidden(dve, n_turns * 2 - 2, 0)
            hidden(dve, n_turns * 2 - 1, 1)
            def x2_tile(j):
                b, v = j % 2, min(j, 1)
                dve.wait_ge(comb[b], 32 * (j // 2 + 1))
                if j:
                    dve.wait_ge(x1_ok, j + 3)
                dve.wait_ge(cmb_w, j + 1)
                dve.scalar_tensor_tensor(ymoe, cmb[:, b, 1, :], wcol[:, 1, j:j + 1], cmb[:, b, 0, :], ALU.mult,
                                         ALU.add).then_inc(moe_ok, 1)
                dve.wait_ge(moe_ok, j + 1)
                chain.do(dve.tensor_tensor(ymoe, ymoe, g2[:, v, :], ALU.mult))
                dve.tensor_tensor(x1[:, j, :], x1[:, j, :], ymoe, ALU.add).then_inc(x1_ok, 1)

            def y_tile(j):
                dve.wait_ge(rstd, 5 + j)
                chain.do(dve.reciprocal(fst[:, 9 + j:10 + j], fst[:, 6 + j:7 + j]))
                dve.scalar_tensor_tensor(x1[:, j, :], x1[:, j, :], fst[:, 9 + j:10 + j], fnw, ALU.mult,
                                         ALU.mult).then_inc(y_ok, 1)

            x2_tile(0)
            x2_tile(1)
            y_tile(0)
            x2_tile(2)
            y_tile(1)
            y_tile(2)


N_SMALL = 17
N_OUT = 7


_OUTS = [(1, P, D), (1, 2 * P, D), (1, 1, HM, PM, NS), (1, 1, HM, PM, NS), (1, 1, 16, 64, 64), (1, 1, 16, 64, 64)]


def kernel(**inputs):
    import numpy as np
    import concourse.bacc as bacc
    from concourse.bass_utils import run_bass_kernel_spmd

    nc = bacc.Bacc("TRN2", target_bir_lowering=False, num_devices=1)
    arrays, aps = {}, {}
    for name, value in inputs.items():
        arr = np.ascontiguousarray(value)
        arrays["in_" + name] = arr
        aps[name] = nc.dram_tensor("in_" + name, arr.shape, mybir.dt.from_np(arr.dtype), kind="ExternalInput").ap()
    outs = [nc.dram_tensor(f"out_{i}", shape, F32, kind="ExternalOutput").ap() for i, shape in enumerate(_OUTS)]
    program(nc, aps, outs)
    got = run_bass_kernel_spmd(nc, [arrays], core_ids=[0]).results[0]
    return tuple(got[f"out_{i}"] for i in range(len(_OUTS)))
```
